# Optimizing a Trainium2 kernel written in Bass

```python
import math
import jax, jax.numpy as jnp
from jax import lax
import numpy as np
import jax
import jax.numpy as jnp

D_MODEL = 1024
BATCH = 1
SEQ = 1024
DEPTH = 1

HEAD_DIM = 64
SSM_WIDTH = 3 * D_MODEL // 8
FFT_WIDTH = D_MODEL // 4
ATT_WIDTH = D_MODEL - SSM_WIDTH - FFT_WIDTH
SSM_GROUP = 16
SSM_GROUPS = SSM_WIDTH // SSM_GROUP
SSM_STATE = 64
FFT_HEADS = FFT_WIDTH // HEAD_DIM
N_Q_HEADS = ATT_WIDTH // HEAD_DIM
N_KV_HEADS = 2
GQA_GROUP = N_Q_HEADS // N_KV_HEADS
KV_WIDTH = N_KV_HEADS * HEAD_DIM
IN_WIDTH = SSM_WIDTH + FFT_WIDTH + ATT_WIDTH + 2 * KV_WIDTH
WINDOW = 128
BLOCK = 128
KV_SPAN = 3 * BLOCK
D_FF = ((8 * D_MODEL // 3 + 255) // 256) * 256
DT_MIN = 1e-3
DT_MAX = 1e-1
RMS_EPS = 1e-6
NEG_INF = -1e30


def rms_norm(x, gain):
    xf = x.astype(jnp.float32)
    y = xf * lax.rsqrt(jnp.mean(xf * xf, axis=-1, keepdims=True) + RMS_EPS)
    return (y * gain.astype(jnp.float32)).astype(x.dtype)

def _scan_combine(left, right):
    a_l, h_l = left
    a_r, h_r = right
    return a_l * a_r, a_r * h_l + h_r

def s5_mixer(u, lam_re, lam_im, log_dt, b_re, b_im, c_re, c_im, d_skip, w_glu):
    bsz, seq, _ = u.shape
    f32 = jnp.float32
    uf = u.astype(f32).reshape(bsz, seq, SSM_GROUPS, SSM_GROUP)
    lam = lax.complex(lam_re.astype(f32), lam_im.astype(f32))
    dt = jnp.exp(log_dt.astype(f32))[..., None]
    lam_bar = jnp.exp(lam * dt)
    b = lax.complex(b_re.astype(f32), b_im.astype(f32))
    b_bar = ((lam_bar - 1.0) / lam)[..., None] * b
    states = []
    for d, rev in ((0, False), (1, True)):
        bu = lax.complex(jnp.einsum('bsgc,gpc->bsgp', uf, b_bar[d].real),
                         jnp.einsum('bsgc,gpc->bsgp', uf, b_bar[d].imag))
        a = jnp.broadcast_to(lam_bar[d], bu.shape)
        _, h_dir = lax.associative_scan(_scan_combine, (a, bu), reverse=rev, axis=1)
        states.append(h_dir)
    h = states[0] + states[1]
    y = (jnp.einsum('bsgp,gcp->bsgc', h.real, c_re.astype(f32))
         - jnp.einsum('bsgp,gcp->bsgc', h.imag, c_im.astype(f32)))
    y = y.reshape(bsz, seq, SSM_WIDTH) + d_skip.astype(f32) * u.astype(f32)
    y = jax.nn.gelu(y).astype(u.dtype)
    return y * jax.nn.sigmoid(y @ w_glu)

def fourier_mixer(f, w_fft):
    bsz, seq, _ = f.shape
    ff = f.astype(jnp.float32).reshape(bsz, seq, FFT_HEADS, HEAD_DIM)
    mixed = jnp.fft.fft2(ff, axes=(1, 3), norm='ortho').real.astype(f.dtype)
    return jnp.einsum('bshd,hde->bshe', mixed, w_fft).reshape(bsz, seq, FFT_WIDTH)

def window_attention(q, k, v, sink):
    bsz, seq, _ = q.shape
    nblk = seq // BLOCK
    qb = (q * HEAD_DIM ** -0.5).reshape(bsz, nblk, BLOCK, N_KV_HEADS, GQA_GROUP, HEAD_DIM)

    def band(t):
        t = t.reshape(bsz, seq, N_KV_HEADS, HEAD_DIM)
        t = jnp.pad(t, ((0, 0), (BLOCK, BLOCK), (0, 0), (0, 0)))
        t = t.reshape(bsz, nblk + 2, BLOCK, N_KV_HEADS, HEAD_DIM)
        return jnp.concatenate([t[:, :-2], t[:, 1:-1], t[:, 2:]], axis=2)

    kb, vb = band(k), band(v)
    qi = jnp.arange(BLOCK)[:, None]
    kj = jnp.arange(KV_SPAN)[None, :]
    dist = jnp.abs(qi + BLOCK - kj)
    key_pos = jnp.arange(nblk)[:, None] * BLOCK - BLOCK + kj
    valid = (dist <= WINDOW)[None] & ((key_pos >= 0) & (key_pos < seq))[:, None, :]
    slopes = jnp.exp2(-8.0 * jnp.arange(1, N_Q_HEADS + 1, dtype=jnp.float32) / N_Q_HEADS)
    slopes = slopes.reshape(N_KV_HEADS, GQA_GROUP)
    bias = -slopes[:, :, None, None] * dist.astype(jnp.float32)
    scores = jnp.einsum('bnqkgd,bnskd->bnkgqs', qb, kb).astype(jnp.float32) + bias
    scores = jnp.where(valid[None, :, None, None], scores, NEG_INF)
    sink_l = sink.astype(jnp.float32).reshape(1, 1, N_KV_HEADS, GQA_GROUP, 1, 1)
    m = jnp.maximum(jnp.max(scores, axis=-1, keepdims=True), sink_l)
    p = jnp.exp(scores - m)
    p = p / (jnp.sum(p, axis=-1, keepdims=True) + jnp.exp(sink_l - m))
    out = jnp.einsum('bnkgqs,bnskd->bnqkgd', p.astype(v.dtype), vb)
    return out.reshape(bsz, seq, ATT_WIDTH)

def dwconv3(h, w, b):
    hp = jnp.pad(h, ((0, 0), (1, 1), (0, 0)))
    return hp[:, :-2] * w[0] + hp[:, 1:-1] * w[1] + hp[:, 2:] * w[2] + b

def first_inputs(seed: int = 0) -> dict:
    key = jax.random.key(seed)
    ks = iter(jax.random.split(key, 32))
    nrm = lambda shape, scale: scale * jax.random.normal(next(ks), shape, jnp.float32)
    L, D, G, P = DEPTH, D_MODEL, SSM_GROUPS, SSM_STATE
    lam_im_base = jnp.pi * jnp.arange(P, dtype=jnp.float32)
    return {
        'x': nrm((BATCH, SEQ, D), 1.0),
        'c': nrm((BATCH, D), 1.0),
        'w_ada': nrm((L, D, 6 * D), 0.5 * D ** -0.5),
        'b_ada': nrm((L, 6 * D), 0.01),
        'g_pre_mix': 1.0 + nrm((L, D), 0.05),
        'g_post_mix': 1.0 + nrm((L, D), 0.05),
        'g_pre_ffn': 1.0 + nrm((L, D), 0.05),
        'g_post_ffn': 1.0 + nrm((L, D), 0.05),
        'w_in': nrm((L, D, IN_WIDTH), D ** -0.5),
        'lam_re': -0.5 + nrm((L, 2, G, P), 0.01),
        'lam_im': lam_im_base + nrm((L, 2, G, P), 0.01),
        'log_dt': jax.random.uniform(next(ks), (L, 2, G), jnp.float32,
                                     minval=math.log(DT_MIN), maxval=math.log(DT_MAX)),
        'b_re': nrm((L, 2, G, P, SSM_GROUP), (2 * SSM_GROUP) ** -0.5),
        'b_im': nrm((L, 2, G, P, SSM_GROUP), (2 * SSM_GROUP) ** -0.5),
        'c_re': nrm((L, G, SSM_GROUP, P), (2 * P) ** -0.5),
        'c_im': nrm((L, G, SSM_GROUP, P), (2 * P) ** -0.5),
        'd_skip': nrm((L, SSM_WIDTH), 1.0),
        'w_glu': nrm((L, SSM_WIDTH, SSM_WIDTH), SSM_WIDTH ** -0.5),
        'w_fft': nrm((L, FFT_HEADS, HEAD_DIM, HEAD_DIM), HEAD_DIM ** -0.5),
        'sink': nrm((L, N_Q_HEADS), 1.0),
        'w_out': nrm((L, D, D), D ** -0.5),
        'w_up': nrm((L, D, 2 * D_FF), D ** -0.5),
        'conv_w': nrm((L, 3, 2 * D_FF), 3 ** -0.5),
        'conv_b': nrm((L, 2 * D_FF), 0.01),
        'w_down': nrm((L, D_FF, D), D_FF ** -0.5),
    }

def first_block(x, c, w_ada, b_ada, g_pre_mix, g_post_mix, g_pre_ffn, g_post_ffn, w_in,
              lam_re, lam_im, log_dt, b_re, b_im, c_re, c_im, d_skip, w_glu, w_fft, sink,
              w_out, w_up, conv_w, conv_b, w_down):
    splits = [SSM_WIDTH, SSM_WIDTH + FFT_WIDTH, SSM_WIDTH + FFT_WIDTH + ATT_WIDTH,
              SSM_WIDTH + FFT_WIDTH + ATT_WIDTH + KV_WIDTH]
    for l in range(DEPTH):
        mod = (c @ w_ada[l] + b_ada[l])[:, None, :]
        sh_m, sc_m, gt_m, sh_f, sc_f, gt_f = jnp.split(mod, 6, axis=-1)

        h = rms_norm(x, g_pre_mix[l]) * (1.0 + sc_m) + sh_m
        z = h @ w_in[l]
        u, f, q, k, v = jnp.split(z, splits, axis=-1)
        y_ssm = s5_mixer(u, lam_re[l], lam_im[l], log_dt[l], b_re[l], b_im[l],
                         c_re[l], c_im[l], d_skip[l], w_glu[l])
        y_fft = fourier_mixer(f, w_fft[l])
        y_att = window_attention(q, k, v, sink[l])
        y = jnp.concatenate([y_ssm.astype(x.dtype), y_fft.astype(x.dtype), y_att.astype(x.dtype)], axis=-1) @ w_out[l]
        x = x + gt_m * rms_norm(y, g_post_mix[l])

        h = rms_norm(x, g_pre_ffn[l]) * (1.0 + sc_f) + sh_f
        up = dwconv3(h @ w_up[l], conv_w[l], conv_b[l])
        gate, val = jnp.split(up, 2, axis=-1)
        y = (jax.nn.gelu(gate) * val) @ w_down[l]
        x = x + gt_f * rms_norm(y, g_post_ffn[l])
    return x


N_BRANCHES = 4
BRANCH_WIDTH = D_MODEL // N_BRANCHES
LRU_CONV = 4
LRU_BLOCKS = 8
LRU_BLOCK = BRANCH_WIDTH // LRU_BLOCKS
LRU_C = 8.0
POOL_WINDOWS = (2, 4, 8, 16)
POOL_GROUP = BRANCH_WIDTH // len(POOL_WINDOWS)
HGRN_HEADS = 4
HGRN_DK = BRANCH_WIDTH // HGRN_HEADS
HGRN_DV = BRANCH_WIDTH // HGRN_HEADS
HGRN_CHUNK = 64
SCONV_WIDTH = 3
D_FF_2 = 4 * D_MODEL
N_MIX_SLOTS = 10
IN_WIDTH_2 = N_MIX_SLOTS * BRANCH_WIDTH + N_BRANCHES * D_MODEL
EPS = 1e-6


def rms_norm_2(x, gain):
    xf = x.astype(jnp.float32)
    y = xf * lax.rsqrt(jnp.mean(xf * xf, axis=-1, keepdims=True) + EPS)
    return (y * gain.astype(jnp.float32)).astype(x.dtype)

def causal_depthwise_conv(x, w):
    k = w.shape[0]
    c = x.shape[-1]
    return lax.conv_general_dilated(
        x, w.astype(x.dtype).reshape(k, 1, c), window_strides=(1,),
        padding=[(k - 1, 0)], dimension_numbers=("NWC", "WIO", "NWC"),
        feature_group_count=c)

def block_diag_linear(x, w, b):
    bsz, t, _ = x.shape
    nb, bi, bo = w.shape
    y = jnp.einsum("btnc,ncd->btnd", x.reshape(bsz, t, nb, bi), w.astype(x.dtype))
    return y.reshape(bsz, t, nb * bo) + b.astype(x.dtype)

def rg_lru_branch(x_in, gate_in, conv_w, conv_b, w_a, b_a, w_x, b_x, lam):
    xc = causal_depthwise_conv(x_in, conv_w) + conv_b.astype(x_in.dtype)
    r = jax.nn.sigmoid(block_diag_linear(xc, w_a, b_a).astype(jnp.float32))
    i = jax.nn.sigmoid(block_diag_linear(xc, w_x, b_x).astype(jnp.float32))
    log_a = -LRU_C * r * jax.nn.softplus(-lam.astype(jnp.float32))
    a = jnp.exp(log_a)
    mult = jnp.sqrt(-jnp.expm1(2.0 * log_a))
    u = mult * i * xc.astype(jnp.float32)

    def combine(left, right):
        a_l, h_l = left
        a_r, h_r = right
        return a_l * a_r, a_r * h_l + h_r

    _, h = lax.associative_scan(combine, (a, u), axis=1)
    return (h * jax.nn.gelu(gate_in.astype(jnp.float32))).astype(x_in.dtype)

def pool_branch(x, w, scale):
    bsz, t, _ = x.shape
    xf = x.astype(jnp.float32)
    cs0 = jnp.pad(jnp.cumsum(xf, axis=1), ((0, 0), (1, 0), (0, 0)))
    pos = jnp.arange(1, t + 1, dtype=jnp.float32)[:, None]
    means = []
    for g, win in enumerate(POOL_WINDOWS):
        c = cs0[..., g * POOL_GROUP:(g + 1) * POOL_GROUP]
        window_sum = c[:, 1:] - jnp.pad(c, ((0, 0), (win - 1, 0), (0, 0)))[:, :t]
        means.append(window_sum / jnp.minimum(pos, float(win)))
    d = (jnp.concatenate(means, axis=-1) - xf).astype(x.dtype)
    d = d.reshape(bsz, t, len(POOL_WINDOWS), POOL_GROUP)
    y = jnp.einsum("btgc,gcd->btgd", d, w.astype(x.dtype)).reshape(bsz, t, BRANCH_WIDTH)
    return y * scale.astype(x.dtype)

def hgrn2_chunked(q, log_f, k, v):
    bsz, t, h, dk = q.shape
    dv = v.shape[-1]
    nc = t // HGRN_CHUNK

    def chunks(z):
        return z.reshape(bsz, nc, HGRN_CHUNK, h, z.shape[-1]).transpose(1, 0, 3, 2, 4)

    causal = jnp.tril(jnp.ones((HGRN_CHUNK, HGRN_CHUNK), dtype=bool))[:, :, None]

    def step(state, inp):
        q_c, lf_c, k_c, v_c = inp
        b = jnp.cumsum(lf_c, axis=2)
        diff = b[:, :, :, None, :] - b[:, :, None, :, :]
        decay = jnp.exp(jnp.where(causal, diff, -jnp.inf))
        scores = jnp.einsum("bhtk,bhsk,bhtsk->bhts", q_c, k_c, decay)
        o = (jnp.einsum("bhts,bhsv->bhtv", scores, v_c)
             + jnp.einsum("bhtk,bhkv->bhtv", q_c * jnp.exp(b), state))
        b_last = b[:, :, -1:, :]
        state = (jnp.exp(b_last[:, :, 0, :, None]) * state
                 + jnp.einsum("bhsk,bhsv->bhkv", k_c * jnp.exp(b_last - b), v_c))
        return state, o

    s0 = jnp.zeros((bsz, h, dk, dv), jnp.float32)
    _, o = lax.scan(step, s0, (chunks(q), chunks(log_f), chunks(k), chunks(v)))
    return o.transpose(1, 0, 3, 2, 4).reshape(bsz, t, h, dv)

def hgrn2_branch(hq, hf, hi, hg, lb, norm_gain):
    bsz, t, _ = hq.shape
    shp_k = (bsz, t, HGRN_HEADS, HGRN_DK)
    lb = lb.reshape(HGRN_HEADS, HGRN_DK)
    f = lb + (1.0 - lb) * jax.nn.sigmoid(hf.astype(jnp.float32).reshape(shp_k))
    o = hgrn2_chunked(hq.astype(jnp.float32).reshape(shp_k), jnp.log(f), 1.0 - f,
                      hi.astype(jnp.float32).reshape(bsz, t, HGRN_HEADS, HGRN_DV))
    o = rms_norm_2(o, norm_gain).reshape(bsz, t, BRANCH_WIDTH)
    return (o * jax.nn.silu(hg.astype(jnp.float32))).astype(hq.dtype)

def short_conv_branch(gate_b, gate_c, xs, w):
    return gate_b * causal_depthwise_conv(gate_c * xs, w)

def second_inputs(seed: int = 0) -> dict:
    key = jax.random.key(seed)
    ks = jax.random.split(key, 24)
    f32 = jnp.float32
    W = BRANCH_WIDTH

    def nrm(k, shape, scale):
        return jax.random.normal(k, shape, f32) * scale

    def gain(k, shape):
        return 1.0 + 0.05 * jax.random.normal(k, shape, f32)

    u = jax.random.uniform(ks[12], (DEPTH, W), f32, minval=0.9, maxval=0.999)
    s = u ** (1.0 / LRU_C)
    lam = jnp.log(s) - jnp.log1p(-s)
    return {
        "x": jax.random.normal(ks[0], (BATCH, SEQ, D_MODEL), f32),
        "norm_mix_pre": gain(ks[1], (DEPTH, D_MODEL)),
        "norm_mix_post": gain(ks[2], (DEPTH, D_MODEL)),
        "norm_mlp_pre": gain(ks[3], (DEPTH, D_MODEL)),
        "norm_mlp_post": gain(ks[4], (DEPTH, D_MODEL)),
        "w_in": nrm(ks[5], (DEPTH, D_MODEL, IN_WIDTH_2), D_MODEL ** -0.5),
        "lru_conv_w": nrm(ks[6], (DEPTH, LRU_CONV, W), LRU_CONV ** -0.5),
        "lru_conv_b": nrm(ks[7], (DEPTH, W), 0.02),
        "lru_w_a": nrm(ks[8], (DEPTH, LRU_BLOCKS, LRU_BLOCK, LRU_BLOCK), LRU_BLOCK ** -0.5),
        "lru_b_a": nrm(ks[9], (DEPTH, W), 0.02),
        "lru_w_x": nrm(ks[10], (DEPTH, LRU_BLOCKS, LRU_BLOCK, LRU_BLOCK), LRU_BLOCK ** -0.5),
        "lru_b_x": nrm(ks[11], (DEPTH, W), 0.02),
        "lru_lambda": lam,
        "pool_w": nrm(ks[13], (DEPTH, len(POOL_WINDOWS), POOL_GROUP, POOL_GROUP), POOL_GROUP ** -0.5),
        "pool_scale": 1.0 + 0.1 * jax.random.normal(ks[14], (DEPTH, W), f32),
        "hgrn_lower_bound": nrm(ks[15], (DEPTH, W), 0.5),
        "hgrn_norm": gain(ks[16], (DEPTH, HGRN_DV)),
        "sconv_w": nrm(ks[17], (DEPTH, SCONV_WIDTH, W), SCONV_WIDTH ** -0.5),
        "w_branch": nrm(ks[18], (DEPTH, N_BRANCHES, W, D_MODEL), W ** -0.5),
        "w_out": nrm(ks[19], (DEPTH, D_MODEL, D_MODEL), D_MODEL ** -0.5),
        "w_up": nrm(ks[20], (DEPTH, D_MODEL, D_FF_2), D_MODEL ** -0.5),
        "w_down": nrm(ks[21], (DEPTH, D_FF_2, D_MODEL), D_FF_2 ** -0.5),
    }

def second_block(x, norm_mix_pre, norm_mix_post, norm_mlp_pre, norm_mlp_post, w_in,
              lru_conv_w, lru_conv_b, lru_w_a, lru_b_a, lru_w_x, lru_b_x, lru_lambda,
              pool_w, pool_scale, hgrn_lower_bound, hgrn_norm, sconv_w,
              w_branch, w_out, w_up, w_down):
    bsz, t, _ = x.shape
    lb_cum = jnp.cumsum(jax.nn.softmax(hgrn_lower_bound.astype(jnp.float32), axis=0), axis=0)
    lower_bounds = lb_cum - lb_cum[0:1]
    split_points = [BRANCH_WIDTH * (j + 1) for j in range(N_MIX_SLOTS)]
    h = x
    for l in range(DEPTH):
        u = rms_norm_2(h, norm_mix_pre[l])
        proj = jnp.einsum("btd,dp->btp", u, w_in[l])
        (a_x, a_gate, p_x, c_q, c_f, c_i, c_g, s_b, s_c, s_x,
         gate_logits) = jnp.split(proj, split_points, axis=-1)
        y_a = rg_lru_branch(a_x, a_gate, lru_conv_w[l], lru_conv_b[l], lru_w_a[l], lru_b_a[l],
                            lru_w_x[l], lru_b_x[l], lru_lambda[l])
        y_b = pool_branch(p_x, pool_w[l], pool_scale[l])
        y_c = hgrn2_branch(c_q, c_f, c_i, c_g, lower_bounds[l], hgrn_norm[l])
        y_d = short_conv_branch(s_b, s_c, s_x, sconv_w[l])
        ys = jnp.stack([y_a, y_b, y_c, y_d], axis=2)
        branch_out = jnp.einsum("btkc,kcd->btkd", ys, w_branch[l])
        gates = jax.nn.sigmoid(gate_logits.reshape(bsz, t, N_BRANCHES, D_MODEL))
        merged = jnp.sum(gates * branch_out, axis=2)
        mix = jnp.einsum("btd,de->bte", merged, w_out[l])
        h = h + rms_norm_2(mix, norm_mix_post[l])
        u = rms_norm_2(h, norm_mlp_pre[l])
        hid = jnp.square(jax.nn.relu(jnp.einsum("btd,df->btf", u, w_up[l])))
        m = jnp.einsum("btf,fd->btd", hid, w_down[l])
        h = h + rms_norm_2(m, norm_mlp_post[l])
    return h


def setup_inputs(seed=0):
    out = dict(first_inputs(seed))
    for name, value in second_inputs(seed + 1).items():
        if name != "x":
            out[name + "_2"] = value
    return out


def reference(
    x, c, w_ada, b_ada, g_pre_mix, g_post_mix, g_pre_ffn, g_post_ffn, w_in, lam_re, lam_im,
    log_dt, b_re, b_im, c_re, c_im, d_skip, w_glu, w_fft, sink, w_out, w_up, conv_w, conv_b,
    w_down, norm_mix_pre_2, norm_mix_post_2, norm_mlp_pre_2, norm_mlp_post_2, w_in_2,
    lru_conv_w_2, lru_conv_b_2, lru_w_a_2, lru_b_a_2, lru_w_x_2, lru_b_x_2, lru_lambda_2,
    pool_w_2, pool_scale_2, hgrn_lower_bound_2, hgrn_norm_2, sconv_w_2, w_branch_2, w_out_2,
    w_up_2, w_down_2,
):
    x = first_block(
        x, c, w_ada, b_ada, g_pre_mix, g_post_mix, g_pre_ffn, g_post_ffn, w_in, lam_re, lam_im,
        log_dt, b_re, b_im, c_re, c_im, d_skip, w_glu, w_fft, sink, w_out, w_up, conv_w, conv_b,
        w_down,
    )
    return second_block(
        x, norm_mix_pre_2, norm_mix_post_2, norm_mlp_pre_2, norm_mlp_post_2, w_in_2,
        lru_conv_w_2, lru_conv_b_2, lru_w_a_2, lru_b_a_2, lru_w_x_2, lru_b_x_2, lru_lambda_2,
        pool_w_2, pool_scale_2, hgrn_lower_bound_2, hgrn_norm_2, sconv_w_2, w_branch_2, w_out_2,
        w_up_2, w_down_2,
    )


_drawn_inputs = setup_inputs


def setup_inputs(seed=0):
    import zlib

    import numpy as np

    out = dict(_drawn_inputs(seed))
    spreads = {}
    factors = {'lam_re': 200.0,
     'conv_b': 8.0,
     'lru_b_a_2': 64.0,
     'lru_b_x_2': 30.236,
     'hgrn_norm_2': 14.111,
     'lam_im': 64.0,
     'log_dt': 45.984,
     'b_re': 45.0,
     'b_im': 46.184,
     'c_re': 44.528,
     'c_im': 43.184,
     'lru_conv_b_2': 4.29,
     'pool_scale_2': 3.91}
    for name, (base, spread) in spreads.items():
        noise = np.random.default_rng([zlib.crc32(name.encode()), seed]).standard_normal(out[name].shape)
        drawn = base * np.exp(spread * noise) if base else spread * noise
        out[name] = jnp.asarray(drawn.astype(out[name].dtype))
    for name, factor in factors.items():
        out[name] = (out[name] * factor).astype(out[name].dtype)
    return out
```

```python
import math
from contextlib import ExitStack

import numpy as np
import concourse.bass as bass
from concourse import mybir

F32 = mybir.dt.float32
F32R = mybir.dt.float32r
I32 = mybir.dt.int32
ALU = mybir.AluOpType
ACT = mybir.ActivationFunctionType
AX = mybir.AxisListType

P = 128
T = 1024
D = 1024
NK = 8
EPS = 1e-6
NG = 24
TWO_PI = 2.0 * math.pi
MAGIC = 12582912.0
PI_LO = 3.1415925


class Queue:

    def __init__(self, sem):
        self.sem = sem
        self.items = []
        self.n = 0
        self.seen = {}

    def wait(self, *marks):
        for sem, value in marks:
            if self.seen.get(sem.name, 0) < value:
                self.seen[sem.name] = value
                self.items.append((sem, value))

    def put(self, fn, *after):
        self.wait(*after)
        self.n += 1
        self.items.append((fn, self.sem, 1))
        return (self.sem, self.n)

    def quiet(self, fn, *after):
        self.wait(*after)
        self.items.append((fn, None, 0))

    def dma(self, fn, sem, total, *after):
        self.wait(*after)
        self.items.append((fn, sem, 16))
        return (sem, total)

    def emit(self, eng):
        for it in self.items:
            if len(it) == 2:
                eng.wait_ge(it[0], it[1])
            else:
                ins = it[0](eng)
                if it[1] is not None:
                    ins.then_inc(it[1], it[2])


def weave(*gens):
    live = [[g, n] for g, n in gens]
    while live:
        for entry in list(live):
            for _ in range(entry[1]):
                try:
                    next(entry[0])
                except StopIteration:
                    live.remove(entry)
                    break


PARAM_COLS = {}


def _cols(names):
    at = 0
    for name, n in names:
        PARAM_COLS[name] = (at, n)
        at += n
    return at


NPAR = _cols([
    ("c", 8), ("b_ada", 48), ("g_pre_mix", 8), ("g_post_mix", 8), ("g_pre_ffn", 8), ("g_post_ffn", 8),
    ("conv_w", 132), ("conv_b", 44), ("sink", 6), ("eps", 1),
    ("n1", 8), ("n2", 8), ("n3", 8), ("n4", 8),
    ("lcw", 8), ("lcb", 2), ("lba", 2), ("lbx", 2), ("lam", 2), ("pscale", 2), ("hlb", 2), ("hnorm", 2),
    ("scw", 6),
])

W_ORDER = [("w_in", 10), ("w_out", 8), ("ffn1", 0), ("w_in2", 52), ("w_out2", 8), ("ffn2", 0)]


def ffn_chunks(tiles):
    return [(c, min(4, tiles - c)) for c in range(0, tiles, 4)]


def build(nc, t):
    ctx = ExitStack()
    with ctx:
        names = [0]

        def sb(shape, dt=F32, c=ctx, side=None):
            names[0] += 1
            return c.enter_context(nc.sbuf_tensor(f"t{names[0]}", list(shape), dt, side=side))

        def sem(name):
            return ctx.enter_context(nc.semaphore(name))

        PSB = [ctx.enter_context(nc.psum_tensor(f"ps{i}", [P, 512], F32)) for i in range(4)]
        PSS = ctx.enter_context(nc.psum_tensor("pss", [P, 2, 512], F32))
        PSC = [ctx.enter_context(nc.psum_tensor(f"pc{i}", [P, 512], F32)) for i in range(2)]

        pe, act, dve, pool, sp = (Queue(sem(f"s_{n}")) for n in ("pe", "act", "dve", "pool", "sp"))
        engines = (pe, act, dve, pool)
        dma_total = {}
        dma_last = []
        phase = []

        def dma(q, key, out, in_, *after):
            if key not in dma_total:
                dma_total[key] = [sem("d_" + key), 0]
            e = dma_total[key]
            e[1] += 16
            m = q.dma(lambda g: g.dma_start(out, in_), e[0], e[1], *after, *phase)
            dma_last.append(m)
            return m

        def tt(q, out, a, b, op, *after):
            return q.put(lambda g: g.tensor_tensor(out, a, b, op), *after)

        def ts(q, out, a, s1, s2, op0, op1, *after):
            if op1 is None:
                return q.put(lambda g: g.tensor_scalar(out, a, s1, None, op0), *after)
            return q.put(lambda g: g.tensor_scalar(out, a, s1, s2, op0, op1), *after)

        def stt(out, a, s, b, op0, op1, *after):
            return dve.put(lambda g: g.scalar_tensor_tensor(out=out, in0=a, scalar=s, in1=b, op0=op0, op1=op1), *after)

        def av(out, a, func, *after, bias=None, scale=1.0, accum=None):
            kw = {"scale": scale}
            if bias is not None:
                kw["bias"] = bias
            if accum is not None:
                kw["accum_out"] = accum
            return act.put(lambda g: g.activation(out, a, func, **kw), *after)

        def memset(q, ap, v, *after):
            return q.put(lambda g: g.memset(ap, v), *after)

        def mm(out, lhsT, rhs, start, stop, last, *after):
            f = lambda g: g.matmul(out, lhsT, rhs, start=start, stop=stop)
            if last:
                return pe.put(f, *after)
            pe.quiet(f, *after)

        def transpose(out, in_, *after):
            return pe.put(lambda g: g.transpose(out, in_, ident[:, :]), *after)

        def fence():
            last = {s.name: (s, v) for s, v in sorted(dma_last, key=lambda m: m[1])}
            marks = [(q.sem, q.n) for q in engines] + list(last.values())
            del dma_last[:]
            phase[:] = marks
            for q in engines:
                q.wait(*marks)
            return marks

        par = sb([P, NPAR])
        ident = sb([P, P])
        onesm = sb([P, P])
        mod = sb([P, 48])
        gmod = sb([P, 6, 8])
        A = sb([P, 2, NK, T], F32R)
        wraw = sb([P, 3, 1024])
        whl = sb([P, 3, 2, 1024], F32R)

        def col(name, i=0, n=1):
            at = PARAM_COLS[name][0] + i
            return par[:, at:at + n]

        m_par = dma(act, "par", par[:, :], t["par"])
        m_ident = dma(act, "ident", ident[:, :], t["ident"])
        m_ones = memset(dve, onesm[:, :], 1.0)

        stream = []
        for i in (0, 1, 2, 6, 7, 3, 4, 5, 8, 9):
            stream.append(("w_in", i))
        stream += [("w_out", i) for i in range(8)]

        def ffn_order(name, tiles, per):
            out = []
            up = [(name + "u", i) for i in range(tiles * per)]
            dn = 0
            chunks = ffn_chunks(tiles)
            for n, (c, k) in enumerate(chunks):
                hi = min(c + k + 2, tiles)
                lo = 0 if n == 0 else min(c + 2, tiles)
                out += up[lo * per:hi * per]
                for _ in range(8 * k // 8):
                    out.append((name + "d", dn))
                    dn += 1
            return out

        stream += ffn_order("f1", 22, 2)
        order2 = list(range(6, 14)) + [0, 2, 1, 3, 4, 5, 14, 16, 18, 15, 17, 19]
        gates = [20 + k * 8 + j for j in range(8) for k in range(4)]
        stream += [("w_in2", i) for i in order2 + gates]
        stream += [("w_out2", i) for i in range(8)]
        stream += ffn_order("f2", 32, 1)
        state = {"load": 0, "split": 0, "use": 0}
        loaded, split_hi, split_lo, used = {}, {}, {}, {}

        def load_panel():
            n = state["load"]
            if n >= len(stream):
                return
            name, i = stream[n]
            s = n % 3
            after = [split_hi[n - 3], split_lo[n - 3]] if n >= 3 else []
            e = dma_total.setdefault(f"w{s}", [None, 0])
            if e[0] is None:
                e[0] = sem(f"d_w{s}")
            e[1] += 16
            loaded[n] = sp.dma(lambda g, s=s, a=t[name][i]: g.dma_start(wraw[:, s, :], a), e[0], e[1], *after)
            state["load"] += 1

        def split_panel():
            n = state["split"]
            if n >= len(stream):
                return
            s = n % 3
            after = [used[n - 3]] if n >= 3 else []
            split_hi[n] = av(whl[:, s, 0, :], wraw[:, s, :], ACT.Copy, loaded[n], *after)
            split_lo[n] = tt(pool, whl[:, s, 1, :], wraw[:, s, :], whl[:, s, 0, :].bitcast(F32), ALU.subtract,
                             loaded[n], split_hi[n])
            state["split"] += 1
            load_panel()

        for _ in range(3):
            load_panel()

        def panel(name, i):
            n = state["use"]
            assert stream[n] == (name, i), (stream[n], name, i)
            while state["split"] <= n:
                split_panel()
            state["use"] += 1
            return n

        def panel_done(n, mark):
            used[n] = mark
            while state["split"] <= min(n + 2, len(stream) - 1) and (state["split"] < 3 or state["split"] - 3 in used):
                split_panel()

        def gemm3(out, n, wcols, acts, ks, half, start, stop, last, *after):
            hi = [whl[:, n % 3, 0, c:c + 128] for c in wcols]
            lo = [whl[:, n % 3, 1, c:c + 128] for c in wcols]
            pe.wait(split_hi[n], split_lo[n], *after)
            r = None
            todo = []
            for i, k in enumerate(ks):
                xh = acts[:, 0, k, half * 512:half * 512 + 512]
                xl = acts[:, 1, k, half * 512:half * 512 + 512]
                todo += [(hi[i], xh), (hi[i], xl), (lo[i], xh)]
            for i, (w, x) in enumerate(todo):
                end = i == len(todo) - 1
                r = mm(out, w, x, start and i == 0, stop and end, last and end)
            return r

        banks = {}

        def bank(i):
            return [banks[i]] if i in banks else []

        turn = [0]

        def gemm_tile(name, i, evac, ready):
            n = panel(name, i)
            for half in range(2):
                b = turn[0] % 2
                turn[0] += 1
                m = gemm3(PSB[b][:, :], n, [128 * k for k in range(8)], A, range(8), half, True, True, True,
                          *bank(b), *ready)
                banks[b] = evac(half, PSB[b], m)
                if half == 1:
                    panel_done(n, m)
                yield

        def split_act(dst, j, src, cols, flip, *after):
            h = av(dst[:, 0, j, cols], src, ACT.Copy, *after)
            q = pool if flip else dve
            return tt(q, dst[:, 1, j, cols], src, dst[:, 0, j, cols].bitcast(F32), ALU.subtract, h, *after)

        ALL = slice(0, T)

        def rstd_of(ss, out, n, *after):
            last = None
            for half in range(2):
                c = slice(half * 512, half * 512 + 512)
                m = mm(PSC[half][:, :], onesm[:, :], ss[:, c], True, True, True, m_ones, *bank(6 + half), *after)
                m = av(out[:, c], PSC[half][:, :], ACT.Sqrt, m, m_par, bias=col("eps"), scale=1.0 / n)
                banks[6 + half] = m
                last = dve.put(lambda g, c=c: g.reciprocal(out[:, c], out[:, c]), m)
            return last

        class Norm:

            def __init__(self, ss, sq):
                self.ss, self.sq, self.n, self.done, self.marks = ss, sq, 0, [], [None, None]

            def add(self, src, *after):
                b = self.n % 2
                sq = self.sq[b]
                prior = [self.marks[b]] if self.marks[b] else []
                m = av(sq[:, :], src, ACT.Square, *after, *prior)
                if self.n == 0:
                    self.done = [dve.put(lambda g: g.tensor_copy(self.ss[:, :], sq[:, :]), m)]
                else:
                    self.done = [tt(dve, self.ss[:, :], self.ss[:, :], sq[:, :], ALU.add, m, *self.done)]
                self.marks[b] = self.done[0]
                self.n += 1

        def apply_norm(X, rstd, m_r, gain, shift, tmp, mx, free=()):
            last = []
            tm = [None, None]
            for j in range(8):
                b = j % 2
                prior = [tm[b]] if tm[b] else []
                m = tt(dve, tmp[b][:, :], X[:, j, :], rstd[:, :], ALU.mult, m_r, mx[j], *prior)
                if shift is None:
                    m = ts(dve, tmp[b][:, :], tmp[b][:, :], gain(j), None, ALU.mult, None, m)
                else:
                    m = ts(dve, tmp[b][:, :], tmp[b][:, :], gain(j), shift(j), ALU.mult, ALU.add, m)
                tm[b] = split_act(A, j, tmp[b][:, :], ALL, j % 2 == 1, m, *free)
                last.append(tm[b])
            return last

        ada_w = {}
        pc = ExitStack()
        acc = sb([P, 1024], c=pc, side="right")
        ada_ring = [sb([P, 1024], c=pc, side="right") for _ in range(2)]
        r8 = sb([P, NG])
        ada_used = {}
        nada = [0]
        acc_free = []

        def ada(j):
            m = None
            for k in range(8):
                n = nada[0]
                nada[0] += 1
                b = n % 2
                after = [ada_used[n - 2]] if n >= 2 else []
                ld = dma(act, f"ada{b}", ada_ring[b][:, :], t["w_ada"][j, k], *after)
                dma_last.pop()
                if k == 0:
                    m = ts(dve, acc[:, :], ada_ring[b][:, :], col("c", k), None, ALU.mult, None, ld, m_par, *acc_free)
                else:
                    m = stt(acc[:, :], ada_ring[b][:, :], col("c", k), acc[:, :], ALU.mult, ALU.add, ld, m)
                ada_used[n] = m
                if k % 4 == 3:
                    yield
            for i in range(8):
                r = mm(PSC[0][:, i:i + 1], acc[:, i * 128:i * 128 + 128], onesm[:, 0:1], True, True, i == 7, m, m_ones,
                       *bank(6))
            acc_free[:] = [r]
            r = tt(dve, mod[:, 8 * j:8 * j + 8], PSC[0][:, 0:8], col("b_ada", 8 * j, 8), ALU.add, r, m_par)
            banks[6] = r
            name = ["", "g_pre_mix", "g_post_mix", "", "g_pre_ffn", "g_post_ffn"][j]
            if j in (1, 4):
                r = ts(dve, gmod[:, j, :], mod[:, 8 * j:8 * j + 8], 1.0, None, ALU.add, None, r)
                r = tt(dve, gmod[:, j, :], gmod[:, j, :], col(name, 0, 8), ALU.mult, r)
            elif j in (2, 5):
                r = tt(dve, gmod[:, j, :], mod[:, 8 * j:8 * j + 8], col(name, 0, 8), ALU.mult, r)
            else:
                r = dve.put(lambda g: g.tensor_copy(gmod[:, j, :], mod[:, 8 * j:8 * j + 8]), r)
            ada_w[j] = r
            yield

        def gm(j):
            return lambda i: gmod[:, j, i:i + 1]

        with ExitStack() as c0:
            X = sb([P, NK, T], c=c0)
            ss = sb([P, T], c=c0)
            rstd = sb([P, T], c=c0)
            sq = [sb([P, T], c=c0) for _ in range(2)]
            tmp = [sb([P, T], c=c0) for _ in range(2)]
            mx = []
            nrm = Norm(ss, sq)
            for j in range(8):
                mx.append(dma(act, f"x{j}", X[:, j, :], t["xT"][j]))
            g0 = ada(0)
            g1 = ada(1)
            next(g0)
            for j in range(8):
                nrm.add(X[:, j, :], mx[j])
            for _ in g0:
                pass
            for _ in g1:
                pass
            m_r = rstd_of(ss, rstd, D, *nrm.done)
            mA = apply_norm(X, rstd, m_r, gm(1), gm(0), tmp, mx)
        fence()

        pu = ExitStack()
        uT = sb([P, 3, 8, 128], c=pu)
        fT = sb([P, 2, T], c=pu)
        qT = sb([P, 3, T], c=pu)
        kT = sb([P, T], c=pu)
        vT = sb([P, T], c=pu)
        m_z = {}
        m_us = []
        uscr, vscr, wscr, tscr, cscr, yscr, kscr = (t[n] for n in ("uscr", "vscr", "wscr", "tscr", "cscr", "yscr", "kscr"))

        def w_in_all():
            for i in (0, 1, 2, 6, 7, 3, 4, 5, 8, 9):
                def evac(half, ps, m, i=i):
                    if i < 3:
                        o = uT[:, i, :, half * 64:half * 64 + 64]
                        r = act.put(lambda g: g.activation(o, ps[:, :].rearrange("p (k t) -> p t k", t=8), ACT.Copy), m)
                    else:
                        dst = {6: kT, 7: vT}.get(i)
                        c = slice(half * 512, half * 512 + 512)
                        if dst is not None:
                            o = dst[:, c]
                        elif i < 6:
                            o = qT[:, i - 3, c]
                        else:
                            o = fT[:, i - 8, c]
                        r = av(o, ps[:, :], ACT.Copy, m)
                    m_z[i] = r
                    return r
                yield from gemm_tile("w_in", i, evac, mA)
                if i < 3:
                    m_us.append(dma(sp, "us", uscr[i], uT[:, i, :, :].rearrange("p t k -> p (t k)"), m_z[i]))

        def ada_rest():
            for j in (2, 3, 4, 5):
                yield from ada(j)

        def sinturns(q, out, ph, buf, shift, *after):
            if shift:
                m = ts(q, buf, ph, shift, None, ALU.add, None, *after)
                ph = buf
            else:
                m = None
            a = after + ((m,) if m else ())
            m = ts(q, out, ph, MAGIC, None, ALU.add, None, *a)
            m = ts(q, out, out, MAGIC, None, ALU.subtract, None, m)
            m = tt(q, buf, ph, out, ALU.subtract, m)
            m = ts(q, buf, buf, 0.4999999, -0.4999999, ALU.min, ALU.max, m)
            return av(out, buf, ACT.Sin, m, scale=TWO_PI)

        GB = 6

        def prep():
            with ExitStack() as cp:
                sp4 = sb([P, 3, NG], c=cp)
                Bt = sb([P, 2, NG, 16], c=cp)
                Ct = sb([P, 2, NG, 16], c=cp)
                ex = sb([P, 31], c=cp)
                msk = sb([P, 15], c=cp)
                kidx = sb([P, 128], c=cp)
                w = sb([P, 12, NG], c=cp)
                PW = sb([P, 2, NG, 31], c=cp)
                scr = sb([P, 3, NG * 31], c=cp)
                dI = sb([16, NG, 16], c=cp)
                big = sb([P, 2, GB * 240], c=cp)
                tm = sb([P, 2, GB * 240], c=cp)
                ldp = [dma(act, "sp4", sp4[:, :, :], t["ssm_p"]), dma(act, "Bt", Bt[:, :, :, :], t["ssm_b"]),
                       dma(act, "Ct", Ct[:, :, :, :], t["ssm_c"]), dma(act, "ex", ex[:, :], t["exps"]),
                       dma(act, "msk", msk[:, :], t["mask15"]), dma(act, "kidx", kidx[:, :], t["kidx"]),
                       dma(act, "dI", dI[:, :, :], t["dI"])]
                re, im, ld = sp4[:, 0, :], sp4[:, 1, :], sp4[:, 2, :]
                dt, ar, ai, n_, r_, mag, cs, sn, den, q1, q2, psi = (w[:, i, :] for i in range(12))
                m = av(dt, ld, ACT.Exp, *ldp)
                m1 = tt(dve, ar, re, dt, ALU.mult, m)
                m2 = tt(dve, ai, im, dt, ALU.mult, m)
                m = ts(dve, n_, ai, 1.0 / TWO_PI, MAGIC, ALU.mult, ALU.add, m2)
                m = ts(dve, n_, n_, MAGIC, None, ALU.subtract, None, m)
                r = ai
                for cc in (6.28125, 0.0019350051879882812, 3.01991605743e-07):
                    m = stt(r_, n_, -cc, r, ALU.mult, ALU.add, m)
                    r = r_
                mr = m
                yield
                mm_ = av(mag, ar, ACT.Exp, m1)
                m = ts(dve, q1, r_, PI_LO, -PI_LO, ALU.min, ALU.max, mr)
                ms = av(sn, q1, ACT.Sin, m)
                m = av(q2, q1, ACT.Abs, m)
                m = ts(dve, q2, q2, math.pi / 2, None, ALU.subtract, None, m)
                mc = av(cs, q2, ACT.Sin, m, scale=-1.0)
                mp = ts(dve, psi, r_, 1.0 / TWO_PI, None, ALU.mult, None, mr)
                m = tt(dve, cs, cs, mag, ALU.mult, mc, mm_)
                m = ts(dve, cs, cs, -1.0, None, ALU.add, None, m)
                m = tt(dve, sn, sn, mag, ALU.mult, ms, m)
                m = tt(dve, q1, re, re, ALU.mult, m)
                m = tt(dve, q2, im, im, ALU.mult, m)
                m = tt(dve, den, q1, q2, ALU.add, m)
                m = dve.put(lambda g: g.reciprocal(den, den), m)
                m = tt(dve, q1, cs, re, ALU.mult, m)
                m = tt(dve, q2, sn, im, ALU.mult, m)
                m = tt(dve, q1, q1, q2, ALU.add, m)
                m = tt(dve, n_, q1, den, ALU.mult, m)
                m = tt(dve, q1, sn, re, ALU.mult, m)
                m = tt(dve, q2, cs, im, ALU.mult, m)
                m = tt(dve, q1, q1, q2, ALU.subtract, m)
                m = tt(dve, q1, q1, den, ALU.mult, m)
                yield
                bc = lambda a: a.unsqueeze(2).broadcast_to([P, NG, 16])
                bb = [Bt[:, i, :, :] for i in range(2)]
                s16 = [scr[:, i, 0:NG * 16].rearrange("p (g c) -> p g c", c=16) for i in range(3)]
                m = tt(dve, s16[0], bb[0], bc(n_), ALU.mult, m)
                m = tt(dve, s16[1], bb[1], bc(q1), ALU.mult, m)
                m = tt(dve, s16[0], s16[0], s16[1], ALU.subtract, m)
                m = tt(dve, s16[1], bb[0], bc(q1), ALU.mult, m)
                m = tt(dve, s16[2], bb[1], bc(n_), ALU.mult, m)
                m = tt(dve, bb[1], s16[1], s16[2], ALU.add, m)
                m = dve.put(lambda g: g.tensor_copy(bb[0], s16[0]), m)
                mB = m
                yield
                bg = lambda a: a.unsqueeze(2).broadcast_to([P, NG, 31])
                be = ex[:, :].unsqueeze(1).broadcast_to([P, NG, 31])
                s31 = [scr[:, i, :].rearrange("p (g e) -> p g e", e=31) for i in range(3)]
                m = tt(dve, s31[0], bg(ar), be, ALU.mult, mB)
                mg = av(s31[0], s31[0], ACT.Exp, m)
                m = tt(dve, s31[1], bg(psi), be, ALU.mult, m, mp)
                m = sinturns(dve, PW[:, 1, :, :], s31[1], s31[2], 0.0, m)
                m = sinturns(dve, PW[:, 0, :, :], s31[1], s31[2], 0.25, m)
                m = tt(dve, PW[:, 0, :, :], PW[:, 0, :, :], s31[0], ALU.mult, m, mg)
                m = tt(dve, PW[:, 1, :, :], PW[:, 1, :, :], s31[0], ALU.mult, m)
                bm = msk[:, :].unsqueeze(1).broadcast_to([P, NG, 15])
                m = tt(dve, PW[:, 0, :, 0:15], PW[:, 0, :, 0:15], bm, ALU.mult, m)
                mP = tt(dve, PW[:, 1, :, 0:15], PW[:, 1, :, 0:15], bm, ALU.mult, m)
                yield
                m = ts(dve, q1, psi, 8.0, None, ALU.mult, None, mP)
                m = ts(dve, q2, q1, MAGIC, None, ALU.add, None, m)
                m = ts(dve, q2, q2, MAGIC, None, ALU.subtract, None, m)
                m = tt(dve, q1, q1, q2, ALU.subtract, m)
                m8 = m
                mr8 = av(r8[:, :], ar, ACT.Exp, m1, scale=8.0)
                m_r8.append(mr8)

                def cmul(src, nblk, off, gs, dst_re, dst_im, sgn_im, after):
                    ng = gs.stop - gs.start
                    n = ng * nblk * 16
                    t0 = tm[:, 0, 0:n].rearrange("p (g e c) -> p g e c", e=nblk, c=16)
                    t1 = tm[:, 1, 0:n].rearrange("p (g e c) -> p g e c", e=nblk, c=16)
                    pr, pi = (PW[:, i, gs, off:off + nblk].unsqueeze(3).broadcast_to([P, ng, nblk, 16]) for i in range(2))
                    sr, si = (src[:, i, gs, :].unsqueeze(2).broadcast_to([P, ng, nblk, 16]) for i in range(2))
                    a = tt(dve, t0, sr, pr, ALU.mult, *after)
                    b = tt(pool, t1, si, pi, ALU.mult, *after)
                    a = tt(dve, dst_re, t0, t1, ALU.subtract, a, b)
                    b = tt(dve, t0, sr, pi, ALU.mult, a)
                    c = tt(pool, t1, si, pr, ALU.mult, a)
                    b = tt(dve, dst_im, t0, t1, ALU.add, b, c)
                    if sgn_im:
                        b = ts(dve, dst_im, dst_im, -1.0, None, ALU.mult, None, b)
                    return b

                m = mP
                free = []
                for b0 in range(0, NG, GB):
                    gs = slice(b0, b0 + GB)
                    v4 = lambda i, e: big[:, i, 0:GB * e * 16].rearrange("p (g e c) -> p g e c", e=e, c=16)
                    m = cmul(Ct, 8, 15, gs, v4(0, 8), v4(1, 8), True, (m, *free))
                    yield
                    d1 = dma(sp, f"vs{b0}", vscr[:, :, gs, :], big[:, :, 0:GB * 128].rearrange("p i (g n) -> p i g n", n=128), m)
                    m = cmul(Bt, 8, 23, gs, v4(0, 8), v4(1, 8), False, (m, d1))
                    yield
                    for i in range(2):
                        for g0 in range(0, GB, 3):
                            for g in range(g0, g0 + 3):
                                r = transpose(PSC[1][:, (g - g0) * 128:(g - g0) * 128 + 128],
                                              big[:, i, g * 128:g * 128 + 128], m, m_ident, *bank(7))
                            r = dve.put(lambda g_, i=i, g0=g0: g_.tensor_copy(tm[:, i, g0 * 128:g0 * 128 + 384],
                                                                           PSC[1][:, 0:384]), r, m)
                            banks[7] = r
                            yield
                    d2 = dma(sp, f"ws{b0}", wscr[:, :, gs, :], tm[:, :, 0:GB * 128].rearrange("p i (g n) -> p i g n", n=128), r)
                    m = cmul(Ct, 15, 0, gs, v4(0, 15), v4(1, 15), True, (r, d2))
                    yield
                    for g0 in range(0, GB, 3):
                        for g in range(g0, g0 + 3):
                            o = PSC[1][32 * (g - g0):32 * (g - g0) + 16, 0:240]
                            for i in range(2):
                                rhs = big[:, i, g * 240:g * 240 + 240]
                                r = mm(o, Bt[:, i, b0 + g, :], rhs, i == 0, i == 1, i == 1, m, *bank(7))
                        ko = tm[:, 0, g0 * 240:g0 * 240 + 240]
                        for g in range(g0, g0 + 3):
                            kk = 32 * (g - g0)
                            r = dve.put(lambda g_, kk=kk, ko=ko: g_.tensor_copy(ko[kk:kk + 16, :], PSC[1][kk:kk + 16, 0:240]), r)
                        banks[7] = r
                        for g in range(g0, g0 + 3):
                            kk = 32 * (g - g0)
                            dm = dma(sp, f"ks{b0}_{g0}", kscr[b0 + g], ko[kk:kk + 16, :], r)
                        yield
                    free = [dm]
                    m = r
                m_k = dm
                kb = tm[0:16, 0, 0:NG * 16].rearrange("p (g n) -> p g n", n=16)
                l1 = dma(sp, "kl", kb, kscr[:, :, 112:128].rearrange("g c n -> c g n"), m_k, d2)
                m = tt(dve, kb, kb, dI[:, :, :], ALU.add, l1, *ldp)
                m_k2 = dma(sp, "kl", kscr[:, :, 112:128].rearrange("g c n -> c g n"), kb, m)
                m_prep.extend([m_k2, d1, d2])
                yield
                for b0 in range(0, NG, GB):
                    gs = slice(b0, b0 + GB)
                    n = GB * 128
                    ph = tm[:, 0, 0:n].rearrange("p (g k) -> p g k", k=128)
                    bf = tm[:, 1, 0:n].rearrange("p (g k) -> p g k", k=128)
                    o = [big[:, i, 0:n].rearrange("p (g k) -> p g k", k=128) for i in range(2)]
                    m = tt(dve, ph, q1[:, gs].unsqueeze(2).broadcast_to([P, GB, 128]),
                           kidx[:, :].unsqueeze(1).broadcast_to([P, GB, 128]), ALU.mult, m8, m, m_k2, *free)
                    m = sinturns(dve, o[1], ph, bf, 0.0, m)
                    yield
                    m = sinturns(dve, o[0], ph, bf, 0.25, m)
                    free = [dma(sp, f"cs{b0}", cscr[:, :, gs, :], big[:, :, 0:n].rearrange("p i (g n) -> p i g n", n=128), m)]
                    yield
                m_prep.extend(free)

        m_r8, m_prep = [], []
        weave((w_in_all(), 1), (prep(), 2), (ada_rest(), 1))
        fence()
        pc.close()

        with ExitStack() as c2:
            U = sb([P, NG, 128], c=c2)
            bias = sb([P, 6, 384], c=c2)
            m_bias = dma(sp, "bias", bias[:, :, :], t["bias"])
            vrow = sb([P, 8, 128], c=c2)
            scb = [sb([P, 2, 384], c=c2) for _ in range(2)]
            pts = [sb([P, 384], c=c2) for _ in range(2)]
            small = sb([P, 2, 16], c=c2)
            NB = 4
            WV = sb([P, 4, NB, 128], c=c2)
            Wb, Vb = WV[:, 0:2, :, :], WV[:, 2:4, :, :]
            Tb = sb([P, NB, 128], c=c2)
            Cb = sb([P, 2, NB, 128], c=c2)
            Hb = sb([P, 2, NB, 128], c=c2)
            Mt = sb([P, 2, NB, 128], c=c2)
            Rb = sb([P, NB, 128], c=c2)
            nz = sb([P, 128], c=c2)
            glf = WV[:, :, :, :].rearrange("p a b c -> p (a b c)")[:, 0:1152]
            glw = glf.rearrange("p (a b c) -> p a b c", a=3, b=3)
            m_nz = dma(sp, "nz", nz[:, :], t["nz"])
            ld_u = []
            for s in range(8):
                src = bass.AP(tensor=uscr.tensor, offset=128 * s, ap=[[1024, 16], [16 * 1024, NG], [1, 128]])
                ld_u.append(dma(sp, "ul", U[16 * s:16 * s + 16, :, :], src, *m_us))
            m_y, m_ys = {}, []

            def ssm():
                wfree, tfree, vfree, cfree, hfree = [], [], [], [], []
                for b0 in range(0, NG, NB):
                    gs = slice(b0, b0 + NB)
                    lw = dma(sp, "lw", Wb[:, :, :, :], wscr[:, :, gs, :], *m_prep, *wfree)
                    lt = None
                    for s in range(8):
                        src = bass.AP(tensor=kscr.tensor, offset=b0 * 3840 + (7 - s) * 16,
                                      ap=[[240, 16], [3840, NB], [1, 128]])
                        lt = dma(sp, "lt", Tb[16 * s:16 * s + 16, :, :], src, *m_prep, *tfree)
                    lc = dma(sp, "lc", Cb[:, :, :, :], cscr[:, :, gs, :], *m_prep, *cfree)
                    lv = dma(sp, "lv", Vb[:, :, :, :], vscr[:, :, gs, :], *m_prep, *vfree)
                    for i in range(2):
                        for g in range(NB):
                            r = mm(PSC[i][:, g * 128:g * 128 + 128], Wb[:, i, g, :], U[:, b0 + g, :], True, True,
                                   g == NB - 1, lw, ld_u[-1], *bank(6 + i))
                        m_x = r
                    wfree = [m_x]
                    mrb = dve.put(lambda g_, gs=gs: g_.tensor_tensor(
                        Rb[:, :, :], nz[:, :].unsqueeze(1).broadcast_to([P, NB, 128]),
                        r8[:, gs].unsqueeze(2).broadcast_to([P, NB, 128]), ALU.mult), m_nz, *m_r8)
                    yield
                    x = [PSC[i][:, :].rearrange("p (g k) -> p g k", k=128) for i in range(2)]
                    cs, sn = Cb[:, 0, :, :], Cb[:, 1, :, :]
                    h0, h1 = Hb[:, 0, :, :], Hb[:, 1, :, :]
                    t0, t1 = Mt[:, 0, :, :], Mt[:, 1, :, :]
                    a = tt(dve, h0, x[0], cs, ALU.mult, m_x, lc, *hfree)
                    b = tt(dve, t1, x[0], sn, ALU.mult, a)
                    c = tt(dve, t0, x[1], sn, ALU.mult, b)
                    banks[6] = b
                    d = tt(dve, h1, x[1], cs, ALU.mult, c)
                    banks[7] = d
                    a = tt(pool, h0, h0, t0, ALU.add, c)
                    d = tt(dve, h1, h1, t1, ALU.subtract, d)
                    yield
                    for i in range(2):
                        for lo, rev in ((0, 1), (64, -1)):
                            pr = slice(lo, lo + 64)
                            src = Hb[pr, i, :, :].rearrange("p g k -> p (g k)")[:, ::rev]
                            dst = Mt[pr, i, :, :].rearrange("p g k -> p (g k)")[:, ::rev]
                            rr = Rb[pr, :, :].rearrange("p g k -> p (g k)")[:, ::rev]
                            sc_m = dve.put(lambda g_, src=src, dst=dst, rr=rr: g_.tensor_tensor_scan(
                                dst, rr, src, 0.0, ALU.mult, ALU.add), a, d, mrb)
                    z = memset(pool, Hb[0:64, :, :, 0:1], 0.0, sc_m)
                    z2 = memset(pool, Hb[64:128, :, :, 127:128], 0.0, sc_m)
                    yield
                    for i in range(2):
                        for lo in (0, 64):
                            pr = slice(lo, lo + 64)
                            so = slice(0, 127) if lo == 0 else slice(1, 128)
                            do = slice(1, 128) if lo == 0 else slice(0, 127)
                            c_a = Cb[pr, 0 if i == 0 else 1, :, so]
                            c_b = Cb[pr, 1 if i == 0 else 0, :, so]
                            o = Hb[pr, i, :, do]
                            tmpa = bias_t[pr, :, 0:127]
                            ma = tt(dve, o, Mt[pr, 0, :, so], c_a, ALU.mult, sc_m, z, z2)
                            mb = tt(pool, tmpa, Mt[pr, 1, :, so], c_b, ALU.mult, sc_m, *hx)
                            mh = tt(dve, o, o, tmpa, ALU.subtract if i == 0 else ALU.add, ma, mb)
                            hx[:] = [mh]
                    cfree = [mh]
                    yield
                    for g in range(NB):
                        o = PSC[0][:, g * 128:g * 128 + 128]
                        mm(o, Tb[:, g, :], U[:, b0 + g, :], True, False, False, lt, *bank(6))
                        mm(o, Vb[:, 0, g, :], Hb[:, 0, g, :], False, False, False, lv, mh)
                        r = mm(o, Vb[:, 1, g, :], Hb[:, 1, g, :], False, True, g == NB - 1)
                    tfree, vfree, hfree = [r], [r], [r]
                    r = av(U[:, gs, :], PSC[0][:, :].rearrange("p (g k) -> p g k", k=128), ACT.Copy, r)
                    banks[6] = r
                    for s in range(8):
                        dst = bass.AP(tensor=yscr.tensor, offset=b0 * 16384 + 128 * s,
                                      ap=[[1024, 16], [16 * 1024, NB], [1, 128]])
                        m_ys.append(None)
                        m_ys[-1] = dma(sp, f"ys{b0}", dst, U[16 * s:16 * s + 16, gs, :], r)
                    yield
                m_glw = dma(sp, "glw", glf, t["w_glu"].rearrange("p a b c -> p (a b c)"), *vfree, *wfree)
                ly = []
                for i in range(3):
                    ly.append(dma(sp, "yl", uT[:, i, :, :].rearrange("p t k -> p (t k)"), yscr[i], *m_ys[7::8], *m_us))
                yf = uT[:, :, :, :].rearrange("p i t k -> p i (t k)")
                ge = [av(yf[:, i, :], yf[:, i, :], ACT.Gelu_apprx_tanh, ly[2]) for i in range(3)]
                yield
                gp = [None, None]
                sg = U[:, 0:16, :].rearrange("p (a g) k -> p a (g k)", a=4)
                for j in range(3):
                    for half in range(2):
                        c = slice(half * 512, half * 512 + 512)
                        for i in range(3):
                            r = mm(PSC[half][:, :], glw[:, i, j, :], yf[:, i, c], i == 0, i == 2, i == 2, m_glw, *ge,
                                   *bank(6 + half))
                        b = half
                        prior = [gp[b]] if gp[b] else []
                        m = av(sg[:, b, :], PSC[half][:, :], ACT.Sigmoid, r, *m_ys[7::8], *prior)
                        banks[6 + half] = m
                        m = tt(dve, sg[:, b, :], sg[:, b, :], yf[:, j, c], ALU.mult, m)
                        oh, ol = (A[:, e, j, :].rearrange("p (k t) -> p t k", t=8)[:, 4 * half:4 * half + 4, :] for e in range(2))
                        sv = sg[:, b, :].rearrange("p (t k) -> p t k", k=128)
                        h = av(oh, sv, ACT.Copy, m)
                        gp[b] = tt(dve, ol, sv, oh.bitcast(F32), ALU.subtract, h)
                        m_y[("s", j, half)] = gp[b]
                        yield

            bias_t = sb([P, NB, 128], c=c2)
            hx = []

            def attention():
                for b in range(2):
                    for n in range(4):
                        r = transpose(PSB[2][:, n * 128:n * 128 + 128], vT[:, (4 * b + n) * 128:(4 * b + n) * 128 + 128],
                                      m_z[7], m_ident, *bank(2))
                    r = av(vrow[:, 4 * b:4 * b + 4, :], PSB[2][:, :].rearrange("p (n d) -> p n d", d=128), ACT.Copy, r)
                    banks[2] = r
                m_v = r
                u = 0
                pt_used = [[], []]
                pt_n = 0
                sc_used = [[], []]
                for i in range(3):
                    for n in range(8):
                        b = u % 2
                        u += 1
                        lo = 128 if n == 0 else 0
                        hi = 256 if n == 7 else 384
                        kc = slice((n - 1) * 128 + lo, (n - 1) * 128 + hi)
                        w = hi - lo
                        for g in range(2):
                            pr = slice(64 * g, 64 * g + 64)
                            r = mm(PSS[:, g, 0:w], qT[pr, i, n * 128:n * 128 + 128], kT[pr, kc], True, True, True,
                                   m_z[6], m_z[3], m_z[4], m_z[5], *bank(4))
                        yield
                        sc = scb[b]
                        sm = small[:, b, :]
                        m = stt(sc[:, :, 0:w], PSS[:, :, 0:w], 0.125, bias[:, 2 * i:2 * i + 2, lo:hi], ALU.mult, ALU.add,
                                r, m_bias, *sc_used[b])
                        banks[4] = m
                        m = dve.put(lambda g_, sm=sm, sc=sc, w=w: g_.tensor_reduce(sm[:, 0:2], sc[:, :, 0:w], AX.X, ALU.max), m)
                        m = tt(dve, sm[:, 0:2], sm[:, 0:2], col("sink", 2 * i, 2), ALU.max, m)
                        m = ts(dve, sm[:, 2:4], sm[:, 0:2], -1.0, None, ALU.mult, None, m)
                        m2 = tt(dve, sm[:, 4:6], col("sink", 2 * i, 2), sm[:, 0:2], ALU.subtract, m)
                        for g in range(2):
                            e = av(sc[:, g, 0:w], sc[:, g, 0:w], ACT.Exp, m, bias=sm[:, 2 + g:3 + g], accum=sm[:, 6 + g:7 + g])
                        e2 = av(sm[:, 8:10], sm[:, 4:6], ACT.Exp, m2)
                        yield
                        m = tt(dve, sm[:, 8:10], sm[:, 8:10], sm[:, 6:8], ALU.add, e, e2)
                        m = dve.put(lambda g_, sm=sm: g_.reciprocal(sm[:, 10:12], sm[:, 8:10]), m)
                        for g in range(2):
                            mn = ts(dve, sc[:, g, 0:w], sc[:, g, 0:w], sm[:, 10 + g:11 + g], None, ALU.mult, None, m, e)
                        yield
                        nb = w // 128
                        for g in range(2):
                            for s in range(nb):
                                r = transpose(PSB[2][:, s * 128:s * 128 + 128], sc[:, g, s * 128:s * 128 + 128], mn, *bank(2))
                            pb = pt_n % 2
                            pt_n += 1
                            r = av(pts[pb][:, 0:w], PSB[2][:, 0:w], ACT.Copy, r, *pt_used[pb])
                            banks[2] = r
                            yield
                            o = PSB[3][64 * g:64 * g + 64, (n % 4) * 128:(n % 4) * 128 + 128]
                            for s in range(nb):
                                blk = (n - 1) + lo // 128 + s
                                q = mm(o, vrow[:, blk, 64 * g:64 * g + 64], pts[pb][:, s * 128:s * 128 + 128], s == 0,
                                       s == nb - 1, s == nb - 1, r, m_v, *bank(3))
                            pt_used[pb] = [q]
                            sc_used[b] = [q]
                        if n % 4 == 3:
                            c = slice((n - 3) * 128, (n + 1) * 128)
                            h = act.put(lambda g_, c=c, i=i: g_.activation(A[:, 0, 5 + i, c], PSB[3][:, :], ACT.Copy), q)
                            l = tt(dve, A[:, 1, 5 + i, c], PSB[3][:, :], A[:, 0, 5 + i, c].bitcast(F32), ALU.subtract, h)
                            banks[3] = l
                            m_y[("a", i, n // 4)] = l
                        yield

            weave((ssm(), 1), (attention(), 3))
        m_f = fence()
        with ExitStack() as c2:
            FA = sb([P, 8, 2, 256], c=c2)
            dft = [sb([P, 1024], c=c2) for _ in range(4)]
            c64 = sb([P, 2, 128], c=c2)
            wf = sb([P, 2, 128], c=c2)
            WC = sb([P, 2, 2, 128], c=c2)
            l1 = dma(sp, "c64", c64[:, :, :], t["c64"], *m_f)
            l2 = dma(sp, "wf", wf[:, :, :], t["w_fft"], *m_f)
            for pr in range(2):
                for i in range(2):
                    r = mm(PSC[0][:, (pr * 2 + i) * 128:(pr * 2 + i) * 128 + 128], c64[:, i, :], wf[:, pr, :], True, True,
                           True, l1, l2, *bank(6))
            r = dve.put(lambda g: g.tensor_copy(WC[:, :, :, :].rearrange("p a b c -> p (a b c)"), PSC[0][:, :]), r)
            banks[6] = r
            m_wc = r
            fa = []
            for tt_ in range(8):
                b = 6 + tt_ % 2
                for pr in range(2):
                    r = mm(PSC[tt_ % 2][:, pr * 256:pr * 256 + 256], fT[:, pr, tt_ * 128:tt_ * 128 + 128],
                           WC[:, pr, :, :].rearrange("p a b -> p (a b)"), True, True, True, m_wc, m_z[9], m_z[8], *bank(b))
                o = FA[:, tt_, :, :].rearrange("p a b -> p (a b)")
                if tt_ % 2:
                    r = av(o, PSC[1][:, :], ACT.Copy, r)
                else:
                    r = dve.put(lambda g, o=o: g.tensor_copy(o, PSC[0][:, :]), r)
                banks[b] = r
                fa.append(r)
            used_d = {}
            n = 0
            for half in range(2):
                for tp in range(8):
                    s = n % 4
                    after = [used_d[n - 4]] if n >= 4 else []
                    ld = dma(sp, f"dft{s}", dft[s][:, :], t["dft"][half, tp], *m_f, *after)
                    for i in range(2):
                        for pr in range(2):
                            r = mm(PSB[pr][:, :], FA[:, tp, pr, i * 128:i * 128 + 128], dft[s][:, i * 512:i * 512 + 512],
                                   tp == 0 and i == 0, tp == 7 and i == 1, True, ld, fa[tp], *bank(pr))
                    used_d[n] = r
                    n += 1
                for pr in range(2):
                    c = slice(half * 512, half * 512 + 512)
                    h = av(A[:, 0, 3 + pr, c], PSB[pr][:, :], ACT.Copy, r)
                    l = tt(dve, A[:, 1, 3 + pr, c], PSB[pr][:, :], A[:, 0, 3 + pr, c].bitcast(F32), ALU.subtract, h)
                    banks[pr] = l
                    m_y[("f", pr, half)] = l
        pu.close()
        fence()

        def out_proj(name, Y, nrm, ready, b0):
            for j in range(8):
                def evac(half, ps, m, j=j):
                    return av(Y[:, j, half * 512:half * 512 + 512], ps[:, :], ACT.Copy, m, *b0)
                for _ in gemm_tile(name, j, evac, ready):
                    pass
                last = banks[(turn[0] - 1) % 2]
                nrm.add(Y[:, j, :], last)

        def residual(Y, nrm, xsrc, xdst, post, pre, shift, c, xin=None, final=False):
            X = sb([P, NK, T], c=c)
            rstd = sb([P, T], c=c)
            tmp = nrm.sq
            f = fence()
            key = f"xl{names[0]}"
            mx = [dma(act, f"{key}_{j}", X[:, j, :], xsrc[j], *f) for j in range(8)]
            m_r = rstd_of(nrm.ss, rstd, D, *nrm.done)
            n2 = Norm(nrm.ss, nrm.sq)
            outm = []
            st = []
            for j in range(8):
                m = tt(dve, Y[:, j, :], Y[:, j, :], rstd[:, :], ALU.mult, m_r)
                m = stt(X[:, j, :], Y[:, j, :], post(j), X[:, j, :], ALU.mult, ALU.add, m, mx[j])
                outm.append(m)
                st.append(dma(pool, f"{key}s", xdst[j], X[:, j, :], m))
                if not final:
                    n2.add(X[:, j, :], m)
            if final:
                return st
            m_r = rstd_of(n2.ss, rstd, D, *n2.done)
            return apply_norm(X, rstd, m_r, pre, shift, tmp, outm)

        def norm_bufs(c):
            return Norm(sb([P, T], c=c), [sb([P, T], c=c) for _ in range(2)])

        with ExitStack() as c3:
            Y = sb([P, NK, T], c=c3)
            nrm = norm_bufs(c3)
            out_proj("w_out", Y, nrm, list(m_y.values()), ())
            mA = residual(Y, nrm, t["xT"], t["xs"], gm(2), gm(4), gm(3), c3)
        fence()

        def ffn(name, tiles, per, make_hid, Y, c):
            H = sb([P, 2, 6, T], F32R, c=c)
            hid_m, hid_free = {}, {}
            chunks = ffn_chunks(tiles)
            dn = [0]
            y_m = {}

            def up(i):
                for _ in make_hid(i, H, hid_free.get(i - 6), hid_m):
                    pass

            def down(ci):
                c0, k = chunks[ci]
                per_panel = 8 // k
                for pn in range(8 // per_panel):
                    n = panel(name + "d", dn[0])
                    dn[0] += 1
                    for mi in range(per_panel):
                        j = pn * per_panel + mi
                        for half in range(2):
                            b = turn[0] % 2
                            turn[0] += 1
                            r = gemm3(PSB[b][:, :], n, [(mi * k + kk) * 128 for kk in range(k)], H,
                                      [(c0 + kk) % 6 for kk in range(k)], half, True, True, True, *bank(b),
                                      *[hid_m[c0 + kk] for kk in range(k)])
                            o = Y[:, j, half * 512:half * 512 + 512]
                            if ci == 0:
                                banks[b] = dve.put(lambda g, o=o, b=b: g.tensor_copy(o, PSB[b][:, :]), r)
                            else:
                                banks[b] = tt(dve, o, o, PSB[b][:, :], ALU.add, r, y_m[(j, half)])
                            y_m[(j, half)] = banks[b]
                        if ci == len(chunks) - 1:
                            yield (j, y_m[(j, 0)], y_m[(j, 1)])
                    panel_done(n, r)
                for kk in range(k):
                    hid_free[c0 + kk] = r

            for n, (c0, k) in enumerate(chunks):
                lo = 0 if n == 0 else min(c0 + 2, tiles)
                for i in range(lo, min(c0 + k + 2, tiles)):
                    up(i)
                yield from down(n)

        with ExitStack() as c4:
            Y = sb([P, NK, T], c=c4)
            with ExitStack() as c5:
                pad = [sb([P, T + 2], c=c5) for _ in range(3)]
                cv = [sb([P, T], c=c5) for _ in range(2)]
                pm = [memset(dve, p[:, 0:T + 2:T + 1], 0.0) for p in pad]
                pad_free = [[], [], []]
                cv_free = [[], []]
                np_ = [0]

                def hid1(i, H, free, hid_m):
                    done = []
                    for e in range(2):
                        pi = np_[0] % 3
                        np_[0] += 1
                        pd = pad[pi]

                        def evac(half, ps, m):
                            return av(pd[:, 1 + half * 512:513 + half * 512], ps[:, :], ACT.Copy, m, *pad_free[pi])
                        yield from gemm_tile("f1u", 2 * i + e, evac, mA)
                        last = banks[(turn[0] - 1) % 2]
                        ch = i + 22 * e
                        w = lambda j: col("conv_w", 44 * j + ch)
                        o = cv[e]
                        m = ts(dve, o[:, :], pd[:, 0:T], w(0), col("conv_b", ch), ALU.mult, ALU.add, last, *pm, *cv_free[e])
                        m = stt(o[:, :], pd[:, 1:T + 1], w(1), o[:, :], ALU.mult, ALU.add, m)
                        m = stt(o[:, :], pd[:, 2:T + 2], w(2), o[:, :], ALU.mult, ALU.add, m)
                        pad_free[pi] = [m]
                        if e == 0:
                            m = av(o[:, :], o[:, :], ACT.Gelu_apprx_tanh, m)
                        done.append(m)
                    m = tt(dve, cv[0][:, :], cv[0][:, :], cv[1][:, :], ALU.mult, *done)
                    cv_free[1] = [m]
                    f = [free] if free else []
                    m = split_act(H, i % 6, cv[0][:, :], ALL, True, m, *f)
                    cv_free[0] = [m]
                    hid_m[i] = m

                yd = [x for x in ffn("f1", 22, 2, hid1, Y, c5)]
            f = fence()
            nrm = norm_bufs(c4)
            for j, a, b in yd:
                nrm.add(Y[:, j, :], a, b)
            mA = residual(Y, nrm, t["xs"], t["xs2"], gm(5), lambda j: col("n1", j), None, c4)
        fence()

        pb2 = ExitStack()
        c6 = ExitStack()
        bd = sb([P, 8, 128], c=c6)
        lbd = dma(sp, "bd", bd[:, :, :], t["bd"])
        cc = sb([P, 64], c=c6)

        def stor(n):
            return sb([P, n, T], c=c6)

        hz = stor(8)
        z2 = stor(0 + 4)
        m_h = {}

        def proj(i, dst, marks, free=()):
            def evac(half, ps, m):
                r = av(dst[:, half * 512:half * 512 + 512], ps[:, :], ACT.Copy, m, *free)
                marks[i] = r
                return r
            yield from gemm_tile("w_in2", i, evac, mA)

        def proj_h():
            for i in range(6, 14):
                yield from proj(i, hz[:, i - 6, :], m_h)

        for _ in proj_h():
            pass

        yb_m = {}

        def hgrn():
            with ExitStack() as ch:
                bcum = sb([P, T], c=ch)
                E = sb([P, T], c=ch)
                Qp = sb([P, T], c=ch)
                Kp = sb([P, T], c=ch)
                Kt = sb([P, T], c=ch)
                kdt = sb([P, 128], c=ch)
                vr = sb([P, 8, 128], c=ch)
                st = sb([P, 128], c=ch)
                msk = sb([P, 8, 128], I32, c=ch)
                rst = sb([P, T], c=ch)
                lm = dma(sp, "msk2", msk[:, :, :], t["hmask"])
                lr = dma(sp, "rst", rst[:, :], t["rst"])
                m = av(cc[:, 0:2], col("hlb", 0, 2), ACT.Copy, m_par)
                m = tt(dve, cc[:, 2:4], cc[:, 0:2], cc[:, 0:2], ALU.subtract, m)
                m = av(cc[:, 2:4], cc[:, 2:4], ACT.Exp, m)
                m = dve.put(lambda g: g.reciprocal(cc[:, 4:6], cc[:, 2:4]), m)
                m = tt(dve, cc[:, 2:4], cc[:, 2:4], cc[:, 4:6], ALU.mult, m)
                m = tt(dve, cc[:, 6:8], cc[:, 2:4], cc[:, 2:4], ALU.subtract, m)
                mlb = ts(dve, cc[:, 8:10], cc[:, 6:8], -1.0, 1.0, ALU.mult, ALU.add, m)
                yield
                last = []
                for tl in range(2):
                    q, f, v, g = (hz[:, 2 * e + tl, :] for e in range(4))
                    mz = [m_h[6 + 2 * e + tl] for e in range(4)]
                    m = av(f, f, ACT.Sigmoid, mz[1])
                    m = ts(dve, f, f, cc[:, 8 + tl:9 + tl], cc[:, 6 + tl:7 + tl], ALU.mult, ALU.add, m, mlb)
                    mk = ts(dve, Kt[:, :], f, -1.0, 1.0, ALU.mult, ALU.add, m, *last)
                    m = ts(dve, f, f, 2.0 ** -63, None, ALU.max, None, m)
                    m = av(f, f, ACT.Ln, m)
                    mb = dve.put(lambda g_, f=f: g_.tensor_tensor_scan(bcum[:, :], rst[:, :], f, 0.0, ALU.mult, ALU.add),
                                 m, lr, *last)
                    yield
                    for b in range(2):
                        for n in range(4):
                            r = transpose(PSB[2][:, n * 128:n * 128 + 128],
                                          v[:, (4 * b + n) * 128:(4 * b + n) * 128 + 128], mz[2], *bank(2))
                        r = av(vr[:, 4 * b:4 * b + 4, :], PSB[2][:, :].rearrange("p (n d) -> p n d", d=128), ACT.Copy, r, *last)
                        banks[2] = r
                    mv = r
                    yield
                    lv_free = list(last)
                    for L in range(8):
                        if L == 7:
                            mq, mk2 = mz[0], mk
                            qs, ks = q, Kt[:, :]
                        else:
                            w = 1 << L
                            nb = T // (2 * w)
                            b3 = bcum[:, :].rearrange("p (n w) -> p n w", w=2 * w)
                            e3 = E[:, :].rearrange("p (n w) -> p n w", w=2 * w)
                            m = tt(dve, e3, b3, b3[:, :, w - 1:w].broadcast_to([P, nb, 2 * w]), ALU.subtract, mb, *lv_free)
                            m = av(E[:, :], E[:, :], ACT.Abs, m)
                            me = av(E[:, :], E[:, :], ACT.Exp, m, scale=-1.0)
                            mq = tt(dve, Qp[:, :], q, E[:, :], ALU.mult, me, mz[0], *lv_free)
                            mk2 = tt(pool, Kp[:, :], Kt[:, :], E[:, :], ALU.mult, me, mk, *lv_free)
                            qs, ks = Qp[:, :], Kp[:, :]
                        yield
                        for h in range(2):
                            pr = slice(64 * h, 64 * h + 64)
                            for b in range(2):
                                pb = (h * 2 + b) % 2
                                for n in range(4):
                                    cs_ = slice((4 * b + n) * 128, (4 * b + n) * 128 + 128)
                                    r = mm(PSS[:, pb, n * 128:n * 128 + 128], ks[pr, cs_], qs[pr, cs_], True, True, True,
                                           mq, mk2, *bank(4 + pb))
                                o = hs[:, h, b * 512:b * 512 + 512].rearrange("p (n s) -> p n s", s=128)
                                mkx = msk[:, L, :].unsqueeze(1).broadcast_to([P, 4, 128])
                                src = PSS[:, pb, :].rearrange("p (n s) -> p n s", s=128)
                                r2 = dve.put(lambda g_, o=o, mkx=mkx, src=src: g_.copy_predicated(o, mkx, src), r, lm, *hs_m)
                                banks[4 + pb] = r2
                                if L:
                                    pass
                            yield
                        hs_m[:] = [r2]
                        lv_free = [r]
                    m_sc = r2
                    m = memset(dve, st[:, :], 0.0, *last)
                    ms = m
                    b3 = bcum[:, :].rearrange("p (n w) -> p n w", w=128)
                    e3 = E[:, :].rearrange("p (n w) -> p n w", w=128)
                    m = av(E[:, :], bcum[:, :], ACT.Exp, mb, *lv_free)
                    mq = tt(dve, Qp[:, :], q, E[:, :], ALU.mult, m, *lv_free)
                    m = tt(dve, e3, b3, b3[:, :, 127:128].broadcast_to([P, 8, 128]), ALU.subtract, mq)
                    m = av(E[:, :], E[:, :], ACT.Exp, m, scale=-1.0)
                    mk2 = tt(dve, Kp[:, :], Kt[:, :], E[:, :], ALU.mult, m)
                    m_el = av(cc[:, 16:24], b3[:, :, 127], ACT.Exp, mb, *last)
                    yield
                    for n in range(8):
                        cs_ = slice(n * 128, n * 128 + 128)
                        o = PSB[3][:, (n % 4) * 128:(n % 4) * 128 + 128]
                        for h in range(2):
                            oh = PSB[3][64 * h:64 * h + 64, (n % 4) * 128:(n % 4) * 128 + 128]
                            mm(oh, vr[:, n, 64 * h:64 * h + 64], hs[:, h, cs_], True, False, False, mv, m_sc, *bank(3))
                            ro = mm(oh, st[:, 64 * h:64 * h + 64], Qp[:, cs_], False, True, True, mq, ms)
                        if n < 7:
                            r = transpose(PSB[2][:, 0:128], Kp[:, cs_], mk2, *bank(2))
                            r = av(kdt[:, :], PSB[2][:, 0:128], ACT.Copy, r, *kd_free)
                            banks[2] = r
                            r = mm(PSS[:, 0, 0:128], kdt[:, :], vr[:, n, :], True, True, True, r, *bank(4))
                            kd_free[:] = [r]
                            for h in range(2):
                                pr = slice(64 * h, 64 * h + 64)
                                c_ = slice(64 * h, 64 * h + 64)
                                ms = stt(st[pr, c_], st[pr, c_], cc[pr, 16 + n:17 + n], PSS[pr, 0, c_], ALU.mult, ALU.add,
                                         r, ro, m_el)
                            banks[4] = ms
                        if n % 4 == 3:
                            c = slice((n - 3) * 128, (n + 1) * 128)
                            mo = av(E[:, c], PSB[3][:, :], ACT.Copy, ro, mk2)
                            banks[3] = mo
                        yield
                    m = av(Qp[:, :], E[:, :], ACT.Square, mo, ro)
                    mg = av(g, g, ACT.Silu, mz[3])
                    for half in range(2):
                        c = slice(half * 512, half * 512 + 512)
                        r = mm(PSS[:, half, :], bd[:, 6, :], Qp[:, c], True, True, True, m, lbd, *bank(4 + half))
                        m2 = av(Kp[:, c], PSS[:, half, :], ACT.Sqrt, r, bias=col("eps"), scale=1.0 / 64)
                        banks[4 + half] = m2
                    m = dve.put(lambda g_: g_.reciprocal(Kp[:, :], Kp[:, :]), m2)
                    m = tt(dve, E[:, :], E[:, :], Kp[:, :], ALU.mult, m)
                    m = stt(E[:, :], E[:, :], col("hnorm", tl), g, ALU.mult, ALU.mult, m, mg)
                    yb_m[4 + tl] = dma(sp, f"yh{tl}", t["yb"][4 + tl], E[:, :], m)
                    last = [m, m2, yb_m[4 + tl]]
                    yield

        hs = sb([P, 2, T], c=c6)
        hs_m = [memset(dve, hs[:, :, :], 0.0)]
        kd_free = []
        gm_ = {}

        def rest():
            a = z2
            for tl in range(2):
                for e in range(2):
                    yield from proj(2 * e + tl, a[:, e, :], gm_, tuple(rfree))
                with ExitStack() as cr:
                    pass
                x, g = a[:, 0, :], a[:, 1, :]
                xc, r_ = a[:, 2, :], a[:, 3, :]
                mx_, mg_ = gm_[tl], gm_[2 + tl]
                w = lambda j: col("lcw", 2 * j + tl)
                m = ts(dve, xc, x, w(3), col("lcb", tl), ALU.mult, ALU.add, mx_, *rfree)
                for d in (1, 2, 3):
                    m = stt(xc[:, d:T], x[:, 0:T - d], w(3 - d), xc[:, d:T], ALU.mult, ALU.add, m)
                yield
                m0 = m
                for half in range(2):
                    c = slice(half * 512, half * 512 + 512)
                    r = mm(PSC[0][:, :], bd[:, tl, :], xc[:, c], True, True, True, m0, lbd, *bank(6))
                    m = av(r_[:, c], PSC[0][:, :], ACT.Sigmoid, r, bias=col("lba", tl))
                    banks[6] = m
                    r = mm(PSC[1][:, :], bd[:, 2 + tl, :], xc[:, c], True, True, True, m0, lbd, *bank(7))
                    m = av(x[:, c], PSC[1][:, :], ACT.Sigmoid, r, m0, bias=col("lbx", tl))
                    banks[7] = m
                yield
                m1 = tt(dve, x, x, xc, ALU.mult, m)
                m2 = ts(dve, r_, r_, cc[:, 40 + tl:41 + tl], None, ALU.mult, None, m, m_sp)
                m = av(xc, r_, ACT.Tanh, m2, m1, scale=-1.0)
                ma = av(r_, r_, ACT.Exp, m)
                m3 = av(tq[:, :], r_, ACT.Square, ma, *rfree)
                m3 = stt(xc, tq[:, :], 1.0, xc, ALU.add, ALU.mult, m3, m)
                m3 = av(xc, xc, ACT.Sqrt, m3)
                m3 = tt(dve, x, x, xc, ALU.mult, m3)
                yield
                m3 = dve.put(lambda g_, x=x, r_=r_, xc=xc: g_.tensor_tensor_scan(xc, r_, x, 0.0, ALU.mult, ALU.add), m3, ma)
                mg_ = av(g, g, ACT.Gelu_apprx_tanh, mg_)
                m3 = tt(dve, g, xc, g, ALU.mult, m3, mg_)
                yb_m[tl] = dma(sp, f"yr{tl}", t["yb"][tl], g, m3)
                rfree[:] = [m3, yb_m[tl]]
                yield
            for tl in range(2):
                yield from proj(4 + tl, a[:, 0, :], gm_, tuple(rfree))
                x = a[:, 0, :]
                s2, s4 = a[:, 2, :], a[:, 3, :]

                def dbl(dst, src, w, pr, *after):
                    m = dve.put(lambda g_: g_.tensor_copy(dst[pr, 0:w], src[pr, 0:w]), *after)
                    return tt(dve, dst[pr, w:T], src[pr, w:T], src[pr, 0:T - w], ALU.add, *after, m)
                al = slice(0, 128)
                up_ = slice(64, 128)
                if tl == 0:
                    m = dbl(s2, x, 1, al, gm_[4 + tl], *rfree)
                    m = dbl(s4, s2, 2, up_, m)
                    m = dve.put(lambda g_: g_.tensor_copy(s4[0:64, :], s2[0:64, :]), m)
                else:
                    m = dbl(s2, x, 1, al, gm_[4 + tl], *rfree)
                    m = dbl(s4, s2, 2, al, m)
                    m = dbl(s2, s4, 4, al, m)
                    m = dbl(s4, s2, 8, up_, m)
                    m = dve.put(lambda g_: g_.tensor_copy(s4[0:64, :], s2[0:64, :]), m)
                yield
                m0 = tt(dve, s4[:, 0:16], s4[:, 0:16], prec[:, tl, 0:16], ALU.mult, m, lpr)
                m = ts(dve, s4[:, 16:T], s4[:, 16:T], prec[:, tl, 15:16], None, ALU.mult, None, m, lpr, m0)
                m = tt(dve, s4, s4, x, ALU.subtract, m)
                for half in range(2):
                    c = slice(half * 512, half * 512 + 512)
                    r = mm(PSC[half][:, :], bd[:, 4 + tl, :], s4[:, c], True, True, True, m, lbd, *bank(6 + half))
                    r = ts(dve, s2[:, c], PSC[half][:, :], col("pscale", tl), None, ALU.mult, None, r)
                    banks[6 + half] = r
                yb_m[2 + tl] = dma(sp, f"yp{tl}", t["yb"][2 + tl], s2, r)
                rfree[:] = [r, yb_m[2 + tl]]
                yield
            for tl in range(2):
                for e in range(3):
                    yield from proj(14 + 2 * e + tl, a[:, e, :], gm_, tuple(rfree))
                w = lambda j: col("scw", 2 * j + tl)
                m = tt(dve, a[:, 1, :], a[:, 1, :], a[:, 2, :], ALU.mult, gm_[16 + tl], gm_[18 + tl])
                m = ts(dve, a[:, 2, :], a[:, 1, :], w(2), None, ALU.mult, None, m)
                for d in (1, 2):
                    m = stt(a[:, 2, d:T], a[:, 1, 0:T - d], w(2 - d), a[:, 2, d:T], ALU.mult, ALU.add, m)
                m = tt(dve, a[:, 0, :], a[:, 0, :], a[:, 2, :], ALU.mult, m, gm_[14 + tl])
                yb_m[6 + tl] = dma(sp, f"yc{tl}", t["yb"][6 + tl], a[:, 0, :], m)
                rfree[:] = [m, yb_m[6 + tl]]
                yield

        rfree = []
        tq = sb([P, T], c=c6)
        prec = sb([P, 2, 16], c=c6)
        lpr = dma(sp, "prec", prec[:, :, :], t["prec"])
        lam = col("lam", 0, 2)
        s_ = lambda i: cc[:, 24 + 2 * i:26 + 2 * i]
        m = ts(dve, s_(0), lam, -1.0, 0.0, ALU.mult, ALU.max, m_par)
        m2 = av(s_(1), lam, ACT.Abs, m_par)
        m2 = av(s_(1), s_(1), ACT.Exp, m2, scale=-1.0)
        m = ts(dve, s_(2), s_(1), 1.0, None, ALU.add, None, m2, m)
        m2 = av(s_(3), s_(2), ACT.Ln, m)
        m = ts(dve, s_(2), s_(2), -1.0, None, ALU.add, None, m, m2)
        m = ts(dve, s_(4), s_(2), 0.0, None, ALU.is_equal, None, m)
        m = tt(dve, s_(3), s_(3), s_(1), ALU.mult, m)
        m = tt(dve, s_(5), s_(4), s_(1), ALU.mult, m)
        m = tt(dve, s_(3), s_(3), s_(5), ALU.add, m)
        m = tt(dve, s_(2), s_(2), s_(4), ALU.add, m)
        m = dve.put(lambda g: g.reciprocal(s_(2), s_(2)), m)
        m = tt(dve, s_(3), s_(3), s_(2), ALU.mult, m)
        m = tt(dve, s_(3), s_(3), s_(0), ALU.add, m)
        m_sp = ts(dve, cc[:, 40:42], s_(3), -8.0, None, ALU.mult, None, m)

        weave((rest(), 1), (hgrn(), 2))
        fence()
        c6.close()

        with ExitStack() as c7:
            M = sb([P, NK, T], c=c7)
            wb = [sb([P, 2, 128], c=c7) for _ in range(4)]
            sgt = [sb([P, T], c=c7) for _ in range(2)]
            wb_free = {}
            sg_free = [[], []]
            nb_ = 0
            m_m = {}
            f0 = fence()
            YB = sb([P, 8, T], c=c7)
            my = [dma(act, f"ybl{i}", YB[:, i, :], t["yb"][i], *f0, *yb_m.values()) for i in range(8)]
            for j in range(8):
                for k in range(4):
                    s = nb_ % 4
                    after = [wb_free[nb_ - 4]] if nb_ >= 4 else []
                    lw = dma(act, f"wb{s}", wb[s][:, :, :], t["w_branch"][j, k], *f0, *after)
                    b = nb_ % 2

                    def evac(half, ps, m):
                        return av(sgt[b][:, half * 512:half * 512 + 512], ps[:, :], ACT.Sigmoid, m, *sg_free[b])
                    for _ in gemm_tile("w_in2", 20 + 8 * k + j, evac, mA):
                        pass
                    mg = banks[(turn[0] - 1) % 2]
                    for half in range(2):
                        c = slice(half * 512, half * 512 + 512)
                        for e in range(2):
                            r = mm(PSC[half][:, :], wb[s][:, e, :], YB[:, 2 * k + e, c], e == 0, e == 1, e == 1, lw,
                                   my[2 * k + e], *bank(6 + half))
                        if k == 0:
                            r = tt(dve, M[:, j, c], sgt[b][:, c], PSC[half][:, :], ALU.mult, r, mg)
                        else:
                            r = tt(dve, sgt[b][:, c], sgt[b][:, c], PSC[half][:, :], ALU.mult, r, mg)
                        banks[6 + half] = r
                        if k:
                            r = tt(dve, M[:, j, c], M[:, j, c], sgt[b][:, c], ALU.add, r, m_m[(j, half)])
                        m_m[(j, half)] = r
                    wb_free[nb_] = r
                    sg_free[b] = [r]
                    nb_ += 1
            mlast = used[state["use"] - 1]
            mA = [split_act(A, j, M[:, j, :], ALL, j % 2 == 1, m_m[(j, 0)], m_m[(j, 1)], mlast) for j in range(8)]
            f = fence()
        pb2.close()
        with ExitStack() as c8:
            Y = sb([P, NK, T], c=c8)
            nrm = norm_bufs(c8)
            out_proj("w_out2", Y, nrm, mA, ())
            mA = residual(Y, nrm, t["xs2"], t["xs"], lambda j: col("n2", j), lambda j: col("n3", j), None, c8)
        fence()

        with ExitStack() as c9:
            Y = sb([P, NK, T], c=c9)
            with ExitStack() as c10:
                rl = [sb([P, T], c=c10) for _ in range(2)]
                rl_free = [[], []]

                def hid2(i, H, free, hid_m):
                    b = i % 2

                    def evac(half, ps, m):
                        return av(rl[b][:, half * 512:half * 512 + 512], ps[:, :], ACT.Relu, m, *rl_free[b])
                    yield from gemm_tile("f2u", i, evac, mA)
                    last = banks[(turn[0] - 1) % 2]
                    f = [free] if free else []
                    m = tt(dve, rl[b][:, :], rl[b][:, :], rl[b][:, :], ALU.mult, last)
                    m = split_act(H, i % 6, rl[b][:, :], ALL, True, m, *f)
                    rl_free[b] = [m]
                    hid_m[i] = m

                yd = [x for x in ffn("f2", 32, 1, hid2, Y, c10)]
            fence()
            nrm = norm_bufs(c9)
            for j, a, b in yd:
                nrm.add(Y[:, j, :], a, b)
            st = residual(Y, nrm, t["xs"], t["out"], lambda j: col("n4", j), None, None, c9, final=True)
        pool.wait(st[-1])
        for key, (s, total) in dma_total.items():
            sp.wait((s, total))

        assert state["use"] == len(stream)
        block = ctx.enter_context(nc.Block())

        @block.sync
        def _(eng):
            sp.emit(eng)

        @block.gpsimd
        def _(eng):
            pool.emit(eng)

        @block.scalar
        def _(eng):
            act.emit(eng)

        @block.vector
        def _(eng):
            dve.emit(eng)

        @block.tensor
        def _(eng):
            pe.emit(eng)


def _panels(w):
    k, m = w.shape
    a = w.reshape(k // 128, 128, m // 128, 128).transpose(2, 1, 0, 3)
    return np.ascontiguousarray(a).reshape(m // 128, 128, k)


def _down(w):
    out = []
    a = w.reshape(-1, 128, 8, 128)
    for c, k in ffn_chunks(a.shape[0]):
        b = a[c:c + k].transpose(2, 1, 0, 3)
        per = 8 // k
        for j in range(0, 8, per):
            out.append(b[j:j + per].transpose(1, 0, 2, 3).reshape(128, 1024))
    return np.ascontiguousarray(np.stack(out))


def _vec(v):
    return v.reshape(-1, 128).T


def _constants():
    f = np.float32
    out = {"ident": np.eye(128, dtype=f)}
    n = np.arange(1024)
    ang = (n[:, None] * n[None, :]) % 1024 * (2 * np.pi / 1024)
    c, s = np.cos(ang), -np.sin(ang)
    d = np.empty((2, 8, 128, 1024), f)
    for h in range(2):
        for tp in range(8):
            r = slice(tp * 128, tp * 128 + 128)
            d[h, tp, :, 0:512] = c[r, h * 512:h * 512 + 512]
            d[h, tp, :, 512:] = s[r, h * 512:h * 512 + 512]
    out["dft"] = d
    m = np.arange(64)
    a64 = (m[:, None] * m[None, :]) % 64 * (2 * np.pi / 64)
    c64 = np.zeros((128, 2, 128))
    for b in range(2):
        q = slice(64 * b, 64 * b + 64)
        c64[q, 0, q] = np.cos(a64) / 256
        c64[q, 1, q] = np.sin(a64) / 256
    out["c64"] = c64.astype(f)
    dist = np.abs(np.arange(128)[:, None] + 128 - np.arange(384)[None, :]).astype(f)
    slopes = np.exp2(f(-8.0) * np.arange(1, 9 - 2, dtype=f) / f(6))
    bias = np.empty((128, 6, 384), f)
    for i in range(3):
        for g in range(2):
            bias[:, 2 * i + g, :] = np.where(dist <= 128, -slopes[3 * g + i] * dist, f(-1e30))
    out["bias"] = bias
    ex = np.zeros((128, 31), f)
    msk = np.zeros((128, 15), f)
    j = np.arange(15)
    ex[:64, 0:15] = np.maximum(j - 7, 0)
    ex[64:, 0:15] = np.maximum(7 - j, 0)
    msk[:64] = j >= 7
    msk[64:] = j <= 7
    e = np.arange(8)
    ex[:64, 15:23] = e + 1
    ex[64:, 15:23] = 8 - e
    ex[:64, 23:31] = 7 - e
    ex[64:, 23:31] = e
    out["exps"], out["mask15"] = ex, msk
    k = np.arange(128, dtype=f)
    out["kidx"] = np.concatenate([np.tile(k, (64, 1)), np.tile(127 - k, (64, 1))])
    nz = np.ones((128, 128), f)
    nz[:64, 0] = 0
    nz[64:, 127] = 0
    out["nz"] = nz
    hm = np.zeros((128, 8, 128), np.int32)
    sidx, tidx = np.arange(128)[:, None], np.arange(128)[None, :]
    for L in range(7):
        w = 1 << L
        hm[:, L, :] = (sidx // (2 * w) == tidx // (2 * w)) & (sidx % (2 * w) < w) & (tidx % (2 * w) >= w)
    hm[:, 7, :] = sidx == tidx
    out["hmask"] = hm
    rst = np.ones((128, 1024), f)
    rst[:, ::128] = 0
    out["rst"] = rst
    pos = np.arange(1, 1025, dtype=f)
    prec = np.empty((128, 2, 16), f)
    for i, w in enumerate((2, 4, 8, 16)):
        prec[64 * (i % 2):64 * (i % 2) + 64, i // 2, :] = 1.0 / np.minimum(pos[:16], w)
    out["prec"] = prec
    return out


def _blocks(mats, n):
    per = 128 // n
    out = np.zeros((mats.shape[0] // per, 128, 128), mats.dtype)
    for i in range(mats.shape[0]):
        r = slice((i % per) * n, (i % per) * n + n)
        out[i // per, r, r] = mats[i]
    return out


def _layout(v):
    a = dict(_constants())
    a["xT"] = np.ascontiguousarray(v["x"][0].T).reshape(8, 128, 1024)
    a["w_ada"] = np.ascontiguousarray(v["w_ada"][0].reshape(8, 128, 6, 1024).transpose(2, 0, 1, 3))
    pair = np.concatenate([np.arange(64) + 64 * h for i in range(3) for h in (i, 3 + i)])
    w_in = v["w_in"][0]
    cols = np.concatenate([np.arange(384), 640 + pair, np.arange(1024, 1280), np.arange(384, 640)])
    a["w_in"] = _panels(w_in[:, cols])
    rows = np.concatenate([np.arange(640), 640 + pair])
    a["w_out"] = _panels(v["w_out"][0][rows])
    up = v["w_up"][0].reshape(1024, 2, 22, 128).transpose(0, 2, 1, 3).reshape(1024, 5632)
    a["f1u"] = _panels(up)
    a["f1d"] = _down(v["w_down"][0])
    a["w_in2"] = _panels(v["w_in_2"][0])
    a["w_out2"] = _panels(v["w_out_2"][0])
    a["f2u"] = _panels(v["w_up_2"][0])
    a["f2d"] = _down(v["w_down_2"][0])
    wb = v["w_branch_2"][0].reshape(4, 2, 128, 8, 128)
    a["w_branch"] = np.ascontiguousarray(wb.transpose(3, 0, 2, 1, 4))
    a["w_glu"] = np.ascontiguousarray(v["w_glu"][0].reshape(3, 128, 3, 128).transpose(1, 0, 2, 3))
    a["w_fft"] = np.ascontiguousarray(_blocks(v["w_fft"][0], 64).transpose(1, 0, 2))
    one = np.ones((64, 64), np.float32)
    bd = np.concatenate([_blocks(v["lru_w_a_2"][0], 32), _blocks(v["lru_w_x_2"][0], 32), _blocks(v["pool_w_2"][0], 64),
                         _blocks(np.stack([one, one]), 64), np.zeros((1, 128, 128), np.float32)])
    a["bd"] = np.ascontiguousarray(bd.transpose(1, 0, 2))
    G, S = 24, 64
    p = np.empty((2, S, 3, G), np.float32)
    p[:, :, 0] = v["lam_re"][0].transpose(0, 2, 1)
    p[:, :, 1] = v["lam_im"][0].transpose(0, 2, 1)
    p[:, :, 2] = v["log_dt"][0][:, None, :]
    a["ssm_p"] = p.reshape(128, 3, G)
    b = np.stack([v["b_re"][0], v["b_im"][0]]).transpose(1, 3, 0, 2, 4)
    a["ssm_b"] = np.ascontiguousarray(b).reshape(128, 2, G, 16)
    c = np.stack([v["c_re"][0], v["c_im"][0]]).transpose(3, 0, 1, 2)
    a["ssm_c"] = np.ascontiguousarray(np.concatenate([c, c]))
    dI = np.zeros((16, G, 16), np.float32)
    i16 = np.arange(16)
    dI[i16, :, i16] = v["d_skip"][0].reshape(G, 16).T
    a["dI"] = dI
    par = np.empty((128, NPAR), np.float32)

    def put(name, x):
        at, n = PARAM_COLS[name]
        par[:, at:at + n] = x

    put("c", _vec(v["c"][0]))
    put("b_ada", _vec(v["b_ada"][0]))
    for n in ("g_pre_mix", "g_post_mix", "g_pre_ffn", "g_post_ffn"):
        put(n, _vec(v[n][0]))
    put("conv_w", _vec(v["conv_w"][0]))
    put("conv_b", _vec(v["conv_b"][0]))
    s = v["sink"][0]
    put("sink", np.array([s[3 * g + i] for i in range(3) for g in range(2)], np.float32)[None, :])
    put("eps", np.float32(EPS))
    for n, k in (("n1", "norm_mix_pre_2"), ("n2", "norm_mix_post_2"), ("n3", "norm_mlp_pre_2"), ("n4", "norm_mlp_post_2"),
                 ("lcw", "lru_conv_w_2"), ("lcb", "lru_conv_b_2"), ("lba", "lru_b_a_2"), ("lbx", "lru_b_x_2"),
                 ("lam", "lru_lambda_2"), ("pscale", "pool_scale_2"), ("hlb", "hgrn_lower_bound_2"), ("scw", "sconv_w_2")):
        put(n, _vec(v[k][0]))
    put("hnorm", np.concatenate([v["hgrn_norm_2"][0]] * 2)[:, None])
    a["par"] = par
    return a


SCRATCH = {
    "uscr": (3, 128, 1024), "yscr": (3, 128, 1024), "vscr": (128, 2, NG, 128), "wscr": (128, 2, NG, 128),
    "tscr": (128, 8), "cscr": (128, 2, NG, 128), "kscr": (NG, 16, 240), "yb": (8, 128, 1024), "xs": (8, 128, 1024), "xs2": (8, 128, 1024),
}


def kernel(**inputs):
    import concourse.bacc as _bacc
    from concourse.bass_utils import run_bass_kernel_spmd as _run

    arrays = {k: np.ascontiguousarray(a) for k, a in _layout({k: np.asarray(a) for k, a in inputs.items()}).items()}
    nc = _bacc.Bacc("TRN2", target_bir_lowering=False, num_devices=1)
    t = {}
    for k, a in arrays.items():
        t[k] = nc.dram_tensor("in_" + k, a.shape, mybir.dt.from_np(a.dtype), kind="ExternalInput").ap()
    for k, shape in SCRATCH.items():
        t[k] = nc.dram_tensor(k, shape, F32).ap()
    t["out"] = nc.dram_tensor("out_T", (8, 128, 1024), F32, kind="ExternalOutput").ap()
    build(nc, t)
    r = _run(nc, [{"in_" + k: a for k, a in arrays.items()}], core_ids=[0])
    return np.ascontiguousarray(r.results[0]["out_T"].reshape(1024, 1024).T).reshape(1, 1024, 1024)
```

```python
import math
from contextlib import ExitStack
from itertools import chain

import numpy as np
import concourse.bass as bass
from concourse import mybir

F32 = mybir.dt.float32
F32R = mybir.dt.float32r
I32 = mybir.dt.int32
ALU = mybir.AluOpType
ACT = mybir.ActivationFunctionType
AX = mybir.AxisListType

P = 128
T = 1024
D = 1024
NK = 8
EPS = 1e-6
NG = 24
TWO_PI = 2.0 * math.pi
TURN = 6.283185
MAGIC = 12582912.0
PI_LO = 3.1415925


class Queue:

    def __init__(self, sem):
        self.sem = sem
        self.items = []
        self.n = 0
        self.seen = {}

    def wait(self, *marks):
        for sem, value in marks:
            if self.seen.get(sem.name, 0) < value:
                self.seen[sem.name] = value
                self.items.append((sem, value))

    def put(self, fn, *after):
        self.wait(*after)
        self.n += 1
        self.items.append((fn, self.sem, 1))
        return (self.sem, self.n)

    def quiet(self, fn, *after):
        self.wait(*after)
        self.items.append((fn, None, 0))

    def dma(self, fn, sem, total, *after):
        self.wait(*after)
        self.items.append((fn, sem, 16))
        return (sem, total)

    def emit(self, eng):
        for it in self.items:
            if len(it) == 2:
                eng.wait_ge(it[0], it[1])
            else:
                ins = it[0](eng)
                if it[1] is not None:
                    ins.then_inc(it[1], it[2])


def weave(*gens):
    live = [[g, n] for g, n in gens]
    while live:
        for entry in list(live):
            for _ in range(entry[1]):
                try:
                    next(entry[0])
                except StopIteration:
                    live.remove(entry)
                    break


PARAM_COLS = {}


def _cols(names):
    at = 0
    for name, n in names:
        PARAM_COLS[name] = (at, n)
        at += n
    return at


NPAR = _cols([
    ("c", 8), ("b_ada", 48), ("g_pre_mix", 8), ("g_post_mix", 8), ("g_pre_ffn", 8), ("g_post_ffn", 8),
    ("conv_w", 132), ("conv_b", 44), ("sink", 6), ("eps", 1),
    ("n1", 8), ("n2", 8), ("n3", 8), ("n4", 8),
    ("lcw", 8), ("lcb", 2), ("lba", 2), ("lbx", 2), ("lam", 2), ("pscale", 2), ("hlb", 2), ("hnorm", 2),
    ("scw", 6),
])

ORDER2 = [0, 20, 2, 28, 36, 44, 1, 21, 3, 29, 37, 45, 4, 22, 30, 5, 38, 46, 14, 23, 16, 31, 18, 39, 47, 15, 24, 17, 32, 19, 40, 48, 25, 33, 41, 49, 26, 34, 42, 50, 27, 35, 43, 51]
REC = None


def ffn_chunks(tiles):
    return [(c, min(4, tiles - c)) for c in range(0, tiles, 4)]


def build(nc, t):
    ctx = ExitStack()
    with ctx:
        names = [0]

        def sb(shape, dt=F32, c=ctx, side=None):
            names[0] += 1
            return c.enter_context(nc.sbuf_tensor(f"t{names[0]}", list(shape), dt, side=side))

        def sem(name):
            return ctx.enter_context(nc.semaphore(name))

        PSB = [ctx.enter_context(nc.psum_tensor(f"ps{i}", [P, 512], F32)) for i in range(4)]
        PSS = ctx.enter_context(nc.psum_tensor("pss", [P, 2, 512], F32))
        PSC = [ctx.enter_context(nc.psum_tensor(f"pc{i}", [P, 512], F32)) for i in range(2)]

        pe, act, dve, pool, sp = (Queue(sem(f"s_{n}")) for n in ("pe", "act", "dve", "pool", "sp"))
        engines = (pe, act, dve, pool)
        dma_total = {}
        dma_last = []
        phase = []

        def dma(q, key, out, in_, *after):
            if key not in dma_total:
                dma_total[key] = [sem("d_" + key), 0]
            e = dma_total[key]
            e[1] += 16
            m = q.dma(lambda g: g.dma_start(out, in_), e[0], e[1], *after, *phase)
            dma_last.append(m)
            return m

        def tt(q, out, a, b, op, *after):
            return q.put(lambda g: g.tensor_tensor(out, a, b, op), *after)

        def ts(q, out, a, s1, s2, op0, op1, *after):
            if op1 is None:
                return q.put(lambda g: g.tensor_scalar(out, a, s1, None, op0), *after)
            return q.put(lambda g: g.tensor_scalar(out, a, s1, s2, op0, op1), *after)

        def stt(out, a, s, b, op0, op1, *after):
            return dve.put(lambda g: g.scalar_tensor_tensor(out=out, in0=a, scalar=s, in1=b, op0=op0, op1=op1), *after)

        def av(out, a, func, *after, bias=None, scale=1.0, accum=None):
            kw = {"scale": scale}
            if bias is not None:
                kw["bias"] = bias
            if accum is not None:
                kw["accum_out"] = accum
            return act.put(lambda g: g.activation(out, a, func, **kw), *after)

        def memset(q, ap, v, *after):
            return q.put(lambda g: g.memset(ap, v), *after)

        def mm(out, lhsT, rhs, start, stop, last, *after, skip=False):
            kw = {"skip_group_check": True} if skip else {}
            f = lambda g: g.matmul(out, lhsT, rhs, start=start, stop=stop, **kw)
            if last:
                return pe.put(f, *after)
            pe.quiet(f, *after)

        def transpose(out, in_, *after):
            return pe.put(lambda g: g.transpose(out, in_, ident[:, :]), *after)

        def fence(pe_too=True):
            last = {s.name: (s, v) for s, v in sorted(dma_last, key=lambda m: m[1])}
            marks = [(q.sem, q.n) for q in engines] + list(last.values())
            del dma_last[:]
            phase[:] = marks
            for q in engines[0 if pe_too else 1:]:
                q.wait(*marks)
            return marks

        par = sb([P, NPAR])
        ident = sb([P, P])
        onesm = sb([P, P])
        mod = sb([P, 48])
        gmod = sb([P, 6, 8])
        r8 = sb([P, NG])
        halfpi = sb([P, 1])
        A = sb([P, 2, NK, T], F32R)
        wraw = sb([P, 3, 1024])
        whl = sb([P, 3, 2, 1024], F32R)

        def col(name, i=0, n=1):
            at = PARAM_COLS[name][0] + i
            return par[:, at:at + n]

        m_par = dma(act, "par", par[:, :], t["par"])
        m_ident = dma(act, "ident", ident[:, :], t["ident"])
        m_ones = memset(dve, onesm[:, :], 1.0)
        m_hpi = memset(dve, halfpi[:, :], math.pi / 2)

        stream = []
        for i in (0, 1, 2, 6, 7, 3, 4, 5, 8, 9):
            stream.append(("w_in", i))
        stream += [("w_out", i) for i in range(8)]

        def ffn_order(name, tiles, per):
            out = []
            up = [(name + "u", i) for i in range(tiles * per)]
            dn = 0
            chunks = ffn_chunks(tiles)
            for n, (c, k) in enumerate(chunks):
                hi = min(c + k + 2, tiles)
                lo = 0 if n == 0 else min(c + 2, tiles)
                out += up[lo * per:hi * per]
                for _ in range(8 * k // 8):
                    out.append((name + "d", dn))
                    dn += 1
            return out

        stream += ffn_order("f1", 22, 2)
        stream += [("w_in2", i) for i in range(6, 14)]
        stream += [("w_in2", i) for i in (ORDER2 or range(44))]
        stream += [("w_out2", i) for i in range(8)]
        stream += ffn_order("f2", 32, 1)
        state = {"load": 0, "split": 0, "use": 0}
        loaded, split_hi, split_lo, used = {}, {}, {}, {}

        def load_panel():
            n = state["load"]
            if n >= len(stream):
                return
            name, i = stream[n]
            s = n % 3
            after = [split_hi[n - 3], split_lo[n - 3]] if n >= 3 else []
            e = dma_total.setdefault(f"w{s}", [None, 0])
            if e[0] is None:
                e[0] = sem(f"d_w{s}")
            e[1] += 16
            loaded[n] = sp.dma(lambda g, s=s, a=t[name][i]: g.dma_start(wraw[:, s, :], a), e[0], e[1], *after)
            state["load"] += 1

        def split_panel():
            n = state["split"]
            if n >= len(stream):
                return
            s = n % 3
            after = [used[n - 3]] if n >= 3 else []
            split_hi[n] = av(whl[:, s, 0, :], wraw[:, s, :], ACT.Copy, loaded[n], *after)
            split_lo[n] = tt(pool, whl[:, s, 1, :], wraw[:, s, :], whl[:, s, 0, :].bitcast(F32), ALU.subtract,
                             loaded[n], split_hi[n])
            state["split"] += 1
            load_panel()

        def panel(name, i):
            n = state["use"]
            if REC is not None and name == "w_in2" and i not in range(6, 14):
                REC.append(i)
                stream[n] = (name, i)
            assert stream[n] == (name, i), (stream[n], name, i)
            while state["split"] <= n:
                split_panel()
            state["use"] += 1
            return n

        def panel_done(n, mark):
            used[n] = mark
            while state["split"] <= min(n + 2, len(stream) - 1) and (state["split"] < 3 or state["split"] - 3 in used):
                split_panel()

        def gemm3(out, n, wcols, acts, ks, half, ready, *after):
            pe.wait(split_hi[n], split_lo[n], *after)
            r = None
            for i, k in enumerate(ks):
                hi = whl[:, n % 3, 0, wcols[i]:wcols[i] + 128]
                lo = whl[:, n % 3, 1, wcols[i]:wcols[i] + 128]
                xh = acts[:, 0, k, half * 512:half * 512 + 512]
                xl = acts[:, 1, k, half * 512:half * 512 + 512]
                pe.wait(*ready(half, i))
                mm(out, hi, xh, i == 0, False, False)
                mm(out, hi, xl, False, False, False)
                r = mm(out, lo, xh, False, i == len(ks) - 1, i == len(ks) - 1)
            return r

        banks = {}

        def bank(i):
            return [banks[i]] if i in banks else []

        turn = [0]

        ring = [2]

        def next_bank():
            turn[0] += 1
            return turn[0] % ring[0]

        def gemm_half(name, n, half, evac, ready):
            b = next_bank()
            m = gemm3(PSB[b][:, :], n, [128 * k for k in range(8)], A, range(8), half, ready, *bank(b))
            banks[b] = evac(half, PSB[b], m)
            return m, banks[b]

        def gemm_seq(name, idxs, evac_of, ready, head=0):
            idxs = list(idxs)
            first = idxs[:head]
            if first:
                ns = [panel(name, i) for i in first]
                for i, n in zip(first, ns):
                    gemm_half(name, n, 0, evac_of(i), ready)
                    yield None
                for i, n in zip(first, ns):
                    m, e = gemm_half(name, n, 1, evac_of(i), ready)
                    panel_done(n, m)
                    yield (i, e)
            for i in idxs[head:]:
                n = panel(name, i)
                gemm_half(name, n, 0, evac_of(i), ready)
                yield None
                m, e = gemm_half(name, n, 1, evac_of(i), ready)
                panel_done(n, m)
                yield (i, e)

        def until_tile(seq):
            for r in seq:
                if r is not None:
                    return r

        ALL = slice(0, T)
        HALF = [slice(0, 512), slice(512, T)]

        def by_half(mA):
            return lambda half, k: [mA[half][k]]

        def split_act(dst, j, src, cols, flip, *after):
            h = av(dst[:, 0, j, cols], src, ACT.Copy, *after)
            q = pool if flip else dve
            return tt(q, dst[:, 1, j, cols], src, dst[:, 0, j, cols].bitcast(F32), ALU.subtract, h, *after)

        rcol = sb([P, 4])
        m_rcol = []

        def rows_of(src, ps, first, last, *after):
            r = None
            for b in range(4):
                r = mm(ps[:, b:b + 1], src[:, b * 128:b * 128 + 128], onesm[:, 0:1], first and b == 0, last, b == 3, m_ones,
                       *after, skip=True)
            return r

        def rstd_bank(ps, bk, n, diag, mark):
            m = av(rcol[:, :], ps[:, 0:4], ACT.Sqrt, mark, m_par, *m_rcol, bias=col("eps"), scale=1.0 / n)
            m = dve.put(lambda g: g.reciprocal(rcol[:, :], rcol[:, :]), m)
            m = tt(dve, diag[:, :].rearrange("p (b t) -> p b t", t=128), ident[:, :].unsqueeze(1).broadcast_to([P, 4, 128]),
                   rcol[:, :].unsqueeze(2).broadcast_to([P, 4, 128]), ALU.mult, m, m_ident)
            m_rcol[:] = [m]
            return mm(ps[:, :], onesm[:, :], diag[:, :], True, True, True, m, *bank(bk))

        class Norm:

            def __init__(self, ss, sq):
                self.ss, self.sq, self.n, self.done, self.marks = ss, sq, [0, 0], [[], []], [[], []]
                self.i = 0

            def add(self, src, half, *after):
                b = self.i % 2
                self.i += 1
                c = HALF[half]
                sq = self.sq[b]
                m = av(sq[:, :], src, ACT.Square, *after, *self.marks[b])
                if self.n[half] == 0:
                    m = dve.put(lambda g: g.tensor_copy(self.ss[:, c], sq[:, :]), m)
                else:
                    m = tt(dve, self.ss[:, c], self.ss[:, c], sq[:, :], ALU.add, m, *self.done[half])
                self.done[half] = [m]
                self.marks[b] = [m]
                self.n[half] += 1

        def norm_bufs(c):
            return Norm(sb([P, T], c=c), [sb([P, 512], c=c) for _ in range(2)])

        tmp_marks = [[], []]

        def apply_half(src, half, rb, bk, gain, shift, tmp, mark, ready, free=()):
            out = []
            tm = tmp_marks
            c = HALF[half]
            for j in range(8):
                b = j % 2
                m = stt(tmp[b][:, :], src(j)[:, c], gain(j), rb[:, :], ALU.mult, ALU.mult, mark, *ready(j), *tm[b])
                if j == 7:
                    banks[bk] = m
                if shift is not None:
                    m = av(tmp[b][:, :], tmp[b][:, :], ACT.Identity, m, bias=shift(j), scale=1.0)
                tm[b] = [split_act(A, j, tmp[b][:, :], c, j % 2 == 1, m, *free)]
                out.append(tm[b][0])
            return out

        ada_w = {}
        c0 = ExitStack()
        acc = sb([P, 1024], c=c0)
        ada_ring = [sb([P, 1024], c=c0) for _ in range(4)]
        ada_used = {}
        nada = [0]
        acc_free = []

        def ada(j):
            m = None
            for k in range(8):
                n = nada[0]
                nada[0] += 1
                b = n % 4
                after = [ada_used[n - 4]] if n >= 4 else []
                ld = dma(sp, f"ada{b}", ada_ring[b][:, :], t["w_ada"][j, k], *after)
                dma_last.pop()
                if k == 0:
                    m = ts(dve, acc[:, :], ada_ring[b][:, :], col("c", k), None, ALU.mult, None, ld, m_par, *acc_free)
                else:
                    m = stt(acc[:, :], ada_ring[b][:, :], col("c", k), acc[:, :], ALU.mult, ALU.add, ld, m)
                ada_used[n] = m
                if k % 2 == 1:
                    yield
            for i in range(8):
                r = mm(PSC[0][:, i:i + 1], acc[:, i * 128:i * 128 + 128], onesm[:, 0:1], True, True, i == 7, m, m_ones,
                       *bank(6))
            acc_free[:] = [r]
            r = tt(dve, mod[:, 8 * j:8 * j + 8], PSC[0][:, 0:8], col("b_ada", 8 * j, 8), ALU.add, r, m_par)
            banks[6] = r
            name = ["", "g_pre_mix", "g_post_mix", "", "g_pre_ffn", "g_post_ffn"][j]
            if j in (1, 4):
                r = ts(dve, gmod[:, j, :], mod[:, 8 * j:8 * j + 8], 1.0, None, ALU.add, None, r)
                r = tt(dve, gmod[:, j, :], gmod[:, j, :], col(name, 0, 8), ALU.mult, r)
            elif j in (2, 5):
                r = tt(dve, gmod[:, j, :], mod[:, 8 * j:8 * j + 8], col(name, 0, 8), ALU.mult, r)
            else:
                r = dve.put(lambda g: g.tensor_copy(gmod[:, j, :], mod[:, 8 * j:8 * j + 8]), r)
            ada_w[j] = r
            yield

        def gm(j):
            return lambda i: gmod[:, j, i:i + 1]

        X = sb([P, NK, T], c=c0)
        sq = [sb([P, 512], c=c0) for _ in range(2)]
        tmp = [sb([P, 512], c=c0) for _ in range(2)]
        diag = sb([P, 512], c=c0)
        mA = []

        def first_norm():
            mx = [dma(act, f"x{j}", X[:, j, :], t["xT"][j]) for j in range(8)]
            g0 = chain(ada(0), ada(1))
            next(g0)
            yield
            sq_free = [[], []]
            for j in range(8):
                for half in range(2):
                    m = av(sq[half][:, :], X[:, j, HALF[half]], ACT.Square, mx[j], *sq_free[half])
                    r = rows_of(sq[half][:, :], PSB[half], j == 0, j == 7, m)
                    sq_free[half] = [r]
                next(g0, None)
                yield
            for _ in g0:
                yield
            for _ in range(3):
                load_panel()
            for half in range(2):
                m_r = rstd_bank(PSB[half], half, D, diag, r)
                mA.append(apply_half(lambda j: X[:, j, :], half, PSB[half], half, gm(1), gm(0), tmp, m_r,
                                     lambda j: [mx[j], ada_w[0], ada_w[1]]))
                yield

        uscr, vscr, wscr, cscr, yscr, kscr = (t[n] for n in ("uscr", "vscr", "wscr", "cscr", "yscr", "kscr"))
        GB = 3
        m_r8, m_prep = [], {}

        def sincos(cos, sin, ph, *after):
            m = ts(dve, cos, ph, MAGIC, MAGIC, ALU.add, ALU.subtract, *after)
            m = tt(dve, ph, ph, cos, ALU.subtract, m)
            m1 = av(cos, ph, ACT.Abs, m)
            m2 = av(sin, ph, ACT.Sin, m, scale=TURN)
            return av(cos, cos, ACT.Sin, m1, m2, m_hpi, bias=halfpi[:, 0:1], scale=-TURN)

        def prep():
            with ExitStack() as cp:
                new = lambda *shape: sb(list(shape), c=cp, side="right")
                sp4 = new(P, 3, NG)
                Bt = new(P, 2, NG, 16)
                Ct = new(P, 2, NG, 16)
                ex = new(P, 31)
                msk = new(P, 15)
                kidx = new(P, 128)
                w = new(P, 12, NG)
                PW = new(P, 2, NG, 31)
                dI = new(16, NG, 16)
                R = new(P, 5424)
                ldp = [dma(sp, "sp4", sp4[:, :, :], t["ssm_p"]), dma(sp, "Bt", Bt[:, :, :, :], t["ssm_b"]),
                       dma(sp, "Ct", Ct[:, :, :, :], t["ssm_c"]), dma(sp, "ex", ex[:, :], t["exps"]),
                       dma(sp, "msk", msk[:, :], t["mask15"]), dma(sp, "kidx", kidx[:, :], t["kidx"]),
                       dma(sp, "dI", dI[:, :, :], t["dI"])]
                yield
                re, im, ld = sp4[:, 0, :], sp4[:, 1, :], sp4[:, 2, :]
                dt, ar, ai, n_, r_, mag, cs, sn, den, q1, q2, psi = (w[:, i, :] for i in range(12))
                m = av(dt, ld, ACT.Exp, *ldp)
                m1 = tt(dve, ar, re, dt, ALU.mult, m)
                m2 = tt(dve, ai, im, dt, ALU.mult, m)
                m = ts(dve, n_, ai, 1.0 / TWO_PI, MAGIC, ALU.mult, ALU.add, m2)
                m = ts(dve, n_, n_, MAGIC, None, ALU.subtract, None, m)
                r = ai
                for cc in (6.28125, 0.0019350051879882812, 3.01991605743e-07):
                    m = stt(r_, n_, -cc, r, ALU.mult, ALU.add, m)
                    r = r_
                mr = m
                yield
                mm_ = av(mag, ar, ACT.Exp, m1)
                m = ts(dve, q1, r_, PI_LO, -PI_LO, ALU.min, ALU.max, mr)
                ms = av(sn, q1, ACT.Sin, m)
                m = av(q2, q1, ACT.Abs, m)
                m = ts(dve, q2, q2, math.pi / 2, None, ALU.subtract, None, m)
                mc = av(cs, q2, ACT.Sin, m, scale=-1.0)
                mp = ts(dve, psi, r_, 1.0 / TWO_PI, None, ALU.mult, None, mr)
                yield
                bg = lambda a: a.unsqueeze(2).broadcast_to([P, NG, 31])
                be = ex[:, :].unsqueeze(1).broadcast_to([P, NG, 31])
                s31 = [R[:, i * 744:i * 744 + 744].rearrange("p (g e) -> p g e", e=31) for i in range(2)]
                m3 = tt(dve, s31[0], bg(ar), be, ALU.mult, m1, mc)
                mg = av(s31[0], s31[0], ACT.Exp, m3)
                m3 = tt(dve, s31[1], bg(psi), be, ALU.mult, mp)
                mP = sincos(PW[:, 0, :, :], PW[:, 1, :, :], s31[1], m3)
                m = tt(dve, cs, cs, mag, ALU.mult, mc, mm_)
                m = ts(dve, cs, cs, -1.0, None, ALU.add, None, m)
                m = tt(dve, sn, sn, mag, ALU.mult, ms, m)
                m = tt(dve, q1, re, re, ALU.mult, m)
                m = tt(dve, q2, im, im, ALU.mult, m)
                m = tt(dve, den, q1, q2, ALU.add, m)
                m = dve.put(lambda g: g.reciprocal(den, den), m)
                m = tt(dve, q1, cs, re, ALU.mult, m)
                m = tt(dve, q2, sn, im, ALU.mult, m)
                m = tt(dve, q1, q1, q2, ALU.add, m)
                m = tt(dve, n_, q1, den, ALU.mult, m)
                m = tt(dve, q1, sn, re, ALU.mult, m)
                m = tt(dve, q2, cs, im, ALU.mult, m)
                m = tt(dve, q1, q1, q2, ALU.subtract, m)
                m = tt(dve, q1, q1, den, ALU.mult, m)
                yield
                bc = lambda a: a.unsqueeze(2).broadcast_to([P, NG, 16])
                bb = [Bt[:, i, :, :] for i in range(2)]
                s16 = [R[:, 1488 + 384 * i:1872 + 384 * i].rearrange("p (g c) -> p g c", c=16) for i in range(3)]
                m = tt(dve, s16[0], bb[0], bc(n_), ALU.mult, m)
                m = tt(dve, s16[1], bb[1], bc(q1), ALU.mult, m)
                m = tt(dve, s16[0], s16[0], s16[1], ALU.subtract, m)
                m = tt(dve, s16[1], bb[0], bc(q1), ALU.mult, m)
                m = tt(dve, s16[2], bb[1], bc(n_), ALU.mult, m)
                m = tt(dve, bb[1], s16[1], s16[2], ALU.add, m)
                m = dve.put(lambda g: g.tensor_copy(bb[0], s16[0]), m)
                yield
                m = tt(dve, PW[:, 0, :, :], PW[:, 0, :, :], s31[0], ALU.mult, mP, mg)
                m = tt(dve, PW[:, 1, :, :], PW[:, 1, :, :], s31[0], ALU.mult, m)
                bm = msk[:, :].unsqueeze(1).broadcast_to([P, NG, 15])
                m = tt(dve, PW[:, 0, :, 0:15], PW[:, 0, :, 0:15], bm, ALU.mult, m)
                mP = tt(dve, PW[:, 1, :, 0:15], PW[:, 1, :, 0:15], bm, ALU.mult, m)
                m = ts(dve, q1, psi, 8.0, None, ALU.mult, None, mP)
                m = ts(dve, q2, q1, MAGIC, None, ALU.add, None, m)
                m = ts(dve, q2, q2, MAGIC, None, ALU.subtract, None, m)
                m8 = tt(dve, q1, q1, q2, ALU.subtract, m)
                m_r8.append(av(r8[:, :], ar, ACT.Exp, m1, scale=8.0))
                yield
                pend = []
                cs_free = [[], []]

                def flush():
                    for f in pend:
                        f()
                    del pend[:]

                for n in range(4):
                    b = n % 2
                    gs = slice(6 * n, 6 * n + 6)
                    at = 2304 * b
                    ph, co, si = (R[:, at + 768 * i:at + 768 * i + 768].rearrange("p (g k) -> p g k", k=128) for i in range(3))
                    m = tt(dve, ph, q1[:, gs].unsqueeze(2).broadcast_to([P, 6, 128]),
                           kidx[:, :].unsqueeze(1).broadcast_to([P, 6, 128]), ALU.mult, m8, mP, *cs_free[b])
                    m = sincos(co, si, ph, m)

                    def store(gs=gs, at=at, b=b, m=m):
                        d = dma(sp, f"cs{b}", cscr[:, :, gs, :],
                                R[:, at + 768:at + 2304].rearrange("p (i g k) -> p i g k", i=2, k=128), m)
                        cs_free[b] = [d]
                    pend.append(store)
                    yield
                    flush()
                m_prep["c"] = cs_free[0] + cs_free[1]

                tm = [R[:, 720 * i:720 * i + 720] for i in range(2)]
                bigs = {"v": (1440, 8), "w": (2208, 8), "k": (2976, 15)}
                Wt = R[:, 4416:5184]
                ko = R[:, 5184:5424]
                ldk = m_prep["c"]

                def cmul(src, name, off, gs, neg, *after):
                    at, nblk = bigs[name]
                    n = GB * nblk * 16
                    v4 = lambda a: a[:, 0:n].rearrange("p (g e c) -> p g e c", e=nblk, c=16)
                    t0, t1 = v4(tm[0]), v4(tm[1])
                    d_re, d_im = v4(R[:, at:at + n]), v4(R[:, at + n:at + 2 * n])
                    pr, pi = (PW[:, i, gs, off:off + nblk].unsqueeze(3).broadcast_to([P, GB, nblk, 16]) for i in range(2))
                    sr, si = (src[:, i, gs, :].unsqueeze(2).broadcast_to([P, GB, nblk, 16]) for i in range(2))
                    a = tt(dve, t0, sr, pr, ALU.mult, *after)
                    b = tt(pool, t1, si, pi, ALU.mult, *after)
                    a = tt(dve, d_re, t0, t1, ALU.subtract, a, b)
                    b = tt(dve, t0, sr, pi, ALU.mult, a)
                    c = tt(pool, t1, si, pr, ALU.mult, a)
                    if neg:
                        return stt(d_im, t0, -1.0, t1, ALU.mult, ALU.subtract, b, c)
                    return tt(dve, d_im, t0, t1, ALU.add, b, c)

                free = {"v": [], "wt": [], "k": []}
                m = mP
                w_pe = []
                for b0 in range(0, NG, GB):
                    gs = slice(b0, b0 + GB)
                    m = cmul(Ct, "v", 15, gs, True, m, *ldk, *free["v"])

                    def st_v(gs=gs, m=m):
                        free["v"] = [dma(sp, "vs", vscr[:, :, gs, :],
                                         R[:, 1440:2208].rearrange("p (i g n) -> p i g n", i=2, n=128), m)]
                    pend.append(st_v)
                    yield
                    mw = m = cmul(Bt, "w", 23, gs, False, m, *w_pe)
                    yield
                    flush()
                    m = cmul(Ct, "k", 0, gs, True, m, *free["k"])
                    for i in range(2):
                        for g in range(GB):
                            r = transpose(PSC[i][:, g * 128:g * 128 + 128],
                                          R[:, 2208 + i * 384 + g * 128:2336 + i * 384 + g * 128], mw, m_ident, *bank(6 + i))
                        banks[6 + i] = av(Wt[:, i * 384:i * 384 + 384], PSC[i][:, 0:384], ACT.Copy, r, *free["wt"], *ldk)
                    w_pe = [r]

                    def st_w(gs=gs, m=banks[7]):
                        free["wt"] = [dma(sp, "ws", wscr[:, :, gs, :], Wt.rearrange("p (i g n) -> p i g n", i=2, n=128), m)]
                    pend.append(st_w)
                    yield
                    flush()
                    for g in range(GB):
                        o = PSC[1][32 * g:32 * g + 16, 0:240]
                        for i in range(2):
                            at = 2976 + 720 * i + 240 * g
                            r = mm(o, Bt[:, i, b0 + g, :], R[:, at:at + 240], i == 0, i == 1, i == 1, m, *bank(7))
                    k_pe = [r]
                    for g in range(GB):
                        r = av(ko[32 * g:32 * g + 16, :], PSC[1][32 * g:32 * g + 16, 0:240], ACT.Copy, r, *free.get("ko", []), *ldk)
                    banks[7] = r
                    free["k"] = k_pe

                    def st_k(b0=b0, m=r):
                        for g in range(GB):
                            d = dma(sp, "ks", kscr[b0 + g], ko[32 * g:32 * g + 16, :], m)
                        free["ko"] = [d]
                    pend.append(st_k)
                    yield
                flush()
                kb = tm[0][0:16, 0:NG * 16].rearrange("p (g n) -> p g n", n=16)
                l1 = dma(sp, "kl", kb, kscr[:, :, 112:128].rearrange("g c n -> c g n"), *free["ko"], m)
                m = tt(dve, kb, kb, dI[:, :, :], ALU.add, l1, *ldp)
                yield
                m_k2 = dma(sp, "kl2", kscr[:, :, 112:128].rearrange("g c n -> c g n"), kb, m)
                m_prep.update(k=[m_k2], v=free["v"], w=free["wt"])
                prep_done.extend([m, m_k2, w_pe[0], k_pe[0], banks[7], *free["v"], *free["wt"]])

        prep_done = []
        tables = prep()
        norm0 = first_norm()
        next(tables)
        for _ in norm0:
            for _ in range(3):
                next(tables, None)
        c0.close()
        fence(False)

        pu = ExitStack()
        uT = sb([P, 3, 8, 128], c=pu)
        fT = sb([P, 2, T], c=pu)
        qT = sb([P, 3, T], c=pu)
        kT = sb([P, T], c=pu)
        vT = sb([P, T], c=pu)
        m_z, m_us, m_y = {}, [], {}

        def w_in_all():
            def evac_of(i):
                def evac(half, ps, m):
                    if i < 3:
                        o = uT[:, i, :, half * 64:half * 64 + 64]
                        r = act.put(lambda g: g.activation(o, ps[:, :].rearrange("p (k t) -> p t k", t=8), ACT.Copy), m)
                    elif i in (6, 7):
                        r = av((kT if i == 6 else vT)[:, HALF[half]], ps[:, :], ACT.Copy, m)
                    elif i < 6:
                        r = av(qT[:, i - 3, HALF[half]], ps[:, :], ACT.Copy, m, scale=0.125)
                    else:
                        r = av(fT[:, i - 8, HALF[half]], ps[:, :], ACT.Copy, m)
                    m_z[i] = r
                    return r
                return evac
            for r in gemm_seq("w_in", (0, 1, 2, 6, 7, 3, 4, 5, 8, 9), evac_of, by_half(mA), 3):
                if r is not None and r[0] < 3:
                    i = r[0]
                    m_us.append(dma(sp, f"us{i}", uscr[i], uT[:, i, :, :].rearrange("p t k -> p (t k)"), r[1]))
                if r is not None and r[0] == 9:
                    m_z["done"] = used[state["use"] - 1]
                yield

        NB = 4

        def ssm():
            c2 = ExitStack()
            new = lambda *shape: sb(list(shape), c=c2, side="right")
            U = new(P, NG, 128)
            WV = new(P, 4, NB, 128)
            Wb, Vb = WV[:, 0:2, :, :], WV[:, 2:4, :, :]
            Tb = new(P, NB, 128)
            Cb = new(P, 2, NB, 128)
            Hb = new(P, 2, NB, 128)
            Mt = new(P, 2, NB, 128)
            Rb = new(P, NB, 128)
            nz = new(P, 128)
            xt = new(P, NB, 128)
            glf = WV[:, :, :, :].rearrange("p a b c -> p (a b c)")[:, 0:1152]
            glw = glf.rearrange("p (a b c) -> p a b c", a=3, b=3)
            m_nz = dma(sp, "nz", nz[:, :], t["nz"], *prep_done)
            for s in range(8):
                src = bass.AP(tensor=uscr.tensor, offset=128 * s, ap=[[1024, 16], [16 * 1024, NG], [1, 128]])
                ld_u = dma(sp, "ul", U[16 * s:16 * s + 16, :, :], src, *m_us, *prep_done)
            free = {"w": prep_done, "t": prep_done, "v": prep_done, "c": prep_done, "h": prep_done, "x": prep_done}
            lw, lt, lv, lc = {}, {}, {}, {}

            def load_w(b0):
                if b0 < NG:
                    lw[b0] = dma(sp, "lw", Wb, wscr[:, :, b0:b0 + NB, :], *m_prep["w"], *free["w"])

            def load_c(b0):
                if b0 < NG:
                    lc[b0] = dma(sp, "lc", Cb[:, :, :, :], cscr[:, :, b0:b0 + NB, :], *m_prep["c"], *free["c"])

            def load_tv(b0):
                if b0 < NG:
                    for s in range(8):
                        src = bass.AP(tensor=kscr.tensor, offset=b0 * 3840 + (7 - s) * 16,
                                      ap=[[240, 16], [3840, NB], [1, 128]])
                        lt[b0] = dma(sp, "lt", Tb[16 * s:16 * s + 16, :, :], src, *m_prep["k"], *free["t"])
                    lv[b0] = dma(sp, "lv", Vb, vscr[:, :, b0:b0 + NB, :], *m_prep["v"], *free["v"])

            load_w(0)
            load_c(0)
            load_tv(0)
            yield
            m_ys = None
            for b0 in range(0, NG, NB):
                gs = slice(b0, b0 + NB)
                for i in range(2):
                    for g in range(NB):
                        r = mm(PSC[i][:, g * 128:g * 128 + 128], Wb[:, i, g, :], U[:, b0 + g, :], True, True,
                               g == NB - 1, lw[b0], ld_u, *bank(6 + i))
                    m_x = r
                free["w"] = [m_x]
                load_w(b0 + NB)
                mrb = tt(dve, Rb[:, :, :], nz[:, :].unsqueeze(1).broadcast_to([P, NB, 128]),
                         r8[:, gs].unsqueeze(2).broadcast_to([P, NB, 128]), ALU.mult, m_nz, *m_r8, *free["x"])
                yield
                x = [PSC[i][:, :].rearrange("p (g k) -> p g k", k=128) for i in range(2)]
                cs, sn = Cb[:, 0, :, :], Cb[:, 1, :, :]
                h0, h1 = Hb[:, 0, :, :], Hb[:, 1, :, :]
                t0, t1 = Mt[:, 0, :, :], Mt[:, 1, :, :]
                a = tt(dve, h0, x[0], cs, ALU.mult, m_x, lc[b0], *free["h"])
                b = tt(dve, t1, x[0], sn, ALU.mult, a)
                banks[6] = b
                c = tt(dve, t0, x[1], sn, ALU.mult, b)
                d = tt(dve, h1, x[1], cs, ALU.mult, c)
                banks[7] = d
                a = tt(pool, h0, h0, t0, ALU.add, c)
                d = tt(dve, h1, h1, t1, ALU.subtract, d)
                yield
                for i in (1, 0):
                    for lo, rev in ((0, 1), (64, -1)):
                        pr = slice(lo, lo + 64)
                        src = Hb[pr, i, :, :].rearrange("p g k -> p (g k)")[:, ::rev]
                        dst = Mt[pr, i, :, :].rearrange("p g k -> p (g k)")[:, ::rev]
                        rr = Rb[pr, :, :].rearrange("p g k -> p (g k)")[:, ::rev]
                        sc_m = dve.put(lambda g_, src=src, dst=dst, rr=rr: g_.tensor_tensor_scan(
                            dst, rr, src, 0.0, ALU.mult, ALU.add), d, mrb, *([a] if i == 0 else []))
                z = memset(dve, Hb[0:64, :, :, 0:1], 0.0, sc_m)
                z2 = memset(dve, Hb[64:128, :, :, 127:128], 0.0, sc_m)
                yield
                for i in range(2):
                    for lo in (0, 64):
                        pr = slice(lo, lo + 64)
                        so = slice(0, 127) if lo == 0 else slice(1, 128)
                        do = slice(1, 128) if lo == 0 else slice(0, 127)
                        c_a = Cb[pr, 0 if i == 0 else 1, :, so]
                        c_b = Cb[pr, 1 if i == 0 else 0, :, so]
                        o = Hb[pr, i, :, do]
                        tmpa = xt[pr, :, 0:127]
                        ma = tt(dve, o, Mt[pr, 0, :, so], c_a, ALU.mult, sc_m, z, z2)
                        mb = tt(dve if lo else pool, tmpa, Mt[pr, 1, :, so], c_b, ALU.mult, sc_m, *free["x"])
                        mh = tt(dve, o, o, tmpa, ALU.subtract if i == 0 else ALU.add, ma, mb)
                        free["x"] = [mh]
                free["c"] = [mh]
                load_c(b0 + NB)
                yield
                for g in range(NB):
                    o = PSC[0][:, g * 128:g * 128 + 128]
                    mm(o, Tb[:, g, :], U[:, b0 + g, :], True, False, False, lt[b0], *bank(6))
                    mm(o, Vb[:, 0, g, :], Hb[:, 0, g, :], False, False, False, lv[b0], mh)
                    r = mm(o, Vb[:, 1, g, :], Hb[:, 1, g, :], False, True, g == NB - 1)
                free["t"] = free["v"] = free["h"] = [r]
                load_tv(b0 + NB)
                r = av(U[:, gs, :], PSC[0][:, :].rearrange("p (g k) -> p g k", k=128), ACT.Copy, r)
                banks[6] = r
                for s in range(8):
                    dst = bass.AP(tensor=yscr.tensor, offset=b0 * 16384 + 128 * s,
                                  ap=[[1024, 16], [16 * 1024, NB], [1, 128]])
                    m_ys = dma(act if s % 2 else sp, "ysa" if s % 2 else "ysb", dst, U[16 * s:16 * s + 16, gs, :], r)
                    ysm[s % 2] = m_ys
                yield
            m_glw = dma(sp, "glw", glf, t["w_glu"].rearrange("p a b c -> p (a b c)"), *free["v"], *free["w"])
            for i in range(3):
                ly = dma(sp, "yl", uT[:, i, :, :].rearrange("p t k -> p (t k)"), yscr[i], *ysm, *m_us)
            yf = uT[:, :, :, :].rearrange("p i t k -> p i (t k)")
            ge = [av(yf[:, i, :], yf[:, i, :], ACT.Gelu_apprx_tanh, ly) for i in range(3)]
            yield
            gp = [ysm, ysm]
            sg = U[:, 0:16, :].rearrange("p (a g) k -> p a (g k)", a=4)
            for j in range(3):
                for half in range(2):
                    c = slice(half * 512, half * 512 + 512)
                    for i in range(3):
                        r = mm(PSC[half][:, :], glw[:, i, j, :], yf[:, i, c], i == 0, i == 2, i == 2, m_glw, *ge,
                               *bank(6 + half))
                    b = half
                    m = av(sg[:, b, :], PSC[half][:, :], ACT.Sigmoid, r, *gp[b])
                    banks[6 + half] = m
                    m = tt(dve, sg[:, b, :], sg[:, b, :], yf[:, j, c], ALU.mult, m)
                    oh, ol = (A[:, e, j, :].rearrange("p (k t) -> p t k", t=8)[:, 4 * half:4 * half + 4, :] for e in range(2))
                    sv = sg[:, b, :].rearrange("p (t k) -> p t k", k=128)
                    h = av(oh, sv, ACT.Copy, m, m_z["done"])
                    m = tt(dve, ol, sv, oh.bitcast(F32), ALU.subtract, h)
                    gp[b] = [m]
                    m_y[("s", j, half)] = m
                    yield
            c2.close()

        ysm = [None, None]

        def attention():
            with ExitStack() as ca:
                dist = sb([P, 384], c=ca)
                m_dist = dma(sp, "dist", dist[:, :], t["dist"])
                vrow = sb([P, 8, 128], c=ca)
                scb = [sb([P, 2, 384], c=ca) for _ in range(3)]
                pts = [sb([P, 384], c=ca) for _ in range(2)]
                small = sb([P, 3, 16], c=ca)
                for b in range(2):
                    for n in range(4):
                        r = transpose(PSB[2 + b][:, n * 128:n * 128 + 128],
                                      vT[:, (4 * b + n) * 128:(4 * b + n) * 128 + 128], m_z[7], m_ident, *bank(2 + b))
                    r = av(vrow[:, 4 * b:4 * b + 4, :], PSB[2 + b][:, :].rearrange("p (n d) -> p n d", d=128), ACT.Copy, r)
                    banks[2 + b] = r
                m_v = r
                units = [(i, n) for i in range(3) for n in range(8)]
                span = lambda n: (128 if n == 0 else 0, 256 if n == 7 else 384)
                sc_free = [[], [], []]
                pt_used = [[], []]
                pt_n = [0]
                mst = {}

                def stage_a(u):
                    i, n = units[u]
                    b = u % 3
                    lo, hi = span(n)
                    kc = slice((n - 1) * 128 + lo, (n - 1) * 128 + hi)
                    w = hi - lo
                    sc, sm = scb[b], small[:, b, :]
                    for g in range(2):
                        pr = slice(64 * g, 64 * g + 64)
                        r = mm(PSS[:, g, 0:w], qT[pr, i, n * 128:n * 128 + 128], kT[pr, kc], True, True, True,
                               m_z[6], m_z[3 + i], *bank(4 + g))
                        slope = float(np.exp2(np.float32(-8.0) * np.float32(3 * g + i + 1) / np.float32(6)))
                        m = stt(sc[:, g, 0:w], dist[:, lo:hi], slope, PSS[:, g, 0:w], ALU.mult, ALU.add, r, m_dist, *sc_free[b])
                        banks[4 + g] = m
                    m = dve.put(lambda g_: g_.tensor_reduce(sm[:, 0:2], sc[:, :, 0:w], AX.X, ALU.max), m)
                    m = tt(dve, sm[:, 0:2], sm[:, 0:2], col("sink", 2 * i, 2), ALU.max, m)
                    m1 = ts(dve, sm[:, 2:4], sm[:, 0:2], -1.0, None, ALU.mult, None, m)
                    m2 = tt(dve, sm[:, 4:6], col("sink", 2 * i, 2), sm[:, 0:2], ALU.subtract, m)
                    mst[u] = m2

                def stage_b(u):
                    i, n = units[u]
                    b = u % 3
                    lo, hi = span(n)
                    w = hi - lo
                    sc, sm = scb[b], small[:, b, :]
                    for g in range(2):
                        e = av(sc[:, g, 0:w], sc[:, g, 0:w], ACT.Exp, mst[u], bias=sm[:, 2 + g:3 + g], accum=sm[:, 6 + g:7 + g])
                    e = av(sm[:, 8:10], sm[:, 4:6], ACT.Exp, mst[u])
                    m = tt(dve, sm[:, 8:10], sm[:, 8:10], sm[:, 6:8], ALU.add, e)
                    m = dve.put(lambda g_: g_.reciprocal(sm[:, 10:12], sm[:, 8:10]), m)
                    for g in range(2):
                        mn = ts(dve, sc[:, g, 0:w], sc[:, g, 0:w], sm[:, 10 + g:11 + g], None, ALU.mult, None, m, e)
                    mst[u] = mn

                def stage_c(u):
                    i, n = units[u]
                    b = u % 3
                    lo, hi = span(n)
                    w = hi - lo
                    nb = w // 128
                    sc = scb[b]
                    for g in range(2):
                        for s in range(nb):
                            r = transpose(PSB[2][:, s * 128:s * 128 + 128], sc[:, g, s * 128:s * 128 + 128], mst[u], *bank(2))
                        pb = pt_n[0] % 2
                        pt_n[0] += 1
                        r = av(pts[pb][:, 0:w], PSB[2][:, 0:w], ACT.Copy, r, *pt_used[pb])
                        banks[2] = r
                        o = PSB[3][64 * g:64 * g + 64, (n % 4) * 128:(n % 4) * 128 + 128]
                        for s in range(nb):
                            blk = (n - 1) + lo // 128 + s
                            q = mm(o, vrow[:, blk, 64 * g:64 * g + 64], pts[pb][:, s * 128:s * 128 + 128], s == 0,
                                   s == nb - 1, s == nb - 1, r, m_v, *bank(3))
                        pt_used[pb] = [q]
                        if g == 0:
                            yield
                    sc_free[b] = [q]
                    if n % 4 == 3:
                        c = slice((n - 3) * 128, (n + 1) * 128)
                        h = av(A[:, 0, 5 + i, c], PSB[3][:, :], ACT.Copy, q, m_z["done"])
                        l = tt(dve, A[:, 1, 5 + i, c], PSB[3][:, :], A[:, 0, 5 + i, c].bitcast(F32), ALU.subtract, h)
                        banks[3] = l
                        m_y[("a", i, n // 4)] = l
                        mst["out"] = l
                    mst["last"] = q

                nu = len(units)
                for u in range(nu + 2):
                    if u < nu:
                        stage_a(u)
                        yield
                    if 0 <= u - 1 < nu:
                        stage_b(u - 1)
                        yield
                    if 0 <= u - 2 < nu:
                        yield from stage_c(u - 2)
                        yield
                att_done.extend([mst["last"], mst["out"]])

        att_done = []

        def fourier():
            with ExitStack() as cf:
                FA = sb([P, 8, 2, 256], c=cf)
                WC = sb([P, 2, 2, 128], c=cf)
                alt = sb([P, 1], c=cf)
                c64 = kT[:, 0:256].rearrange("p (i d) -> p i d", i=2)
                wf = kT[:, 256:512].rearrange("p (i d) -> p i d", i=2)
                dft = [qT[:, i, :] for i in range(3)] + [vT[:, :]]
                l0 = dma(sp, "alt", alt[:, :], t["alt"], *att_done)
                l1 = dma(sp, "c64", c64, t["c64"], *att_done)
                l2 = dma(sp, "wf", wf, t["w_fft"], *att_done)
                used_d, ld = {}, {}

                def load_d(n):
                    if n < 8:
                        ld[n] = dma(sp, f"dft{n % 4}", dft[n % 4], t["dft"][n], *att_done, *used_d.get(n - 4, []))
                for n in range(4):
                    load_d(n)
                for pr in range(2):
                    for i in range(2):
                        r = mm(PSB[0][:, (pr * 2 + i) * 128:(pr * 2 + i) * 128 + 128], c64[:, i, :], wf[:, pr, :], True, True,
                               True, l1, l2, *bank(0))
                m_wc = dve.put(lambda g: g.tensor_copy(WC[:, :, :, :].rearrange("p a b c -> p (a b c)"), PSB[0][:, :]), r,
                               *att_done)
                banks[0] = m_wc
                yield
                fa = []
                for tp in range(8):
                    b = tp % 2
                    for pr in range(2):
                        r = mm(PSB[b][:, pr * 256:pr * 256 + 256], fT[:, pr, tp * 128:tp * 128 + 128],
                               WC[:, pr, :, :].rearrange("p a b -> p (a b)"), True, True, True, m_wc, m_z[9], m_z[8], *bank(b))
                    o = FA[:, tp, :, :].rearrange("p a b -> p (a b)")
                    if tp % 2:
                        r = av(o, PSB[1][:, :], ACT.Copy, r, *att_done)
                    else:
                        r = dve.put(lambda g, o=o: g.tensor_copy(o, PSB[0][:, :]), r, *att_done)
                    banks[b] = r
                    fa.append(r)
                    yield
                for tp in range(8):
                    for i in range(2):
                        for pr in range(2):
                            b = 2 * i + pr
                            r = mm(PSB[b][:, :], FA[:, tp, pr, i * 128:i * 128 + 128], dft[tp % 4][:, i * 512:i * 512 + 512],
                                   tp == 0, tp == 7, True, ld[tp], fa[tp], fa[7], *bank(b))
                    used_d[tp] = [r]
                    load_d(tp + 4)
                    yield
                m_pq = r
                for pr in range(2):
                    for tp in range(8):
                        r = mm(PSS[:, 0, pr:pr + 1], FA[:, tp, pr, 0:128], alt[:, :], tp == 0, tp == 7, tp == 7, l0,
                               *bank(4))
                m_mid = r
                yield
                lo_, hi_ = slice(0, 512), slice(1023, 512, -1)
                for pr in range(2):
                    Pb, Qb = PSB[pr], PSB[2 + pr]
                    st = FA[:, 2 * pr:2 * pr + 2, :, :].rearrange("p a b c -> p (a b c)")
                    a = dve.put(lambda g, Pb=Pb, st=st: g.tensor_copy(st[:, 0:512], Pb[:, :]), m_pq, m_mid)
                    b1 = tt(dve, st[:, 513:1024], st[:, 1:512], Qb[:, 1:512], ALU.subtract, a)
                    b2 = tt(dve, st[:, 0:512], st[:, 0:512], Qb[:, :], ALU.add, b1)
                    banks[pr], banks[2 + pr] = a, b2
                    b3 = dve.put(lambda g, pr=pr, st=st: g.tensor_copy(st[:, 512:513], PSS[:, 0, pr:pr + 1]), m_mid, b2)
                    banks[4] = b3
                    for half, src, dst in ((0, st[:, 0:512], HALF[0]), (1, st[:, 512:513], slice(512, 513)),
                                           (1, st[:, 513:1024], slice(1023, 512, -1))):
                        h = av(A[:, 0, 3 + pr, dst], src, ACT.Copy, b3, m_z["done"])
                        l = tt(dve, A[:, 1, 3 + pr, dst], src, A[:, 0, 3 + pr, dst].bitcast(F32), ALU.subtract, h)
                        m_y[("f", pr, dst.start)] = l
                    yield

        def after_projections():
            while 8 not in m_z:
                yield
            yield from attention()
            yield from fourier()

        def state_space():
            yield from tables
            while len(m_us) < 3:
                yield
            yield from ssm()

        weave((w_in_all(), 1), (state_space(), 1), (after_projections(), 2))
        pu.close()
        fence(False)

        def ada_rest():
            for j in (2, 4, 3, 5):
                yield from ada(j)

        def out_proj(name, Y, nrm, ready, step=None):
            def evac_of(j):
                def evac(half, ps, m):
                    o = Y[:, j, HALF[half]]
                    r = av(o, ps[:, :], ACT.Copy, m)
                    nrm.add(o, half, r)
                    return r
                return evac
            for _ in gemm_seq(name, range(8), evac_of, ready):
                if step is not None:
                    next(step, None)

        def residual(Y, nrm, X, mx, xdst, post, pre, shift, c, tmp, final=False, key="", diag=None):
            if diag is None:
                diag = sb([P, 512], c=c)
            sqr = nrm.sq
            sq_free = [nrm.marks[0], nrm.marks[1]]
            mA = []
            st = []
            for half in range(2):
                cs = HALF[half]
                b1, b2 = 6 + half, 4 + half
                p1, p2 = PSC[half], PSS[:, half, :]
                m = rows_of(nrm.ss[:, cs], p1, True, True, *nrm.done[half], *bank(b1))
                m_r = rstd_bank(p1, b1, D, diag, m)
                outm = []
                for j in range(8):
                    m = stt(Y[:, j, cs], Y[:, j, cs], post(j), p1[:, :], ALU.mult, ALU.mult, m_r)
                    if j == 7:
                        banks[b1] = m
                    m = tt(dve, Y[:, j, cs], Y[:, j, cs], X(j)[:, cs], ALU.add, m, mx[j])
                    outm.append(m)
                    if final:
                        st.append(dma(sp, f"{key}s{half}{j % 4}", xdst[j, :, cs], Y[:, j, cs], m))
                    else:
                        b = j % 2
                        m = av(sqr[b][:, :], Y[:, j, cs], ACT.Square, m, *sq_free[b])
                        r = rows_of(sqr[b][:, :], p2, j == 0, j == 7, m, *bank(b2))
                        sq_free[b] = [r]
                if final:
                    continue
                m_r = rstd_bank(p2, b2, D, diag, r)
                mA.append(apply_half(lambda j: Y[:, j, :], half, p2, b2, pre, shift, tmp, m_r, lambda j: [outm[j]]))
                if half == 1:
                    for j in range(8):
                        st.append(dma(sp, f"{key}s{j % 4}", xdst[j], Y[:, j, :], outm[j]))
            return mA, st

        ring[0] = 4
        pc = ExitStack()
        acc = sb([P, 1024], c=pc, side="right")
        ada_ring = [sb([P, 1024], c=pc, side="right") for _ in range(4)]
        with ExitStack() as c3:
            Y = sb([P, NK, T], c=c3)
            X = sb([P, NK, T], c=c3)
            nrm = norm_bufs(c3)
            tmp = [sb([P, 512], c=c3) for _ in range(2)]
            mx = [dma(act, f"xa{j}", X[:, j, :], t["xT"][j]) for j in range(8)]
            ys = list(m_y.values())
            rest_ada = ada_rest()
            out_proj("w_out", Y, nrm, lambda half, k: ys, rest_ada)
            for _ in rest_ada:
                pass
            mA, _ = residual(Y, nrm, lambda j: X[:, j, :], mx, t["xs"], gm(2), gm(4), gm(3), c3, tmp, key="ra")
        pc.close()
        fence(False)

        def ffn(name, tiles, seq_of, make_hid, Y, nrm, H, xsrc, key):
            hid_m, hid_free = {}, {}
            chunks = ffn_chunks(tiles)
            dn = [0]
            y_m = {}
            mx = []

            def down(ci):
                c0, k = chunks[ci]
                per_panel = 8 // k
                fin = ci == len(chunks) - 1
                ready = lambda half, i: [hid_m[c0 + i]]
                for pn in range(8 // per_panel):
                    n = panel(name + "d", dn[0])
                    dn[0] += 1
                    for mi in range(per_panel):
                        j = pn * per_panel + mi
                        for half in range(2):
                            b = next_bank()
                            r = gemm3(PSB[b][:, :], n, [(mi * k + kk) * 128 for kk in range(k)], H,
                                      [(c0 + kk) % 6 for kk in range(k)], half, ready, *bank(b))
                            o = Y[:, j, HALF[half]]
                            if ci == 0:
                                banks[b] = dve.put(lambda g, o=o, b=b: g.tensor_copy(o, PSB[b][:, :]), r)
                            else:
                                banks[b] = tt(dve, o, o, PSB[b][:, :], ALU.add, r, y_m[(j, half)])
                            y_m[(j, half)] = banks[b]
                            if fin:
                                nrm.add(o, half, banks[b])
                    panel_done(n, r)
                for kk in range(k):
                    hid_free[c0 + kk] = [r]

            seq = seq_of()
            for n, (c0, k) in enumerate(chunks):
                lo = 0 if n == 0 else min(c0 + 2, tiles)
                for i in range(lo, min(c0 + k + 2, tiles)):
                    hid_m[i] = make_hid(i, seq, H, hid_free.get(i - 6, []))
                    if i == tiles - 1:
                        done = used[state["use"] - 1]
                        for j in range(8):
                            mx.append(dma(sp, f"{key}x{j}", A[:, 0, j, :].bitcast(F32), xsrc[j], done))
                down(n)
            return mx

        XA = lambda j: A[:, 0, j, :].bitcast(F32)
        with ExitStack() as c4:
            Y = sb([P, NK, T], c=c4)
            c5 = ExitStack()
            H = sb([P, 2, 6, T], F32R, c=c5)
            pad = [sb([P, T + 2], c=c5) for _ in range(3)]
            cv = sb([P, T], c=c5)
            nrm = norm_bufs(c5)
            for p in pad:
                memset(dve, p[:, 0:T + 2:T + 1], 0.0)
            pad_m = [(dve.sem, dve.n)]
            pad_free = [[], [], []]
            cv_free = []

            def evac_f1(i):
                def evac(half, ps, m):
                    return av(pad[i % 3][:, 1 + half * 512:513 + half * 512], ps[:, :], ACT.Copy, m, *pad_free[i % 3])
                return evac

            def hid1(i, seq, H, free):
                def conv(out, pd, e, *after):
                    ch = i + 22 * e
                    w = lambda j: col("conv_w", 44 * j + ch)
                    m = ts(dve, out, pd[:, 0:T], w(0), col("conv_b", ch), ALU.mult, ALU.add, *pad_m, *after)
                    m = stt(out, pd[:, 1:T + 1], w(1), out, ALU.mult, ALU.add, m)
                    return stt(out, pd[:, 2:T + 2], w(2), out, ALU.mult, ALU.add, m)
                a, b = (2 * i) % 3, (2 * i + 1) % 3
                _, last = until_tile(seq)
                mg = conv(cv[:, :], pad[a], 0, last, *cv_free)
                mg2 = av(cv[:, :], cv[:, :], ACT.Gelu_apprx_tanh, mg)
                _, last = until_tile(seq)
                v = pad[a][:, 1:T + 1]
                m = conv(v, pad[b], 1, last, mg)
                pad_free[b] = [m]
                m = tt(dve, v, v, cv[:, :], ALU.mult, m, mg2)
                cv_free[:] = [m]
                m = split_act(H, i % 6, v, ALL, True, m, *free)
                pad_free[a] = [m]
                return m

            mxa = ffn("f1", 22, lambda: gemm_seq("f1u", range(44), evac_f1, by_half(mA), 3), hid1, Y, nrm, H, t["xs"], "f1")
            tmp = [cv[:, 0:512], cv[:, 512:T]]
            cx = ExitStack()
            mA, st1 = residual(Y, nrm, XA, mxa, t["xs2"], gm(5), lambda j: col("n1", j), None, cx, tmp, key="rb",
                              diag=pad[0][:, 0:512])
            cx.close()
            c5.close()
        fence(False)

        pb2 = ExitStack()
        c6 = ExitStack()
        bd = sb([P, 8, 128], c=c6)
        lbd = dma(sp, "bd", bd[:, :, :], t["bd"])
        cc = sb([P, 64], c=c6)

        def stor(n):
            return sb([P, n, T], c=c6)

        hz = stor(8)
        z2 = stor(0 + 4)
        m_h = {}

        def proj(idx, dsts, marks, free=(), head=0):
            at = dict(zip(idx, dsts))

            def evac_of(i):
                def evac(half, ps, m):
                    r = av(at[i][:, HALF[half]], ps[:, :], ACT.Copy, m, *free)
                    marks[i] = r
                    return r
                return evac
            yield from gemm_seq("w_in2", idx, evac_of, by_half(mA), head)

        ring[0] = 2
        fill = []
        sgt = [sb([P, T], c=c6) for _ in range(2)]
        sg_free = [[], []]
        gate_order = [(j, k) for j in range(8) for k in range(4)]

        def gates_ahead():
            for n, (j, k) in enumerate(gate_order):
                b = n % 2

                def evac_of(i, b=b):
                    def evac(half, ps, m):
                        return av(sgt[b][:, HALF[half]], ps[:, :], ACT.Sigmoid, m, *sg_free[b])
                    return evac
                for r in gemm_seq("w_in2", [20 + 8 * k + j], evac_of, by_half(mA)):
                    if r is not None:
                        d = dma(sp, f"gs{b}", t["gs"][n], sgt[b][:, :], r[1])
                        sg_free[b] = [d]
                        fill.append(d)
                    yield

        for _ in proj(list(range(6, 14)), [hz[:, i, :] for i in range(8)], m_h, (), 3):
            pass

        yb_m = {}

        def hgrn():
            with ExitStack() as ch:
                bcum = sb([P, T], c=ch)
                E = sb([P, T], c=ch)
                Qp = sb([P, T], c=ch)
                Kp = sb([P, T], c=ch)
                Kt = sb([P, T], c=ch)
                kdt = sb([P, 128], c=ch)
                vr = sb([P, 8, 128], c=ch)
                st = sb([P, 128], c=ch)
                msk = sb([P, 8, 128], mybir.dt.uint8, c=ch)
                lm = dma(sp, "msk2", E[:, :], t["hmask"].rearrange("p l s -> p (l s)"))
                lm = dve.put(lambda g: g.tensor_copy(msk[:, :, :].rearrange("p l s -> p (l s)"), E[:, :]), lm)
                m = av(cc[:, 0:2], col("hlb", 0, 2), ACT.Copy, m_par)
                m = tt(dve, cc[:, 2:4], cc[:, 0:2], cc[:, 0:2], ALU.subtract, m)
                m = av(cc[:, 2:4], cc[:, 2:4], ACT.Exp, m)
                m = dve.put(lambda g: g.reciprocal(cc[:, 4:6], cc[:, 2:4]), m)
                m = tt(dve, cc[:, 2:4], cc[:, 2:4], cc[:, 4:6], ALU.mult, m)
                m = tt(dve, cc[:, 6:8], cc[:, 2:4], cc[:, 2:4], ALU.subtract, m)
                mlb = ts(dve, cc[:, 8:10], cc[:, 6:8], -1.0, 1.0, ALU.mult, ALU.add, m)
                yield
                last = []
                for tl in range(2):
                    q, f, v, g = (hz[:, 2 * e + tl, :] for e in range(4))
                    mz = [m_h[6 + 2 * e + tl] for e in range(4)]
                    m = av(f, f, ACT.Sigmoid, mz[1])
                    m = ts(dve, f, f, cc[:, 8 + tl:9 + tl], cc[:, 6 + tl:7 + tl], ALU.mult, ALU.add, m, mlb)
                    mk = ts(dve, Kt[:, :], f, -1.0, 1.0, ALU.mult, ALU.add, m, *last)
                    m = ts(dve, f, f, 2.0 ** -63, None, ALU.max, None, m)
                    m = av(f, f, ACT.Ln, m)
                    for n in range(8):
                        c = slice(n * 128, n * 128 + 128)
                        mb = dve.put(lambda g_, f=f, c=c: g_.tensor_tensor_scan(bcum[:, c], onesm[:, :], f[:, c], 0.0,
                                                                              ALU.mult, ALU.add), m, m_ones, *last)
                    yield
                    for b in range(2):
                        for n in range(4):
                            r = transpose(PSB[2][:, n * 128:n * 128 + 128],
                                          v[:, (4 * b + n) * 128:(4 * b + n) * 128 + 128], mz[2], *bank(2))
                        r = av(vr[:, 4 * b:4 * b + 4, :], PSB[2][:, :].rearrange("p (n d) -> p n d", d=128), ACT.Copy, r, *last)
                        banks[2] = r
                    mv = r
                    yield
                    lv_free = list(last)
                    for L in range(8):
                        if L == 7:
                            mq, mk2 = mz[0], mk
                            qs, ks = q, Kt[:, :]
                        else:
                            w = 1 << L
                            nb = T // (2 * w)
                            b3 = bcum[:, :].rearrange("p (n w) -> p n w", w=2 * w)
                            e3 = E[:, :].rearrange("p (n w) -> p n w", w=2 * w)
                            m = tt(dve, e3, b3, b3[:, :, w - 1:w].broadcast_to([P, nb, 2 * w]), ALU.subtract, mb, *lv_free)
                            m = av(E[:, :], E[:, :], ACT.Abs, m)
                            me = av(E[:, :], E[:, :], ACT.Exp, m, scale=-1.0)
                            mq = tt(dve, Qp[:, :], q, E[:, :], ALU.mult, me, mz[0], *lv_free)
                            mk2 = tt(pool, Kp[:, :], Kt[:, :], E[:, :], ALU.mult, me, mk, *lv_free)
                            qs, ks = Qp[:, :], Kp[:, :]
                        yield
                        for h in range(2):
                            pr = slice(64 * h, 64 * h + 64)
                            for b in range(2):
                                pb = (h * 2 + b) % 2
                                for n in range(4):
                                    cs_ = slice((4 * b + n) * 128, (4 * b + n) * 128 + 128)
                                    r = mm(PSS[:, pb, n * 128:n * 128 + 128], ks[pr, cs_], qs[pr, cs_], True, True, True,
                                           mq, mk2, *bank(4 + pb))
                                o = hs[:, h, b * 512:b * 512 + 512].rearrange("p (n s) -> p n s", s=128)
                                mkx = msk[:, L, :].unsqueeze(1).broadcast_to([P, 4, 128])
                                src = PSS[:, pb, :].rearrange("p (n s) -> p n s", s=128)
                                r2 = dve.put(lambda g_, o=o, mkx=mkx, src=src: g_.copy_predicated(o, mkx, src), r, lm, *hs_m)
                                banks[4 + pb] = r2
                                if L:
                                    pass
                            yield
                        hs_m[:] = [r2]
                        lv_free = [r]
                    m_sc = r2
                    m = memset(dve, st[:, :], 0.0, *last)
                    ms = m
                    b3 = bcum[:, :].rearrange("p (n w) -> p n w", w=128)
                    e3 = E[:, :].rearrange("p (n w) -> p n w", w=128)
                    m = av(E[:, :], bcum[:, :], ACT.Exp, mb, *lv_free)
                    mq = tt(dve, Qp[:, :], q, E[:, :], ALU.mult, m, *lv_free)
                    m = tt(dve, e3, b3, b3[:, :, 127:128].broadcast_to([P, 8, 128]), ALU.subtract, mq)
                    m = av(E[:, :], E[:, :], ACT.Exp, m, scale=-1.0)
                    mk2 = tt(dve, Kp[:, :], Kt[:, :], E[:, :], ALU.mult, m)
                    m_el = av(cc[:, 16:24], b3[:, :, 127], ACT.Exp, mb, *last)
                    yield
                    for n in range(8):
                        cs_ = slice(n * 128, n * 128 + 128)
                        o = PSB[3][:, (n % 4) * 128:(n % 4) * 128 + 128]
                        for h in range(2):
                            oh = PSB[3][64 * h:64 * h + 64, (n % 4) * 128:(n % 4) * 128 + 128]
                            mm(oh, vr[:, n, 64 * h:64 * h + 64], hs[:, h, cs_], True, False, False, mv, m_sc, *bank(3))
                            ro = mm(oh, st[:, 64 * h:64 * h + 64], Qp[:, cs_], False, True, True, mq, ms)
                        if n < 7:
                            r = transpose(PSB[2][:, 0:128], Kp[:, cs_], mk2, *bank(2))
                            r = av(kdt[:, :], PSB[2][:, 0:128], ACT.Copy, r, *kd_free)
                            banks[2] = r
                            r = mm(PSS[:, 0, 0:128], kdt[:, :], vr[:, n, :], True, True, True, r, *bank(4))
                            kd_free[:] = [r]
                            for h in range(2):
                                pr = slice(64 * h, 64 * h + 64)
                                c_ = slice(64 * h, 64 * h + 64)
                                ms = stt(st[pr, c_], st[pr, c_], cc[pr, 16 + n:17 + n], PSS[pr, 0, c_], ALU.mult, ALU.add,
                                         r, ro, m_el)
                            banks[4] = ms
                        if n % 4 == 3:
                            c = slice((n - 3) * 128, (n + 1) * 128)
                            mo = av(E[:, c], PSB[3][:, :], ACT.Copy, ro, mk2)
                            banks[3] = mo
                        yield
                    m = av(Qp[:, :], E[:, :], ACT.Square, mo, ro)
                    mg = av(g, g, ACT.Silu, mz[3])
                    for half in range(2):
                        c = slice(half * 512, half * 512 + 512)
                        r = mm(PSS[:, half, :], bd[:, 6, :], Qp[:, c], True, True, True, m, lbd, *bank(4 + half))
                        m2 = av(Kp[:, c], PSS[:, half, :], ACT.Sqrt, r, bias=col("eps"), scale=1.0 / 64)
                        banks[4 + half] = m2
                    m = dve.put(lambda g_: g_.reciprocal(Kp[:, :], Kp[:, :]), m2)
                    m = tt(dve, E[:, :], E[:, :], Kp[:, :], ALU.mult, m)
                    m = stt(E[:, :], E[:, :], col("hnorm", tl), g, ALU.mult, ALU.mult, m, mg)
                    if tl == 1:
                        hdone.append(m)
                    yb_m[4 + tl] = dma(sp, f"yh{tl}", t["yb"][4 + tl], E[:, :], m)
                    last = [m, m2, yb_m[4 + tl]]
                    yield

        hs = sb([P, 2, T], c=c6)
        hs_m = [memset(dve, hs[:, :, :], 0.0)]
        kd_free = []
        gm_ = {}

        def rest():
            a = z2
            for tl in range(2):
                yield from proj([tl, 2 + tl], [a[:, 0, :], a[:, 1, :]], gm_, tuple(rfree))
                x, g = a[:, 0, :], a[:, 1, :]
                xc, r_ = a[:, 2, :], a[:, 3, :]
                mx_, mg_ = gm_[tl], gm_[2 + tl]
                w = lambda j: col("lcw", 2 * j + tl)
                m = ts(dve, xc, x, w(3), col("lcb", tl), ALU.mult, ALU.add, mx_, *rfree)
                for d in (1, 2, 3):
                    m = stt(xc[:, d:T], x[:, 0:T - d], w(3 - d), xc[:, d:T], ALU.mult, ALU.add, m)
                yield
                m0 = m
                for half in range(2):
                    c = slice(half * 512, half * 512 + 512)
                    r = mm(PSC[0][:, :], bd[:, tl, :], xc[:, c], True, True, True, m0, lbd, *bank(6))
                    m = av(r_[:, c], PSC[0][:, :], ACT.Sigmoid, r, bias=col("lba", tl))
                    banks[6] = m
                    r = mm(PSC[1][:, :], bd[:, 2 + tl, :], xc[:, c], True, True, True, m0, lbd, *bank(7))
                    m = av(x[:, c], PSC[1][:, :], ACT.Sigmoid, r, m0, bias=col("lbx", tl))
                    banks[7] = m
                yield
                m1 = tt(dve, x, x, xc, ALU.mult, m)
                m2 = ts(dve, r_, r_, cc[:, 40 + tl:41 + tl], None, ALU.mult, None, m, m_sp)
                m = av(xc, r_, ACT.Tanh, m2, m1, scale=-1.0)
                ma = av(r_, r_, ACT.Exp, m)
                m3 = av(tq[:, :], r_, ACT.Square, ma, *rfree)
                m3 = stt(xc, tq[:, :], 1.0, xc, ALU.add, ALU.mult, m3, m)
                m3 = av(xc, xc, ACT.Sqrt, m3)
                m3 = tt(dve, x, x, xc, ALU.mult, m3)
                yield
                m3 = dve.put(lambda g_, x=x, r_=r_, xc=xc: g_.tensor_tensor_scan(xc, r_, x, 0.0, ALU.mult, ALU.add), m3, ma)
                mg_ = av(g, g, ACT.Gelu_apprx_tanh, mg_)
                m3 = tt(dve, g, xc, g, ALU.mult, m3, mg_)
                yb_m[tl] = dma(sp, f"yr{tl}", t["yb"][tl], g, m3)
                rfree[:] = [m3, yb_m[tl]]
                yield
            for tl in range(2):
                yield from proj([4 + tl], [a[:, 0, :]], gm_, tuple(rfree))
                x = a[:, 0, :]
                s2, s4 = a[:, 2, :], a[:, 3, :]

                def dbl(dst, src, w, pr, *after):
                    m = dve.put(lambda g_: g_.tensor_copy(dst[pr, 0:w], src[pr, 0:w]), *after)
                    return tt(dve, dst[pr, w:T], src[pr, w:T], src[pr, 0:T - w], ALU.add, *after, m)
                al = slice(0, 128)
                up_ = slice(64, 128)
                if tl == 0:
                    m = dbl(s2, x, 1, al, gm_[4 + tl], *rfree)
                    m = dbl(s4, s2, 2, up_, m)
                    m = dve.put(lambda g_: g_.tensor_copy(s4[0:64, :], s2[0:64, :]), m)
                else:
                    m = dbl(s2, x, 1, al, gm_[4 + tl], *rfree)
                    m = dbl(s4, s2, 2, al, m)
                    m = dbl(s2, s4, 4, al, m)
                    m = dbl(s4, s2, 8, up_, m)
                    m = dve.put(lambda g_: g_.tensor_copy(s4[0:64, :], s2[0:64, :]), m)
                yield
                m0 = tt(dve, s4[:, 0:16], s4[:, 0:16], prec[:, tl, 0:16], ALU.mult, m, lpr)
                m = ts(dve, s4[:, 16:T], s4[:, 16:T], prec[:, tl, 15:16], None, ALU.mult, None, m, lpr, m0)
                m = tt(dve, s4, s4, x, ALU.subtract, m)
                for half in range(2):
                    c = slice(half * 512, half * 512 + 512)
                    r = mm(PSC[half][:, :], bd[:, 4 + tl, :], s4[:, c], True, True, True, m, lbd, *bank(6 + half))
                    r = ts(dve, s2[:, c], PSC[half][:, :], col("pscale", tl), None, ALU.mult, None, r)
                    banks[6 + half] = r
                yb_m[2 + tl] = dma(sp, f"yp{tl}", t["yb"][2 + tl], s2, r)
                rfree[:] = [r, yb_m[2 + tl]]
                yield
            for tl in range(2):
                yield from proj([14 + tl, 16 + tl, 18 + tl], [a[:, e, :] for e in range(3)], gm_, tuple(rfree))
                w = lambda j: col("scw", 2 * j + tl)
                m = tt(dve, a[:, 1, :], a[:, 1, :], a[:, 2, :], ALU.mult, gm_[16 + tl], gm_[18 + tl])
                m = ts(dve, a[:, 2, :], a[:, 1, :], w(2), None, ALU.mult, None, m)
                for d in (1, 2):
                    m = stt(a[:, 2, d:T], a[:, 1, 0:T - d], w(2 - d), a[:, 2, d:T], ALU.mult, ALU.add, m)
                m = tt(dve, a[:, 0, :], a[:, 0, :], a[:, 2, :], ALU.mult, m, gm_[14 + tl])
                yb_m[6 + tl] = dma(sp, f"yc{tl}", t["yb"][6 + tl], a[:, 0, :], m)
                rfree[:] = [m, yb_m[6 + tl]]
                yield

        rfree = []
        tq = sb([P, T], c=c6)
        prec = sb([P, 2, 16], c=c6)
        lpr = dma(sp, "prec", prec[:, :, :], t["prec"])
        lam = col("lam", 0, 2)
        s_ = lambda i: cc[:, 24 + 2 * i:26 + 2 * i]
        m = ts(dve, s_(0), lam, -1.0, 0.0, ALU.mult, ALU.max, m_par)
        m2 = av(s_(1), lam, ACT.Abs, m_par)
        m2 = av(s_(1), s_(1), ACT.Exp, m2, scale=-1.0)
        m = ts(dve, s_(2), s_(1), 1.0, None, ALU.add, None, m2, m)
        m2 = av(s_(3), s_(2), ACT.Ln, m)
        m = ts(dve, s_(2), s_(2), -1.0, None, ALU.add, None, m, m2)
        m = ts(dve, s_(4), s_(2), 0.0, None, ALU.is_equal, None, m)
        m = tt(dve, s_(3), s_(3), s_(1), ALU.mult, m)
        m = tt(dve, s_(5), s_(4), s_(1), ALU.mult, m)
        m = tt(dve, s_(3), s_(3), s_(5), ALU.add, m)
        m = tt(dve, s_(2), s_(2), s_(4), ALU.add, m)
        m = dve.put(lambda g: g.reciprocal(s_(2), s_(2)), m)
        m = tt(dve, s_(3), s_(3), s_(2), ALU.mult, m)
        m = tt(dve, s_(3), s_(3), s_(0), ALU.add, m)
        m_sp = ts(dve, cc[:, 40:42], s_(3), -8.0, None, ALU.mult, None, m)

        hdone = []

        def until(g, stop):
            for x in g:
                if stop:
                    return
                yield

        live = [1]

        def both():
            gens = [rest(), hgrn()]
            while gens:
                for g in list(gens):
                    try:
                        next(g)
                        yield
                    except StopIteration:
                        gens.remove(g)
            live.clear()

        work, ahead = both(), gates_ahead()
        while live:
            next(work, None)
            next(work, None)
            next(ahead, None)
        fence(False)
        c6.close()

        ring[0] = 4
        with ExitStack() as c7:
            M = sb([P, NK, T], c=c7)
            wb = [sb([P, 2, 128], c=c7) for _ in range(4)]
            sgt = [sb([P, T], c=c7) for _ in range(3)]
            wb_free, sg_free, m_m = {}, {}, {}
            YB = sb([P, 8, T], c=c7)
            my = [dma(sp, f"ybl{i}", YB[:, i, :], t["yb"][i], *yb_m.values()) for i in range(8)]

            def wb_load(n):
                if n < 32:
                    j, k = gate_order[n]
                    return dma(sp, f"wb{n % 4}", wb[n % 4][:, :, :], t["w_branch"][j, k], *wb_free.get(n - 4, []))
            ld = {n: wb_load(n) for n in range(2)}

            def gate(n):
                b = n % 3
                j, k = gate_order[n]
                if n < len(fill):
                    m = dma(sp, f"gl{b}", sgt[b][:, :], t["gs"][n], *fill[-2:], *sg_free.get(n - 3, []))
                    return m

                def evac_of(i):
                    def evac(half, ps, m):
                        return av(sgt[b][:, HALF[half]], ps[:, :], ACT.Sigmoid, m, *sg_free.get(n - 3, []))
                    return evac
                _, e = until_tile(gemm_seq("w_in2", [20 + 8 * k + j], evac_of, by_half(mA)))
                return e

            gm2 = {0: gate(0)}
            for n, (j, k) in enumerate(gate_order):
                if n + 1 < 32:
                    gm2[n + 1] = gate(n + 1)
                if n + 2 < 32:
                    ld[n + 2] = wb_load(n + 2)
                mg, s, b = gm2[n], n % 4, n % 3
                for half in range(2):
                    c = HALF[half]
                    bk = 6 + half
                    for e in range(2):
                        r = mm(PSC[half][:, :], wb[s][:, e, :], YB[:, 2 * k + e, c], e == 0, e == 1, e == 1, ld[n],
                               my[2 * k + e], *bank(bk))
                    wb_free[n] = [r]
                    if k == 0:
                        r = tt(dve, M[:, j, c], sgt[b][:, c], PSC[half][:, :], ALU.mult, r, mg)
                    else:
                        r = tt(dve, sgt[b][:, c], sgt[b][:, c], PSC[half][:, :], ALU.mult, r, mg)
                    banks[bk] = r
                    if k:
                        r = tt(dve, M[:, j, c], M[:, j, c], sgt[b][:, c], ALU.add, r, m_m[(j, half)])
                    m_m[(j, half)] = r
                sg_free[n] = [r]
            done = used[state["use"] - 1]
            mA = [[split_act(A, j, M[:, j, c], c, j % 2 == 1, m_m[(j, h)], done) for j in range(8)]
                  for h, c in enumerate(HALF)]
            fence(False)
        with ExitStack() as c8:
            Y = sb([P, NK, T], c=c8)
            X = sb([P, NK, T], c=c8)
            nrm = norm_bufs(c8)
            tmp = [sb([P, 512], c=c8) for _ in range(2)]
            mx = [dma(act, f"xc{j}", X[:, j, :], t["xs2"][j]) for j in range(8)]
            out_proj("w_out2", Y, nrm, by_half(mA))
            mA, _ = residual(Y, nrm, lambda j: X[:, j, :], mx, t["xs"], lambda j: col("n2", j), lambda j: col("n3", j), None,
                             c8, tmp, key="rc")
        fence(False)

        with ExitStack() as c9:
            Y = sb([P, NK, T], c=c9)
            H = sb([P, 2, 6, T], F32R, c=c9)
            rl = [sb([P, T], c=c9) for _ in range(3)]
            nrm = norm_bufs(c9)
            rl_free = [[], [], []]

            def evac_f2(i):
                def evac(half, ps, m):
                    return av(rl[i % 3][:, HALF[half]], ps[:, :], ACT.Relu, m, *rl_free[i % 3])
                return evac

            def hid2(i, seq, H, free):
                v = rl[i % 3][:, :]
                _, last = until_tile(seq)
                m = tt(dve, v, v, v, ALU.mult, last)
                m = split_act(H, i % 6, v, ALL, True, m, *free)
                rl_free[i % 3] = [m]
                return m

            mxa = ffn("f2", 32, lambda: gemm_seq("f2u", range(32), evac_f2, by_half(mA), 3), hid2, Y, nrm, H, t["xs"], "f2")
            with ExitStack() as cx:
                _, st = residual(Y, nrm, XA, mxa, t["out"], lambda j: col("n4", j), None, None, cx, None, final=True, key="rd",
                                 diag=rl[0][:, 0:512])
        for key, (s, total) in dma_total.items():
            sp.wait((s, total))

        assert state["use"] == len(stream)
        block = ctx.enter_context(nc.Block())

        @block.sync
        def _(eng):
            sp.emit(eng)

        @block.gpsimd
        def _(eng):
            pool.emit(eng)

        @block.scalar
        def _(eng):
            act.emit(eng)

        @block.vector
        def _(eng):
            dve.emit(eng)

        @block.tensor
        def _(eng):
            pe.emit(eng)


def _panels(w):
    k, m = w.shape
    a = w.reshape(k // 128, 128, m // 128, 128).transpose(2, 1, 0, 3)
    return np.ascontiguousarray(a).reshape(m // 128, 128, k)


def _down(w):
    out = []
    a = w.reshape(-1, 128, 8, 128)
    for c, k in ffn_chunks(a.shape[0]):
        b = a[c:c + k].transpose(2, 1, 0, 3)
        per = 8 // k
        for j in range(0, 8, per):
            out.append(b[j:j + per].transpose(1, 0, 2, 3).reshape(128, 1024))
    return np.ascontiguousarray(np.stack(out))


def _vec(v):
    return v.reshape(-1, 128).T


def _constants():
    f = np.float32
    out = {"ident": np.eye(128, dtype=f)}
    n = np.arange(1024)
    ang = (n[:, None] * n[None, :]) % 1024 * (2 * np.pi / 1024)
    c, s = np.cos(ang), -np.sin(ang)
    d = np.empty((8, 128, 1024), f)
    for tp in range(8):
        r = slice(tp * 128, tp * 128 + 128)
        d[tp, :, 0:512] = c[r, 0:512]
        d[tp, :, 512:] = s[r, 0:512]
    out["dft"] = d
    m = np.arange(64)
    a64 = (m[:, None] * m[None, :]) % 64 * (2 * np.pi / 64)
    c64 = np.zeros((128, 2, 128))
    for b in range(2):
        q = slice(64 * b, 64 * b + 64)
        c64[q, 0, q] = np.cos(a64) / 256
        c64[q, 1, q] = np.sin(a64) / 256
    out["c64"] = c64.astype(f)
    dist = np.abs(np.arange(128)[:, None] + 128 - np.arange(384)[None, :]).astype(f)
    out["dist"] = np.where(dist <= 128, -dist, f(-1e30)).astype(f)
    out["alt"] = (1 - 2 * (np.arange(128) % 2)).astype(f)[:, None]
    ex = np.zeros((128, 31), f)
    msk = np.zeros((128, 15), f)
    j = np.arange(15)
    ex[:64, 0:15] = np.maximum(j - 7, 0)
    ex[64:, 0:15] = np.maximum(7 - j, 0)
    msk[:64] = j >= 7
    msk[64:] = j <= 7
    e = np.arange(8)
    ex[:64, 15:23] = e + 1
    ex[64:, 15:23] = 8 - e
    ex[:64, 23:31] = 7 - e
    ex[64:, 23:31] = e
    out["exps"], out["mask15"] = ex, msk
    k = np.arange(128, dtype=f)
    out["kidx"] = np.concatenate([np.tile(k, (64, 1)), np.tile(127 - k, (64, 1))])
    nz = np.ones((128, 128), f)
    nz[:64, 0] = 0
    nz[64:, 127] = 0
    out["nz"] = nz
    hm = np.zeros((128, 8, 128), f)
    sidx, tidx = np.arange(128)[:, None], np.arange(128)[None, :]
    for L in range(7):
        w = 1 << L
        hm[:, L, :] = (sidx // (2 * w) == tidx // (2 * w)) & (sidx % (2 * w) < w) & (tidx % (2 * w) >= w)
    hm[:, 7, :] = sidx == tidx
    out["hmask"] = hm
    pos = np.arange(1, 1025, dtype=f)
    prec = np.empty((128, 2, 16), f)
    for i, w in enumerate((2, 4, 8, 16)):
        prec[64 * (i % 2):64 * (i % 2) + 64, i // 2, :] = 1.0 / np.minimum(pos[:16], w)
    out["prec"] = prec
    return out


def _blocks(mats, n):
    per = 128 // n
    out = np.zeros((mats.shape[0] // per, 128, 128), mats.dtype)
    for i in range(mats.shape[0]):
        r = slice((i % per) * n, (i % per) * n + n)
        out[i // per, r, r] = mats[i]
    return out


def _layout(v):
    a = dict(_constants())
    a["xT"] = np.ascontiguousarray(v["x"][0].T).reshape(8, 128, 1024)
    a["w_ada"] = np.ascontiguousarray(v["w_ada"][0].reshape(8, 128, 6, 1024).transpose(2, 0, 1, 3))
    pair = np.concatenate([np.arange(64) + 64 * h for i in range(3) for h in (i, 3 + i)])
    w_in = v["w_in"][0]
    cols = np.concatenate([np.arange(384), 640 + pair, np.arange(1024, 1280), np.arange(384, 640)])
    a["w_in"] = _panels(w_in[:, cols])
    rows = np.concatenate([np.arange(640), 640 + pair])
    a["w_out"] = _panels(v["w_out"][0][rows])
    up = v["w_up"][0].reshape(1024, 2, 22, 128).transpose(0, 2, 1, 3).reshape(1024, 5632)
    a["f1u"] = _panels(up)
    a["f1d"] = _down(v["w_down"][0])
    a["w_in2"] = _panels(v["w_in_2"][0])
    a["w_out2"] = _panels(v["w_out_2"][0])
    a["f2u"] = _panels(v["w_up_2"][0])
    a["f2d"] = _down(v["w_down_2"][0])
    wb = v["w_branch_2"][0].reshape(4, 2, 128, 8, 128)
    a["w_branch"] = np.ascontiguousarray(wb.transpose(3, 0, 2, 1, 4))
    a["w_glu"] = np.ascontiguousarray(v["w_glu"][0].reshape(3, 128, 3, 128).transpose(1, 0, 2, 3))
    a["w_fft"] = np.ascontiguousarray(_blocks(v["w_fft"][0], 64).transpose(1, 0, 2))
    one = np.ones((64, 64), np.float32)
    bd = np.concatenate([_blocks(v["lru_w_a_2"][0], 32), _blocks(v["lru_w_x_2"][0], 32), _blocks(v["pool_w_2"][0], 64),
                         _blocks(np.stack([one, one]), 64), np.zeros((1, 128, 128), np.float32)])
    a["bd"] = np.ascontiguousarray(bd.transpose(1, 0, 2))
    G, S = 24, 64
    p = np.empty((2, S, 3, G), np.float32)
    p[:, :, 0] = v["lam_re"][0].transpose(0, 2, 1)
    p[:, :, 1] = v["lam_im"][0].transpose(0, 2, 1)
    p[:, :, 2] = v["log_dt"][0][:, None, :]
    a["ssm_p"] = p.reshape(128, 3, G)
    b = np.stack([v["b_re"][0], v["b_im"][0]]).transpose(1, 3, 0, 2, 4)
    a["ssm_b"] = np.ascontiguousarray(b).reshape(128, 2, G, 16)
    c = np.stack([v["c_re"][0], v["c_im"][0]]).transpose(3, 0, 1, 2)
    a["ssm_c"] = np.ascontiguousarray(np.concatenate([c, c]))
    dI = np.zeros((16, G, 16), np.float32)
    i16 = np.arange(16)
    dI[i16, :, i16] = v["d_skip"][0].reshape(G, 16).T
    a["dI"] = dI
    par = np.empty((128, NPAR), np.float32)

    def put(name, x):
        at, n = PARAM_COLS[name]
        par[:, at:at + n] = x

    put("c", _vec(v["c"][0]))
    put("b_ada", _vec(v["b_ada"][0]))
    for n in ("g_pre_mix", "g_post_mix", "g_pre_ffn", "g_post_ffn"):
        put(n, _vec(v[n][0]))
    put("conv_w", _vec(v["conv_w"][0]))
    put("conv_b", _vec(v["conv_b"][0]))
    s = v["sink"][0]
    put("sink", np.array([s[3 * g + i] for i in range(3) for g in range(2)], np.float32)[None, :])
    put("eps", np.float32(EPS))
    for n, k in (("n1", "norm_mix_pre_2"), ("n2", "norm_mix_post_2"), ("n3", "norm_mlp_pre_2"), ("n4", "norm_mlp_post_2"),
                 ("lcw", "lru_conv_w_2"), ("lcb", "lru_conv_b_2"), ("lba", "lru_b_a_2"), ("lbx", "lru_b_x_2"),
                 ("lam", "lru_lambda_2"), ("pscale", "pool_scale_2"), ("hlb", "hgrn_lower_bound_2"), ("scw", "sconv_w_2")):
        put(n, _vec(v[k][0]))
    put("hnorm", np.concatenate([v["hgrn_norm_2"][0]] * 2)[:, None])
    a["par"] = par
    return a


SCRATCH = {
    "uscr": (3, 128, 1024), "yscr": (3, 128, 1024), "vscr": (128, 2, NG, 128), "wscr": (128, 2, NG, 128),
    "cscr": (128, 2, NG, 128), "kscr": (NG, 16, 240), "yb": (8, 128, 1024), "gs": (32, 128, 1024), "xs": (8, 128, 1024), "xs2": (8, 128, 1024),
}


def kernel(**inputs):
    import concourse.bacc as _bacc
    from concourse.bass_utils import run_bass_kernel_spmd as _run

    arrays = {k: np.ascontiguousarray(a) for k, a in _layout({k: np.asarray(a) for k, a in inputs.items()}).items()}
    nc = _bacc.Bacc("TRN2", target_bir_lowering=False, num_devices=1)
    t = {}
    for k, a in arrays.items():
        t[k] = nc.dram_tensor("in_" + k, a.shape, mybir.dt.from_np(a.dtype), kind="ExternalInput").ap()
    for k, shape in SCRATCH.items():
        t[k] = nc.dram_tensor(k, shape, F32).ap()
    t["out"] = nc.dram_tensor("out_T", (8, 128, 1024), F32, kind="ExternalOutput").ap()
    build(nc, t)
    r = _run(nc, [{"in_" + k: a for k, a in arrays.items()}], core_ids=[0])
    return np.ascontiguousarray(r.results[0]["out_T"].reshape(1024, 1024).T).reshape(1, 1024, 1024)
```

```python
import math
from contextlib import ExitStack
from itertools import chain

import numpy as np
import concourse.bass as bass
from concourse import mybir

F32 = mybir.dt.float32
F32R = mybir.dt.float32r
I32 = mybir.dt.int32
ALU = mybir.AluOpType
ACT = mybir.ActivationFunctionType
AX = mybir.AxisListType

P = 128
T = 1024
D = 1024
NK = 8
EPS = 1e-6
NG = 24
TWO_PI = 2.0 * math.pi
TURN = 6.283185
MAGIC = 12582912.0
PI_LO = 3.1415925


class Queue:

    def __init__(self, sem):
        self.sem = sem
        self.items = []
        self.n = 0
        self.seen = {}

    def wait(self, *marks):
        for sem, value in marks:
            if self.seen.get(sem.name, 0) < value:
                self.seen[sem.name] = value
                self.items.append((sem, value))

    def put(self, fn, *after):
        self.wait(*after)
        self.n += 1
        self.items.append((fn, self.sem, 1))
        return (self.sem, self.n)

    def quiet(self, fn, *after):
        self.wait(*after)
        self.items.append((fn, None, 0))

    def dma(self, fn, sem, total, *after):
        self.wait(*after)
        self.items.append((fn, sem, 16))
        return (sem, total)

    def emit(self, eng):
        for it in self.items:
            if len(it) == 2:
                eng.wait_ge(it[0], it[1])
            else:
                ins = it[0](eng)
                if it[1] is not None:
                    ins.then_inc(it[1], it[2])


def weave(*gens):
    live = [[g, n] for g, n in gens]
    while live:
        for entry in list(live):
            for _ in range(entry[1]):
                try:
                    next(entry[0])
                except StopIteration:
                    live.remove(entry)
                    break


PARAM_COLS = {}


def _cols(names):
    at = 0
    for name, n in names:
        PARAM_COLS[name] = (at, n)
        at += n
    return at


NPAR = _cols([
    ("c", 8), ("b_ada", 48), ("g_pre_mix", 8), ("g_post_mix", 8), ("g_pre_ffn", 8), ("g_post_ffn", 8),
    ("conv_w", 132), ("conv_b", 44), ("sink", 6), ("eps", 1),
    ("n1", 8), ("n2", 8), ("n3", 8), ("n4", 8),
    ("lcw", 8), ("lcb", 2), ("lba", 2), ("lbx", 2), ("lam", 2), ("pscale", 2), ("hlb", 2), ("hnorm", 2),
    ("scw", 6),
])

ORDER2 = [0, 20, 2, 28, 36, 44, 1, 21, 3, 29, 37, 45, 4, 22, 30, 5, 38, 46, 14, 23, 16, 31, 18, 39, 47, 15, 24, 17, 32, 19, 40, 48, 25, 33, 41, 49, 26, 34, 42, 50, 27, 35, 43, 51]


def ffn_chunks(tiles):
    return [(c, min(4, tiles - c)) for c in range(0, tiles, 4)]


def build(nc, t):
    ctx = ExitStack()
    with ctx:
        names = [0]

        def sb(shape, dt=F32, c=ctx, side=None):
            names[0] += 1
            return c.enter_context(nc.sbuf_tensor(f"t{names[0]}", list(shape), dt, side=side))

        def sem(name):
            return ctx.enter_context(nc.semaphore(name))

        PSB = [ctx.enter_context(nc.psum_tensor(f"ps{i}", [P, 512], F32)) for i in range(4)]
        PSS = ctx.enter_context(nc.psum_tensor("pss", [P, 2, 512], F32))
        PSC = [ctx.enter_context(nc.psum_tensor(f"pc{i}", [P, 512], F32)) for i in range(2)]

        pe, act, dve, pool, sp = (Queue(sem(f"s_{n}")) for n in ("pe", "act", "dve", "pool", "sp"))
        engines = (pe, act, dve, pool)
        dma_total = {}
        dma_last = []
        phase = []

        def dma(q, key, out, in_, *after):
            if key not in dma_total:
                dma_total[key] = [sem("d_" + key), 0]
            e = dma_total[key]
            e[1] += 16
            m = q.dma(lambda g: g.dma_start(out, in_), e[0], e[1], *after, *phase)
            dma_last.append(m)
            return m

        def tt(q, out, a, b, op, *after):
            return q.put(lambda g: g.tensor_tensor(out, a, b, op), *after)

        def ts(q, out, a, s1, s2, op0, op1, *after):
            if op1 is None:
                return q.put(lambda g: g.tensor_scalar(out, a, s1, None, op0), *after)
            return q.put(lambda g: g.tensor_scalar(out, a, s1, s2, op0, op1), *after)

        def stt(out, a, s, b, op0, op1, *after):
            return dve.put(lambda g: g.scalar_tensor_tensor(out=out, in0=a, scalar=s, in1=b, op0=op0, op1=op1), *after)

        def av(out, a, func, *after, bias=None, scale=1.0, accum=None):
            kw = {"scale": scale}
            if bias is not None:
                kw["bias"] = bias
            if accum is not None:
                kw["accum_out"] = accum
            return act.put(lambda g: g.activation(out, a, func, **kw), *after)

        def memset(q, ap, v, *after):
            return q.put(lambda g: g.memset(ap, v), *after)

        def mm(out, lhsT, rhs, start, stop, last, *after, skip=False):
            kw = {"skip_group_check": True} if skip else {}
            f = lambda g: g.matmul(out, lhsT, rhs, start=start, stop=stop, **kw)
            if last:
                return pe.put(f, *after)
            pe.quiet(f, *after)

        def transpose(out, in_, *after):
            return pe.put(lambda g: g.transpose(out, in_, ident[:, :]), *after)

        def fence(pe_too=True):
            last = {s.name: (s, v) for s, v in sorted(dma_last, key=lambda m: m[1])}
            marks = [(q.sem, q.n) for q in engines] + list(last.values())
            del dma_last[:]
            phase[:] = marks
            for q in engines[0 if pe_too else 1:]:
                q.wait(*marks)
            return marks

        par = sb([P, NPAR])
        ident = sb([P, P])
        onesm = sb([P, P])
        mod = sb([P, 48])
        gmod = sb([P, 6, 8])
        r8 = sb([P, NG])
        halfpi = sb([P, 1])
        A = sb([P, 2, NK, T], F32R)
        wraw = sb([P, 3, 1024])
        whl = sb([P, 3, 2, 1024], F32R)

        def col(name, i=0, n=1):
            at = PARAM_COLS[name][0] + i
            return par[:, at:at + n]

        m_par = dma(act, "par", par[:, :], t["par"])
        m_ident = dma(act, "ident", ident[:, :], t["ident"])
        m_ones = memset(dve, onesm[:, :], 1.0)
        m_hpi = memset(dve, halfpi[:, :], math.pi / 2)

        stream = []
        for i in (0, 1, 2, 6, 7, 3, 4, 5, 8, 9):
            stream.append(("w_in", i))
        stream += [("w_out", i) for i in range(8)] * 2

        def ffn_order(name, tiles, per):
            out = []
            up = [(name + "u", i) for i in range(tiles * per)]
            dn = 0
            chunks = ffn_chunks(tiles)
            for n, (c, k) in enumerate(chunks):
                hi = min(c + k + 2, tiles)
                lo = 0 if n == 0 else min(c + 2, tiles)
                out += up[lo * per:hi * per]
                for _ in range(8 * k // 8):
                    out.append((name + "d", dn))
                    dn += 1
                if n == len(chunks) - 1 and k == 4:
                    out += out[-4:]
            return out

        stream += ffn_order("f1", 22, 2)
        stream += [("w_in2", i) for i in range(6, 14)]
        stream += [("w_in2", i) for i in ORDER2]
        stream += [("w_out2", i) for i in range(8)] * 2
        stream += ffn_order("f2", 32, 1)
        state = {"load": 0, "split": 0, "use": 0}
        loaded, split_hi, split_lo, used = {}, {}, {}, {}

        def load_panel():
            n = state["load"]
            if n >= len(stream):
                return
            name, i = stream[n]
            s = n % 3
            after = [split_hi[n - 3], split_lo[n - 3]] if n >= 3 else []
            e = dma_total.setdefault(f"w{s}", [None, 0])
            if e[0] is None:
                e[0] = sem(f"d_w{s}")
            e[1] += 16
            loaded[n] = sp.dma(lambda g, s=s, a=t[name][i]: g.dma_start(wraw[:, s, :], a), e[0], e[1], *after)
            state["load"] += 1

        def split_panel():
            n = state["split"]
            if n >= len(stream):
                return
            s = n % 3
            after = [used[n - 3]] if n >= 3 else []
            split_hi[n] = av(whl[:, s, 0, :], wraw[:, s, :], ACT.Copy, loaded[n], *after)
            split_lo[n] = tt(pool, whl[:, s, 1, :], wraw[:, s, :], whl[:, s, 0, :].bitcast(F32), ALU.subtract,
                             loaded[n], split_hi[n])
            state["split"] += 1
            load_panel()

        def panel(name, i):
            n = state["use"]
            assert stream[n] == (name, i), (stream[n], name, i)
            while state["split"] <= n:
                split_panel()
            state["use"] += 1
            return n

        def panel_done(n, mark):
            used[n] = mark
            while state["split"] <= min(n + 2, len(stream) - 1) and (state["split"] < 3 or state["split"] - 3 in used):
                split_panel()

        def gemm3(out, n, wcols, acts, ks, half, ready, *after):
            pe.wait(split_hi[n], split_lo[n], *after)
            r = None
            for i, k in enumerate(ks):
                hi = whl[:, n % 3, 0, wcols[i]:wcols[i] + 128]
                lo = whl[:, n % 3, 1, wcols[i]:wcols[i] + 128]
                xh = acts[:, 0, k, half * 512:half * 512 + 512]
                xl = acts[:, 1, k, half * 512:half * 512 + 512]
                pe.wait(*ready(half, i))
                mm(out, hi, xh, i == 0, False, False)
                mm(out, hi, xl, False, False, False)
                r = mm(out, lo, xh, False, i == len(ks) - 1, i == len(ks) - 1)
            return r

        banks = {}

        def bank(i):
            return [banks[i]] if i in banks else []

        turn = [0]

        ring = [2]

        def next_bank():
            turn[0] += 1
            return turn[0] % ring[0]

        def gemm_half(name, n, half, evac, ready):
            b = next_bank()
            m = gemm3(PSB[b][:, :], n, [128 * k for k in range(8)], A, range(8), half, ready, *bank(b))
            banks[b] = evac(half, PSB[b], m)
            return m, banks[b]

        heads_out = []

        def heads(name, idxs, mA):
            del heads_out[:]
            for i in idxs:
                n = panel(name, i)
                b = next_bank()
                m = gemm3(PSB[b][:, :], n, [128 * k for k in range(8)], A, range(8), 0, by_half(mA), *bank(b))
                heads_out.append((n, b, m))
                yield

        def gemm_seq(name, idxs, evac_of, ready, head=0, pre=()):
            idxs = list(idxs)
            first = idxs[:head]
            if first:
                if pre:
                    ns = [n for n, _, _ in pre]
                    for i, (_, b, m) in zip(first, pre):
                        banks[b] = evac_of(i)(0, PSB[b], m)
                else:
                    ns = [panel(name, i) for i in first]
                    for i, n in zip(first, ns):
                        gemm_half(name, n, 0, evac_of(i), ready)
                        yield None
                for i, n in zip(first, ns):
                    m, e = gemm_half(name, n, 1, evac_of(i), ready)
                    panel_done(n, m)
                    yield (i, e)
            for i in idxs[head:]:
                n = panel(name, i)
                gemm_half(name, n, 0, evac_of(i), ready)
                yield None
                m, e = gemm_half(name, n, 1, evac_of(i), ready)
                panel_done(n, m)
                yield (i, e)

        def until_tile(seq):
            for r in seq:
                if r is not None:
                    return r

        ALL = slice(0, T)
        HALF = [slice(0, 512), slice(512, T)]

        def by_half(mA):
            return lambda half, k: [mA[half][k]]

        def split_act(dst, j, src, cols, flip, *after):
            h = av(dst[:, 0, j, cols], src, ACT.Copy, *after)
            q = pool if flip else dve
            return tt(q, dst[:, 1, j, cols], src, dst[:, 0, j, cols].bitcast(F32), ALU.subtract, h, *after)

        rcol = sb([P, 4])
        m_rcol = []

        def rows_of(src, ps, first, last, *after):
            r = None
            for b in range(4):
                r = mm(ps[:, b:b + 1], src[:, b * 128:b * 128 + 128], onesm[:, 0:1], first and b == 0, last, b == 3, m_ones,
                       *after, skip=True)
            return r

        def rstd_bank(ps, bk, n, diag, mark):
            m = av(rcol[:, :], ps[:, 0:4], ACT.Sqrt, mark, m_par, *m_rcol, bias=col("eps"), scale=1.0 / n)
            m = dve.put(lambda g: g.reciprocal(rcol[:, :], rcol[:, :]), m)
            m = tt(dve, diag[:, :].rearrange("p (b t) -> p b t", t=128), ident[:, :].unsqueeze(1).broadcast_to([P, 4, 128]),
                   rcol[:, :].unsqueeze(2).broadcast_to([P, 4, 128]), ALU.mult, m, m_ident)
            m_rcol[:] = [m]
            return mm(ps[:, :], onesm[:, :], diag[:, :], True, True, True, m, *bank(bk))

        class Norm:

            def __init__(self, ss, sq):
                self.ss, self.sq, self.n, self.done, self.marks = ss, sq, [0, 0], [[], []], [[], []]
                self.i = 0

            def add(self, src, half, *after):
                b = self.i % 2
                self.i += 1
                c = HALF[half]
                sq = self.sq[b]
                m = av(sq[:, :], src, ACT.Square, *after, *self.marks[b])
                if self.n[half] == 0:
                    m = dve.put(lambda g: g.tensor_copy(self.ss[:, c], sq[:, :]), m)
                else:
                    m = tt(dve, self.ss[:, c], self.ss[:, c], sq[:, :], ALU.add, m, *self.done[half])
                self.done[half] = [m]
                self.marks[b] = [m]
                self.n[half] += 1

        def norm_bufs(c):
            return Norm(sb([P, T], c=c), [sb([P, 512], c=c) for _ in range(2)])

        tmp_marks = [[], [], [], []]

        def apply_half(src, half, rb, bk, gain, shift, tmp, mark, ready, free=()):
            out = []
            tm = tmp_marks
            nt = len(tmp)
            c = HALF[half]
            low = []
            for j in range(9):
                if j < 8:
                    b = j % nt
                    m = stt(tmp[b][:, :], src(j)[:, c], gain(j), rb[:, :], ALU.mult, ALU.mult, mark, *ready(j), *tm[b])
                    if j == 7:
                        banks[bk] = m
                    if shift is None:
                        h = av(A[:, 0, j, c], tmp[b][:, :], ACT.Copy, m, *free)
                    else:
                        h = av(A[:, 0, j, c], tmp[b][:, :], ACT.Identity, m, *free, bias=shift(j), scale=1.0)
                    low.append((j, b, h))
                if j:
                    i, b, h = low.pop(0)
                    hi = A[:, 0, i, c].bitcast(F32)
                    if shift is None:
                        m = tt(pool if i % 2 else dve, A[:, 1, i, c], tmp[b][:, :], hi, ALU.subtract, h)
                    else:
                        m = stt(A[:, 1, i, c], tmp[b][:, :], shift(i), hi, ALU.add, ALU.subtract, h)
                    tm[b] = [m]
                    out.append(m)
            return out

        ada_w = {}
        c0 = ExitStack()
        acc_buf = [sb([P, 1024], c=c0)[:, :]]
        ada_ring = [sb([P, 1024], c=c0)[:, :] for _ in range(4)]
        ada_used = {}
        nada = [0]
        acc_free = []

        def ada(j, bk=4, q=sp):
            m = None
            acc = acc_buf[0]
            for k in range(8):
                n = nada[0]
                nada[0] += 1
                b = n % 4
                ld = dma(q, f"ada{b}{q is sp}", ada_ring[b], t["w_ada"][j, k], *ada_used.get(n - 4, []))
                dma_last.pop()
                if k == 0:
                    m = ts(dve, acc, ada_ring[b], col("c", k), None, ALU.mult, None, ld, m_par, *acc_free)
                else:
                    m = stt(acc, ada_ring[b], col("c", k), acc, ALU.mult, ALU.add, ld, m)
                ada_used[n] = [m]
                if k % 2 == 1:
                    yield
            yield
            ps = (PSS[:, 0, :] if bk == 4 else PSB[bk])[:, 0:8]
            for i in range(8):
                r = mm(ps[:, i:i + 1], acc[:, i * 128:i * 128 + 128], onesm[:, 0:1], True, True, i == 7, m, m_ones, *bank(bk))
            acc_free[:] = [r]
            r = tt(dve, mod[:, 8 * j:8 * j + 8], ps, col("b_ada", 8 * j, 8), ALU.add, r, m_par)
            banks[bk] = r
            name = ["", "g_pre_mix", "g_post_mix", "", "g_pre_ffn", "g_post_ffn"][j]
            if j in (1, 4):
                r = ts(dve, gmod[:, j, :], mod[:, 8 * j:8 * j + 8], 1.0, None, ALU.add, None, r)
                r = tt(dve, gmod[:, j, :], gmod[:, j, :], col(name, 0, 8), ALU.mult, r)
            elif j in (2, 5):
                r = tt(dve, gmod[:, j, :], mod[:, 8 * j:8 * j + 8], col(name, 0, 8), ALU.mult, r)
            else:
                r = dve.put(lambda g: g.tensor_copy(gmod[:, j, :], mod[:, 8 * j:8 * j + 8]), r)
            ada_w[j] = r
            yield

        def gm(j):
            return lambda i: gmod[:, j, i:i + 1]

        X = sb([P, NK, T], c=c0)
        tmp = [sb([P, 512], c=c0) for _ in range(4)]
        sq, diag, diag1 = tmp[0:2], tmp[2], tmp[3]
        mA = []

        def first_norm():
            mx = [dma(act, f"x{j}", X[:, j, :], t["xT"][j]) for j in range(8)]
            g0 = chain(ada(0), ada(1))
            next(g0)
            yield
            sq_free = [[], []]
            for j in range(8):
                for half in range(2):
                    m = av(sq[half][:, :], X[:, j, HALF[half]], ACT.Square, mx[j], *sq_free[half])
                    r = rows_of(sq[half][:, :], PSB[2 + half], j == 0, j == 7, m)
                    sq_free[half] = [r]
                yield
            for _ in range(3):
                load_panel()
            rr = [rstd_bank(PSB[2 + half], 2 + half, D, dg, r) for half, dg in ((0, diag), (1, diag1))]
            for _ in g0:
                yield
            for _ in range(3):
                split_panel()
            for m in tmp_marks:
                m[:] = [rr[1]]
            for half in range(2):
                mA.append(apply_half(lambda j: X[:, j, :], half, PSB[2 + half], 2 + half, gm(1), gm(0), tmp, rr[half],
                                     lambda j: [mx[j], ada_w[0], ada_w[1]]))
                yield

        uscr, vscr, wscr, cscr, yscr, kscr = (t[n] for n in ("uscr", "vscr", "wscr", "cscr", "yscr", "kscr"))
        GB = 3
        m_r8, m_prep = [], {}

        def sincos(cos, sin, ph, *after):
            m = ts(dve, cos, ph, MAGIC, MAGIC, ALU.add, ALU.subtract, *after)
            m = tt(dve, ph, ph, cos, ALU.subtract, m)
            m1 = av(cos, ph, ACT.Abs, m)
            m2 = av(sin, ph, ACT.Sin, m, scale=TURN)
            return av(cos, cos, ACT.Sin, m1, m2, m_hpi, bias=halfpi[:, 0:1], scale=-TURN)

        def prep():
            with ExitStack() as cp:
                new = lambda *shape: sb(list(shape), c=cp, side="right")
                sp4 = new(P, 3, NG)
                Bt = new(P, 2, NG, 16)
                Ct = new(P, 2, NG, 16)
                ex = new(P, 31)
                msk = new(P, 15)
                kidx = new(P, 128)
                w = new(P, 12, NG)
                PW = new(P, 2, NG, 31)
                dI = new(16, NG, 16)
                R = new(P, 6192)
                ldp = [dma(sp, "sp4", sp4[:, :, :], t["ssm_p"]), dma(sp, "Bt", Bt[:, :, :, :], t["ssm_b"]),
                       dma(sp, "Ct", Ct[:, :, :, :], t["ssm_c"]), dma(sp, "ex", ex[:, :], t["exps"]),
                       dma(sp, "msk", msk[:, :], t["mask15"]), dma(sp, "kidx", kidx[:, :], t["kidx"]),
                       dma(sp, "dI", dI[:, :, :], t["dI"])]
                yield
                re, im, ld = sp4[:, 0, :], sp4[:, 1, :], sp4[:, 2, :]
                dt, ar, ai, n_, r_, mag, cs, sn, den, q1, q2, psi = (w[:, i, :] for i in range(12))
                m = av(dt, ld, ACT.Exp, *ldp)
                m1 = tt(dve, ar, re, dt, ALU.mult, m)
                m2 = tt(dve, ai, im, dt, ALU.mult, m)
                m = ts(dve, n_, ai, 1.0 / TWO_PI, MAGIC, ALU.mult, ALU.add, m2)
                m = ts(dve, n_, n_, MAGIC, None, ALU.subtract, None, m)
                r = ai
                for cc in (6.28125, 0.0019350051879882812, 3.01991605743e-07):
                    m = stt(r_, n_, -cc, r, ALU.mult, ALU.add, m)
                    r = r_
                mr = m
                yield
                mm_ = av(mag, ar, ACT.Exp, m1)
                m = ts(dve, q1, r_, PI_LO, -PI_LO, ALU.min, ALU.max, mr)
                ms = av(sn, q1, ACT.Sin, m)
                m = av(q2, q1, ACT.Abs, m)
                m = ts(dve, q2, q2, math.pi / 2, None, ALU.subtract, None, m)
                mc = av(cs, q2, ACT.Sin, m, scale=-1.0)
                mp = ts(dve, psi, r_, 1.0 / TWO_PI, None, ALU.mult, None, mr)
                yield
                bg = lambda a: a.unsqueeze(2).broadcast_to([P, NG, 31])
                be = ex[:, :].unsqueeze(1).broadcast_to([P, NG, 31])
                s31 = [R[:, i * 744:i * 744 + 744].rearrange("p (g e) -> p g e", e=31) for i in range(2)]
                m3 = tt(dve, s31[0], bg(ar), be, ALU.mult, m1, mc)
                mg = av(s31[0], s31[0], ACT.Exp, m3)
                m3 = tt(dve, s31[1], bg(psi), be, ALU.mult, mp)
                mP = sincos(PW[:, 0, :, :], PW[:, 1, :, :], s31[1], m3)
                m = tt(dve, cs, cs, mag, ALU.mult, mc, mm_)
                m = ts(dve, cs, cs, -1.0, None, ALU.add, None, m)
                m = tt(dve, sn, sn, mag, ALU.mult, ms, m)
                m = tt(dve, q1, re, re, ALU.mult, m)
                m = tt(dve, q2, im, im, ALU.mult, m)
                m = tt(dve, den, q1, q2, ALU.add, m)
                m = dve.put(lambda g: g.reciprocal(den, den), m)
                m = tt(dve, q1, cs, re, ALU.mult, m)
                m = tt(dve, q2, sn, im, ALU.mult, m)
                m = tt(dve, q1, q1, q2, ALU.add, m)
                m = tt(dve, n_, q1, den, ALU.mult, m)
                m = tt(dve, q1, sn, re, ALU.mult, m)
                m = tt(dve, q2, cs, im, ALU.mult, m)
                m = tt(dve, q1, q1, q2, ALU.subtract, m)
                m = tt(dve, q1, q1, den, ALU.mult, m)
                yield
                bc = lambda a: a.unsqueeze(2).broadcast_to([P, NG, 16])
                bb = [Bt[:, i, :, :] for i in range(2)]
                s16 = [R[:, 1488 + 384 * i:1872 + 384 * i].rearrange("p (g c) -> p g c", c=16) for i in range(3)]
                m = tt(dve, s16[0], bb[0], bc(n_), ALU.mult, m)
                m = tt(dve, s16[1], bb[1], bc(q1), ALU.mult, m)
                m = tt(dve, s16[0], s16[0], s16[1], ALU.subtract, m)
                m = tt(dve, s16[1], bb[0], bc(q1), ALU.mult, m)
                m = tt(dve, s16[2], bb[1], bc(n_), ALU.mult, m)
                m = tt(dve, bb[1], s16[1], s16[2], ALU.add, m)
                m = dve.put(lambda g: g.tensor_copy(bb[0], s16[0]), m)
                yield
                m = tt(dve, PW[:, 0, :, :], PW[:, 0, :, :], s31[0], ALU.mult, mP, mg)
                m = tt(dve, PW[:, 1, :, :], PW[:, 1, :, :], s31[0], ALU.mult, m)
                bm = msk[:, :].unsqueeze(1).broadcast_to([P, NG, 15])
                m = tt(dve, PW[:, 0, :, 0:15], PW[:, 0, :, 0:15], bm, ALU.mult, m)
                mP = tt(dve, PW[:, 1, :, 0:15], PW[:, 1, :, 0:15], bm, ALU.mult, m)
                m = ts(dve, q1, psi, 8.0, None, ALU.mult, None, mP)
                m = ts(dve, q2, q1, MAGIC, None, ALU.add, None, m)
                m = ts(dve, q2, q2, MAGIC, None, ALU.subtract, None, m)
                m8 = tt(dve, q1, q1, q2, ALU.subtract, m)
                m_r8.append(av(r8[:, :], ar, ACT.Exp, m1, scale=8.0))
                yield
                pend = []
                cs_free = [[], []]

                def flush():
                    for f in pend:
                        f()
                    del pend[:]

                tm = [R[:, 720 * i:720 * i + 720] for i in range(2)]
                bigs = {"v": (1440, 8), "w": (2208, 8), "k": (2976, 15)}
                Wt = R[:, 4416:5184]
                ko = R[:, 5184:5424]
                ldk = []

                def cmul(src, name, off, gs, neg, *after):
                    at, nblk = bigs[name]
                    if name == "v" and (gs.start // GB) % 2:
                        at = 5424
                    n = GB * nblk * 16
                    v4 = lambda a: a[:, 0:n].rearrange("p (g e c) -> p g e c", e=nblk, c=16)
                    t0, t1 = v4(tm[0]), v4(tm[1])
                    d_re, d_im = v4(R[:, at:at + n]), v4(R[:, at + n:at + 2 * n])
                    pr, pi = (PW[:, i, gs, off:off + nblk].unsqueeze(3).broadcast_to([P, GB, nblk, 16]) for i in range(2))
                    sr, si = (src[:, i, gs, :].unsqueeze(2).broadcast_to([P, GB, nblk, 16]) for i in range(2))
                    a = tt(dve, t0, sr, pr, ALU.mult, *after)
                    b = tt(dve, t1, si, pi, ALU.mult, *after)
                    a = tt(dve, d_re, t0, t1, ALU.subtract, a, b)
                    b = tt(dve, t0, sr, pi, ALU.mult, a)
                    c = tt(dve, t1, si, pr, ALU.mult, a)
                    if neg:
                        return stt(d_im, t0, -1.0, t1, ALU.mult, ALU.subtract, b, c)
                    return tt(dve, d_im, t0, t1, ALU.add, b, c)

                free = {"wt": [], "k": []}
                m = mP
                w_pe = []
                for b0 in range(0, NG, GB):
                    gs = slice(b0, b0 + GB)
                    vb = (b0 // GB) % 2
                    vat = 5424 if vb else 1440
                    m = cmul(Ct, "v", 15, gs, True, m, *ldk, *free.get(("v", vb), []))

                    def st_v(gs=gs, m=m, vb=vb, vat=vat):
                        free[("v", vb)] = [dma(pool, f"vs{vb}", vscr[:, :, gs, :],
                                         R[:, vat:vat + 768].rearrange("p (i g n) -> p i g n", i=2, n=128), m)]
                    pend.append(st_v)
                    yield
                    mw = m = cmul(Bt, "w", 23, gs, False, m, *w_pe)
                    yield
                    flush()
                    m = cmul(Ct, "k", 0, gs, True, m, *free["k"])
                    for i in range(2):
                        for g in range(GB):
                            r = transpose(PSC[i][:, g * 128:g * 128 + 128],
                                          R[:, 2208 + i * 384 + g * 128:2336 + i * 384 + g * 128], mw, m_ident, *bank(6 + i))
                        banks[6 + i] = av(Wt[:, i * 384:i * 384 + 384], PSC[i][:, 0:384], ACT.Copy, r, *free["wt"], *ldk)
                    w_pe = [r]

                    def st_w(gs=gs, m=banks[7]):
                        free["wt"] = [dma(pool, "ws", wscr[:, :, gs, :], Wt.rearrange("p (i g n) -> p i g n", i=2, n=128), m)]
                    pend.append(st_w)
                    yield
                    flush()
                    for g in range(GB):
                        o = PSC[1][32 * g:32 * g + 16, 0:240]
                        for i in range(2):
                            at = 2976 + 720 * i + 240 * g
                            r = mm(o, Bt[:, i, b0 + g, :], R[:, at:at + 240], i == 0, i == 1, i == 1, m, *bank(7))
                    k_pe = [r]
                    for g in range(GB):
                        r = av(ko[32 * g:32 * g + 16, :], PSC[1][32 * g:32 * g + 16, 0:240], ACT.Copy, r, *free.get("ko", []), *ldk)
                    banks[7] = r
                    free["k"] = k_pe

                    def st_k(b0=b0, m=r):
                        for g in range(GB):
                            d = dma(pool, "ks", kscr[b0 + g], ko[32 * g:32 * g + 16, :], m)
                        free["ko"] = [d]
                    pend.append(st_k)
                    yield
                flush()
                kb = PW[0:16, 0, :, :].rearrange("p g e -> p (g e)")[:, 0:NG * 16].rearrange("p (g n) -> p g n", n=16)
                l1 = dma(sp, "kl", kb, kscr[:, :, 112:128].rearrange("g c n -> c g n"), *free["ko"], m)
                v_st = [*free[("v", 0)], *free[("v", 1)]]
                mk = m
                rot_free = [v_st, [*v_st, w_pe[0], k_pe[0], banks[7]], [w_pe[0], k_pe[0], *free["wt"]], [*free["wt"], *free["ko"], *v_st]]
                cs_free = [[] for _ in range(4)]
                for n in range(6):
                    b = n % 4
                    gs = slice(4 * n, 4 * n + 4)
                    at = 1536 * b
                    ph, co, si = (R[:, at + 512 * i:at + 512 * i + 512].rearrange("p (g k) -> p g k", k=128) for i in range(3))
                    m = tt(dve, ph, q1[:, gs].unsqueeze(2).broadcast_to([P, 4, 128]),
                           kidx[:, :].unsqueeze(1).broadcast_to([P, 4, 128]), ALU.mult, m8, mP, mk, *rot_free[b], *cs_free[b])
                    m = sincos(co, si, ph, m)

                    def store(gs=gs, at=at, b=b, m=m):
                        cs_free[b] = [dma(pool, f"cs{b}", cscr[:, :, gs, :],
                                          R[:, at + 512:at + 1536].rearrange("p (i g k) -> p i g k", i=2, k=128), m)]
                    pend.append(store)
                    yield
                    flush()
                flush()
                m = tt(dve, kb, kb, dI[:, :, :], ALU.add, l1, *ldp)
                m_k2 = dma(sp, "kl2", kscr[:, :, 112:128].rearrange("g c n -> c g n"), kb, m)
                yield
                m_prep["c"] = [m for f in cs_free for m in f]
                m_prep.update(k=[m_k2], v=v_st, w=free["wt"])
                prep_done.extend([m, m_k2, *m_prep["c"], w_pe[0], k_pe[0], banks[7], *v_st, *free["wt"]])

        prep_done = []
        tables = prep()
        norm0 = first_norm()
        next(tables)
        for n, _ in enumerate(norm0):
            if n % 2:
                next(tables, None)
        c0.close()
        fence(False)

        pu = ExitStack()
        uT = sb([P, 3, 8, 128], c=pu)
        fT = sb([P, 2, T], c=pu)
        qT = sb([P, 3, T], c=pu)
        kT = sb([P, T], c=pu)
        vT = sb([P, T], c=pu)
        ada_fin = []
        acc1 = sb([P, 1024], c=pu)
        m_z, m_us, m_y = {}, [], {}
        dist = sb([P, 384], c=pu)
        alt = sb([P, 1], c=pu)
        m_dist = dma(sp, "dist", dist[:, :], t["dist"])
        l0 = dma(sp, "alt", alt[:, :], t["alt"])

        def ada_rest():
            while "v" not in m_z or len(m_us) < 3:
                yield
            acc_buf[0] = acc1[:, :]
            for b in range(3):
                ada_ring[b] = uT[:, b, :, :].rearrange("p t k -> p (t k)")
                ada_used[nada[0] - 4 + b] = [m_us[b]]
            ada_ring[3] = vT[:, :]
            ada_used[nada[0] - 1] = [m_z["v"]]
            for j in (2, 4, 3, 5):
                yield from ada(j, 1, pool)
            ada_fin.extend(ada_used[nada[0] - 1])

        def w_in_all():
            def evac_of(i):
                def evac(half, ps, m):
                    if i < 3:
                        o = uT[:, i, :, half * 64:half * 64 + 64]
                        r = act.put(lambda g: g.activation(o, ps[:, :].rearrange("p (k t) -> p t k", t=8), ACT.Copy), m)
                    elif i in (6, 7):
                        r = av((kT if i == 6 else vT)[:, HALF[half]], ps[:, :], ACT.Copy, m)
                    elif i < 6:
                        r = av(qT[:, i - 3, HALF[half]], ps[:, :], ACT.Copy, m, scale=0.125)
                    else:
                        r = av(fT[:, i - 8, HALF[half]], ps[:, :], ACT.Copy, m)
                    m_z[i] = r
                    return r
                return evac
            for r in gemm_seq("w_in", (0, 1, 2, 6, 7, 3, 4, 5, 8, 9), evac_of, by_half(mA), 3):
                if r is not None and r[0] < 3:
                    i = r[0]
                    m_us.append(dma(sp, f"us{i}", uscr[i], uT[:, i, :, :].rearrange("p t k -> p (t k)"), r[1]))
                if r is not None and r[0] == 9:
                    m_z["done"] = used[state["use"] - 1]
                yield

        NB = 4

        def ssm():
            c2 = ExitStack()
            new = lambda *shape: sb(list(shape), c=c2, side="right")
            U = new(P, NG, 128)
            WV = new(P, 4, NB, 128)
            Wb, Vb = WV[:, 0:2, :, :], WV[:, 2:4, :, :]
            Tb = new(P, NB, 128)
            Cb = new(P, 2, NB, 128)
            Hb = new(P, 2, NB, 128)
            Mt = new(P, 2, NB, 128)
            Rb = new(P, NB, 128)
            nz = new(P, 128)
            xt = new(P, NB, 128)
            H2 = new(P, 2, NB, 128)
            mz2 = None
            glf = WV[:, :, :, :].rearrange("p a b c -> p (a b c)")[:, 0:1152]
            glw = glf.rearrange("p (a b c) -> p a b c", a=3, b=3)
            m_nz = dma(sp, "nz", nz[:, :], t["nz"], *prep_done)
            for s in range(8):
                src = bass.AP(tensor=uscr.tensor, offset=128 * s, ap=[[1024, 16], [16 * 1024, NG], [1, 128]])
                ld_u = dma(sp, "ul", U[16 * s:16 * s + 16, :, :], src, *m_us, *prep_done)
            free = {"w": prep_done, "t": prep_done, "v": prep_done, "c": prep_done, "h": prep_done, "x": prep_done}
            lw, lt, lv, lc = {}, {}, {}, {}

            def load_w(b0):
                if b0 < NG:
                    lw[b0] = dma(sp, "lw", Wb, wscr[:, :, b0:b0 + NB, :], *m_prep["w"], *free["w"])

            def load_c(b0):
                if b0 < NG:
                    lc[b0] = dma(sp, "lc", Cb[:, :, :, :], cscr[:, :, b0:b0 + NB, :], *m_prep["c"], *free["c"])

            def load_tv(b0):
                if b0 < NG:
                    for s in range(8):
                        src = bass.AP(tensor=kscr.tensor, offset=b0 * 3840 + (7 - s) * 16,
                                      ap=[[240, 16], [3840, NB], [1, 128]])
                        lt[b0] = dma(sp, "lt", Tb[16 * s:16 * s + 16, :, :], src, *m_prep["k"], *free["t"])
                    lv[b0] = dma(sp, "lv", Vb, vscr[:, :, b0:b0 + NB, :], *m_prep["v"], *free["v"])

            load_w(0)
            load_c(0)
            load_tv(0)
            yield
            m_ys = None
            for _ in range(3):
                yield
            for b0 in range(0, NG, NB):
                gs = slice(b0, b0 + NB)
                for i in range(2):
                    for g in range(NB):
                        for d in range(2):
                            r = mm(PSC[i][64 * d:64 * d + 64, g * 128:g * 128 + 128], Wb[:, i, g, 64 * d:64 * d + 64],
                                   U[:, b0 + g, ::1 - 2 * d], True, True, g == NB - 1 and d == 1, lw[b0], ld_u, *bank(6 + i))
                    m_x = r
                free["w"] = [m_x]
                load_w(b0 + NB)
                mrb = tt(dve, Rb[:, :, :], nz[:, :].unsqueeze(1).broadcast_to([P, NB, 128]),
                         r8[:, gs].unsqueeze(2).broadcast_to([P, NB, 128]), ALU.mult, m_nz, *m_r8, *free["x"])
                yield
                x = [PSC[i][:, :].rearrange("p (g k) -> p g k", k=128) for i in range(2)]
                cs, sn = Cb[:, 0, :, :], Cb[:, 1, :, :]
                h0, h1 = Hb[:, 0, :, :], Hb[:, 1, :, :]
                t0, t1 = Mt[:, 0, :, :], Mt[:, 1, :, :]
                a = tt(dve, h0, x[0], cs, ALU.mult, m_x, lc[b0])
                b = tt(dve, t1, x[0], sn, ALU.mult, a)
                banks[6] = b
                c = tt(dve, t0, x[1], sn, ALU.mult, b)
                d = tt(dve, h1, x[1], cs, ALU.mult, c)
                banks[7] = d
                a = tt(pool, h0, h0, t0, ALU.add, c)
                d = tt(dve, h1, h1, t1, ALU.subtract, d)
                yield
                for i in (1, 0):
                    src, dst = (q[:, i, :, :].rearrange("p g k -> p (g k)") for q in (Hb, Mt))
                    rr = Rb[:, :, :].rearrange("p g k -> p (g k)")
                    sc_m = dve.put(lambda g_, src=src, dst=dst, rr=rr: g_.tensor_tensor_scan(
                        dst, rr, src, 0.0, ALU.mult, ALU.add), d, mrb, *([a] if i == 0 else []))
                yield
                if b0 == 0:
                    memset(dve, H2[0:64, :, :, 0:1], 0.0, *prep_done)
                    mz2 = memset(dve, H2[64:128, :, :, 127:128], 0.0)
                so = slice(0, 127)
                for i in range(2):
                    ph, pt = Hb[:, i, :, so], xt[:, :, so]
                    ma = tt(dve, ph, Mt[:, 0, :, so], Cb[:, i, :, so], ALU.mult, sc_m)
                    mb = tt(pool if i == 0 else dve, pt, Mt[:, 1, :, so], Cb[:, 1 - i, :, so], ALU.mult, sc_m, *free["x"])
                    for pr, do in ((slice(0, 64), slice(1, 128)), (slice(64, 128), slice(126, None, -1))):
                        mh = tt(dve, H2[pr, i, :, do], Hb[pr, i, :, so], xt[pr, :, so], ALU.subtract if i == 0 else ALU.add,
                                ma, mb, mz2, *free["h"])
                    free["x"] = [mh]
                free["c"] = [mh]
                load_c(b0 + NB)
                for _ in range(4):
                    yield
                for g in range(NB):
                    o = PSC[0][:, g * 128:g * 128 + 128]
                    mm(o, Tb[:, g, :], U[:, b0 + g, :], True, False, False, lt[b0], *bank(6))
                    for i in range(2):
                        r = mm(o, Vb[:, i, g, :], H2[:, i, g, :], False, i == 1, g == NB - 1 and i == 1, lv[b0], mh)
                free["t"] = free["v"] = free["h"] = [r]
                load_tv(b0 + NB)
                yield
                r = av(U[:, gs, :], PSC[0][:, :].rearrange("p (g k) -> p g k", k=128), ACT.Copy, r)
                banks[6] = r
                for s in range(8):
                    dst = bass.AP(tensor=yscr.tensor, offset=b0 * 16384 + 128 * s,
                                  ap=[[1024, 16], [16 * 1024, NB], [1, 128]])
                    m_ys = dma(act if s % 2 else sp, "ysa" if s % 2 else "ysb", dst, U[16 * s:16 * s + 16, gs, :], r)
                    ysm[s % 2] = m_ys
                yield
            m_glw = dma(sp, "glw", glf, t["w_glu"].rearrange("p a b c -> p (a b c)"), *free["v"], *free["w"])
            while not ada_fin:
                yield
            for i in range(3):
                ly = dma(sp, "yl", uT[:, i, :, :].rearrange("p t k -> p (t k)"), yscr[i], *ysm, *m_us, *ada_fin)
            yf = uT[:, :, :, :].rearrange("p i t k -> p i (t k)")
            for _ in range(4):
                yield
            ge = [av(yf[:, i, :], yf[:, i, :], ACT.Gelu_apprx_tanh, ly) for i in range(3)]
            yield
            yield
            gp = [ysm, ysm]
            glu_next = []

            def glu_out():
                b, j, half, c, m = glu_next.pop(0)
                m = tt(dve, sg[:, b, :], sg[:, b, :], yf[:, j, c], ALU.mult, m)
                oh, ol = (A[:, e, j, :].rearrange("p (k t) -> p t k", t=8)[:, 4 * half:4 * half + 4, :] for e in range(2))
                sv = sg[:, b, :].rearrange("p (t k) -> p t k", k=128)
                h = av(oh, sv, ACT.Copy, m, m_z["done"])
                m = tt(pool, ol, sv, oh.bitcast(F32), ALU.subtract, h)
                gp[b] = [m]
                m_y[("s", j, half)] = m

            sg = U[:, 0:16, :].rearrange("p (a g) k -> p a (g k)", a=4)
            for j in range(3):
                for half in range(2):
                    c = slice(half * 512, half * 512 + 512)
                    for i in range(3):
                        r = mm(PSC[half][:, :], glw[:, i, j, :], yf[:, i, c], i == 0, i == 2, i == 2, m_glw, *ge,
                               *bank(6 + half))
                    b = half
                    m = av(sg[:, b, :], PSC[half][:, :], ACT.Sigmoid, r, *gp[b])
                    banks[6 + half] = m
                    glu_next.append((b, j, half, c, m))
                    yield
                    if len(glu_next) > 1:
                        glu_out()
                        yield
            glu_out()
            c2.close()

        ysm = [None, None]

        def attention():
            with ExitStack() as ca:
                vrow = sb([P, 8, 128], c=ca)
                scb = [sb([P, 2, 384], c=ca) for _ in range(3)]
                pts = [sb([P, 384], c=ca) for _ in range(2)]
                small = sb([P, 3, 16], c=ca)
                for b in range(2):
                    for n in range(4):
                        r = transpose(PSB[2 + b][:, n * 128:n * 128 + 128],
                                      vT[:, (4 * b + n) * 128:(4 * b + n) * 128 + 128], m_z[7], m_ident, *bank(2 + b))
                    r = av(vrow[:, 4 * b:4 * b + 4, :], PSB[2 + b][:, :].rearrange("p (n d) -> p n d", d=128), ACT.Copy, r)
                    banks[2 + b] = r
                m_v = m_z["v"] = r
                units = [(i, n) for i in range(3) for n in range(8)]
                span = lambda n: (128 if n == 0 else 0, 256 if n == 7 else 384)
                sc_free = [[], [], []]
                pt_used = [[], []]
                mst = {}

                def stage_a(u):
                    i, n = units[u]
                    b = u % 3
                    lo, hi = span(n)
                    kc = slice((n - 1) * 128 + lo, (n - 1) * 128 + hi)
                    w = hi - lo
                    sc, sm = scb[b], small[:, b, :]
                    for g in range(2):
                        pr = slice(64 * g, 64 * g + 64)
                        r = mm(PSS[:, g, 0:w], qT[pr, i, n * 128:n * 128 + 128], kT[pr, kc], True, True, True,
                               m_z[6], m_z[3 + i], *bank(4 + g))
                        slope = float(np.exp2(np.float32(-8.0) * np.float32(3 * g + i + 1) / np.float32(6)))
                        m = stt(sc[:, g, 0:w], dist[:, lo:hi], slope, PSS[:, g, 0:w], ALU.mult, ALU.add, r, m_dist, *sc_free[b])
                        banks[4 + g] = m
                    m = dve.put(lambda g_: g_.tensor_reduce(sm[:, 0:2], sc[:, :, 0:w], AX.X, ALU.max), m)
                    m = tt(dve, sm[:, 0:2], sm[:, 0:2], col("sink", 2 * i, 2), ALU.max, m)
                    m1 = ts(dve, sm[:, 2:4], sm[:, 0:2], -1.0, None, ALU.mult, None, m)
                    m2 = tt(dve, sm[:, 4:6], col("sink", 2 * i, 2), sm[:, 0:2], ALU.subtract, m)
                    mst[u] = m2

                def stage_b(u):
                    i, n = units[u]
                    b = u % 3
                    lo, hi = span(n)
                    w = hi - lo
                    sc, sm = scb[b], small[:, b, :]
                    for g in range(2):
                        e = av(sc[:, g, 0:w], sc[:, g, 0:w], ACT.Exp, mst[u], bias=sm[:, 2 + g:3 + g], accum=sm[:, 6 + g:7 + g])
                    mst[("e", u)] = av(sm[:, 8:10], sm[:, 4:6], ACT.Exp, mst[u])

                def stage_n(u):
                    i, n = units[u]
                    b = u % 3
                    lo, hi = span(n)
                    w = hi - lo
                    sc, sm = scb[b], small[:, b, :]
                    e = mst[("e", u)]
                    m = tt(dve, sm[:, 8:10], sm[:, 8:10], sm[:, 6:8], ALU.add, e)
                    m = dve.put(lambda g_: g_.reciprocal(sm[:, 10:12], sm[:, 8:10]), m)
                    for g in range(2):
                        mn = ts(dve, sc[:, g, 0:w], sc[:, g, 0:w], sm[:, 10 + g:11 + g], None, ALU.mult, None, m, e)
                    mst[u] = mn

                def stage_c(u):
                    i, n = units[u]
                    b = u % 3
                    lo, hi = span(n)
                    w = hi - lo
                    sc = scb[b]
                    for g in range(2):
                        tb = 2 if g == 0 else 0
                        for s in range(w // 128):
                            r = transpose(PSB[tb][:, s * 128:s * 128 + 128], sc[:, g, s * 128:s * 128 + 128], mst[u],
                                          *bank(tb))
                        banks[tb] = av(pts[g][:, 0:w], PSB[tb][:, 0:w], ACT.Copy, r, *pt_used[g])
                        mst[(u, g)] = banks[tb]
                    sc_free[b] = [r]

                def stage_d(u):
                    i, n = units[u]
                    lo, hi = span(n)
                    nb = (hi - lo) // 128
                    for g in range(2):
                        o = PSB[3][64 * g:64 * g + 64, (n % 4) * 128:(n % 4) * 128 + 128]
                        for s in range(nb):
                            blk = (n - 1) + lo // 128 + s
                            q = mm(o, vrow[:, blk, 64 * g:64 * g + 64], pts[g][:, s * 128:s * 128 + 128], s == 0,
                                   s == nb - 1, s == nb - 1, mst[(u, g)], m_v, *bank(3))
                        pt_used[g] = [q]
                    if n % 4 == 3:
                        c = slice((n - 3) * 128, (n + 1) * 128)
                        h = av(A[:, 0, 5 + i, c], PSB[3][:, :], ACT.Copy, q, m_z["done"])
                        l = tt(dve, A[:, 1, 5 + i, c], PSB[3][:, :], A[:, 0, 5 + i, c].bitcast(F32), ALU.subtract, h)
                        banks[3] = l
                        m_y[("a", i, n // 4)] = l
                        mst["out"] = l
                    mst["last"] = q

                nu = len(units)
                for u in range(nu + 3):
                    if 0 <= u - 1 < nu:
                        stage_b(u - 1)
                    if u < nu:
                        stage_a(u)
                    if u >= 3:
                        stage_d(u - 3)
                    yield
                    if 0 <= u - 1 < nu:
                        stage_n(u - 1)
                        yield
                    if 0 <= u - 2 < nu:
                        stage_c(u - 2)
                        yield
                att_done.extend([mst["last"], mst["out"]])

        att_done = []

        def fourier():
            while not ada_fin:
                yield
            with ExitStack() as cf:
                FA = sb([P, 8, 2, 256], c=cf)
                c64 = kT[:, 0:256].rearrange("p (i d) -> p i d", i=2)
                WC = kT[:, 512:1024].rearrange("p (a i d) -> p a i d", a=2, i=2)
                wf = kT[:, 256:512].rearrange("p (i d) -> p i d", i=2)
                dft = [qT[:, i, :] for i in range(3)] + [vT[:, :]]
                l1 = dma(sp, "c64", c64, t["c64"], *att_done)
                l2 = dma(sp, "wf", wf, t["w_fft"], *att_done)
                used_d, ld = {}, {}

                def load_d(n):
                    if n < 8:
                        ld[n] = dma(sp, f"dft{n % 4}", dft[n % 4], t["dft"][n], *att_done, *used_d.get(n - 4, []))
                for n in range(4):
                    load_d(n)
                for pr in range(2):
                    for i in range(2):
                        r = mm(PSB[0][:, (pr * 2 + i) * 128:(pr * 2 + i) * 128 + 128], c64[:, i, :], wf[:, pr, :], True, True,
                               True, l1, l2, *bank(0))
                m_wc = dve.put(lambda g: g.tensor_copy(WC.rearrange("p a b c -> p (a b c)"), PSB[0][:, :]), r,
                               *att_done)
                banks[0] = m_wc
                yield
                fa = []
                for tp in range(8):
                    b = tp % 2
                    for pr in range(2):
                        r = mm(PSB[b][:, pr * 256:pr * 256 + 256], fT[:, pr, tp * 128:tp * 128 + 128],
                               WC[:, pr, :, :].rearrange("p a b -> p (a b)"), True, True, True, m_wc, m_z[9], m_z[8], *bank(b))
                    o = FA[:, tp, :, :].rearrange("p a b -> p (a b)")
                    if tp % 2:
                        r = av(o, PSB[1][:, :], ACT.Copy, r, *att_done)
                    else:
                        r = dve.put(lambda g, o=o: g.tensor_copy(o, PSB[0][:, :]), r, *att_done)
                    banks[b] = r
                    fa.append(r)
                    yield
                for tp in range(8):
                    for i in range(2):
                        for pr in range(2):
                            b = 2 * i + pr
                            r = mm(PSB[b][:, :], FA[:, tp, pr, i * 128:i * 128 + 128], dft[tp % 4][:, i * 512:i * 512 + 512],
                                   tp == 0, tp == 7, True, ld[tp], fa[tp], fa[7], *bank(b))
                    used_d[tp] = [r]
                    load_d(tp + 4)
                    yield
                m_pq = r
                for pr in range(2):
                    for tp in range(8):
                        r = mm(PSS[:, 0, pr:pr + 1], FA[:, tp, pr, 0:128], alt[:, :], tp == 0, tp == 7, tp == 7, l0,
                               *bank(4))
                m_mid = r
                yield
                for pr in range(2):
                    Pb, Qb = PSB[pr], PSB[2 + pr]
                    st = FA[:, 2 * pr:2 * pr + 2, :, :].rearrange("p a b c -> p (a b c)")
                    a = dve.put(lambda g, Pb=Pb, st=st: g.tensor_copy(st[:, 0:512], Pb[:, :]), m_pq, m_mid)
                    b1 = tt(dve, st[:, 513:1024], st[:, 1:512], Qb[:, 1:512], ALU.subtract, a)
                    b2 = tt(dve, st[:, 0:512], st[:, 0:512], Qb[:, :], ALU.add, b1)
                    banks[pr], banks[2 + pr] = a, b2
                    b3 = dve.put(lambda g, pr=pr, st=st: g.tensor_copy(st[:, 512:513], PSS[:, 0, pr:pr + 1]), m_mid, b2)
                    banks[4] = b3
                    for half, src, dst in ((0, st[:, 0:512], HALF[0]), (1, st[:, 512:513], slice(512, 513)),
                                           (1, st[:, 513:1024], slice(1023, 512, -1))):
                        h = av(A[:, 0, 3 + pr, dst], src, ACT.Copy, b3, m_z["done"], *ada_fin)
                        l = tt(dve, A[:, 1, 3 + pr, dst], src, A[:, 0, 3 + pr, dst].bitcast(F32), ALU.subtract, h)
                        m_y[("f", pr, dst.start)] = l
                    yield

        def after_projections():
            while 8 not in m_z:
                yield
            yield from attention()
            yield from fourier()

        def state_space():
            yield from tables
            while len(m_us) < 3:
                yield
            yield from ssm()

        weave((w_in_all(), 1), (state_space(), 2), (after_projections(), 2), (ada_rest(), 1))
        pu.close()
        fence(False)

        def out_proj(name, Y, nrm, ready, half):
            def evac_of(j):
                def evac(half, ps, m):
                    o = Y[:, j, HALF[half]]
                    r = av(o, ps[:, :], ACT.Copy, m)
                    nrm.add(o, half, r)
                    return r
                return evac
            for j in range(8):
                n = panel(name, j)
                m, _ = gemm_half(name, n, half, evac_of(j), ready)
                panel_done(n, m)
                yield

        def residual(Y, nrm, X, mx, xdst, post, pre, shift, tmp, diag, final=False, key=""):
            mA = [None, None]
            st = []

            def run(half):
                cs = HALF[half]
                b1, b2 = 6 + half, 4 + half
                p1, p2 = PSC[half], PSS[:, half, :]
                m = rows_of(nrm.ss[:, cs], p1, True, True, *nrm.done[half], *bank(b1))
                m_r = rstd_bank(p1, b1, D, diag, m)
                outm = []
                yield
                for j in range(8):
                    m = stt(Y[:, j, cs], Y[:, j, cs], post(j), p1[:, :], ALU.mult, ALU.mult, m_r)
                    if j == 7:
                        banks[b1] = m
                    m = tt(pool if j % 2 else dve, Y[:, j, cs], Y[:, j, cs], X(j)[:, cs], ALU.add, m, mx[j])
                    outm.append(m)
                    if final:
                        st.append(dma(sp if j % 2 else act, f"{key}s{half}{j % 4}", xdst[j, :, cs], Y[:, j, cs], m))
                        yield
                        continue
                    if j % 2:
                        yield
                        for jj in (j - 1, j):
                            b = nrm.i % 2
                            nrm.i += 1
                            m = av(nrm.sq[b][:, :], Y[:, jj, cs], ACT.Square, outm[jj], *nrm.marks[b])
                            r = rows_of(nrm.sq[b][:, :], p2, jj == 0, jj == 7, m, *bank(b2))
                            nrm.marks[b] = [r]
                        yield
                if final:
                    return
                m_r = rstd_bank(p2, b2, D, diag, r)
                yield
                mA[half] = apply_half(lambda j: Y[:, j, :], half, p2, b2, pre, shift, tmp, m_r, lambda j: [outm[j]])
                if half == 1:
                    for j in range(8):
                        st.append(dma(sp, f"{key}s{j % 4}", xdst[j], Y[:, j, :], outm[j]))
                yield
            return run, mA

        def finish(gemm_of, res, head):
            run, mA = res

            def ahead():
                while state["split"] < min(state["use"] + 3, len(stream)):
                    split_panel()
            for _ in gemm_of(0):
                pass
            weave((gemm_of(1), 1), (run(0), 2))
            ahead()
            if head is None:
                for _ in run(1):
                    pass
            else:
                weave((run(1), 4), (head(mA), 1))
            return mA

        ring[0] = 4
        with ExitStack() as c3:
            Y = sb([P, NK, T], c=c3)
            X = sb([P, NK, T], c=c3)
            nrm = norm_bufs(c3)
            tmp = [sb([P, 512], c=c3) for _ in range(4)]
            diag = sb([P, 512], c=c3)
            mx = [dma(act, f"xa{j}", X[:, j, :], t["xT"][j]) for j in range(8)]
            ys = list(m_y.values())
            res = residual(Y, nrm, lambda j: X[:, j, :], mx, t["xs"], gm(2), gm(4), gm(3), tmp, diag, key="ra")
            mA = finish(lambda half: out_proj("w_out", Y, nrm, lambda half, k: ys, half), res,
                        lambda mA: heads("f1u", (0, 1, 2), mA))
            pre = heads_out[:]
        fence(False)

        def ffn(name, tiles, seq_of, make_hid, Y, nrm, H, xsrc, res_of, head):
            hid_m, hid_free = {}, {}
            chunks = ffn_chunks(tiles)
            dn = [0]
            y_m = {}
            mx = []

            def tile_down(ci, n, mi, j, half):
                c0, k = chunks[ci]
                ready = lambda half, i: [hid_m[c0 + i]]
                b = next_bank()
                r = gemm3(PSB[b][:, :], n, [(mi * k + kk) * 128 for kk in range(k)], H,
                          [(c0 + kk) % 6 for kk in range(k)], half, ready, *bank(b))
                o = Y[:, j, HALF[half]]
                if ci == 0:
                    banks[b] = dve.put(lambda g, o=o, b=b: g.tensor_copy(o, PSB[b][:, :]), r)
                else:
                    banks[b] = tt(dve, o, o, PSB[b][:, :], ALU.add, r, y_m[(j, half)])
                y_m[(j, half)] = banks[b]
                if ci == len(chunks) - 1:
                    nrm.add(o, half, banks[b])
                return r

            def down(ci):
                c0, k = chunks[ci]
                per = 8 // k
                for pn in range(k):
                    n = panel(name + "d", dn[0])
                    dn[0] += 1
                    for mi in range(per):
                        for half in range(2):
                            r = tile_down(ci, n, mi, pn * per + mi, half)
                    panel_done(n, r)
                for kk in range(k):
                    hid_free[c0 + kk] = [r]

            held = {}

            def down_last(half):
                ci = len(chunks) - 1
                k = chunks[ci][1]
                per = 8 // k
                for pn in range(k):
                    if k == 4 or half == 0:
                        held[pn] = panel(name + "d", dn[0] + pn)
                    for mi in range(per):
                        r = tile_down(ci, held[pn], mi, pn * per + mi, half)
                        yield
                    if k == 4 or half == 1:
                        panel_done(held[pn], r)

            seq = seq_of()
            for n, (c0, k) in enumerate(chunks):
                lo = 0 if n == 0 else min(c0 + 2, tiles)
                for i in range(lo, min(c0 + k + 2, tiles)):
                    hid_m[i] = make_hid(i, seq, H, hid_free.get(i - 6, []))
                    if i == tiles - 1:
                        done = used[state["use"] - 1]
                        for j in range(8):
                            mx.append(dma(sp, f"{name}x{j}", A[:, 0, j, :].bitcast(F32), xsrc[j], done))
                if n < len(chunks) - 1:
                    down(n)
            return finish(down_last, res_of(mx), head)

        XA = lambda j: A[:, 0, j, :].bitcast(F32)
        with ExitStack() as c4:
            Y = sb([P, NK, T], c=c4)
            c5 = ExitStack()
            H = sb([P, 2, 6, T], F32R, c=c5)
            pad = [sb([P, T + 2], c=c5) for _ in range(3)]
            cv = sb([P, T], c=c5)
            nrm = norm_bufs(c5)
            for p in pad:
                memset(dve, p[:, 0:T + 2:T + 1], 0.0)
            pad_m = [(dve.sem, dve.n)]
            pad_free = [[], [], []]
            cv_free = []

            def evac_f1(i):
                def evac(half, ps, m):
                    return av(pad[i % 3][:, 1 + half * 512:513 + half * 512], ps[:, :], ACT.Copy, m, *pad_free[i % 3])
                return evac

            def hid1(i, seq, H, free):
                def conv(out, pd, e, *after):
                    ch = i + 22 * e
                    w = lambda j: col("conv_w", 44 * j + ch)
                    m = ts(dve, out, pd[:, 0:T], w(0), col("conv_b", ch), ALU.mult, ALU.add, *pad_m, *after)
                    m = stt(out, pd[:, 1:T + 1], w(1), out, ALU.mult, ALU.add, m)
                    return stt(out, pd[:, 2:T + 2], w(2), out, ALU.mult, ALU.add, m)
                a, b = (2 * i) % 3, (2 * i + 1) % 3
                _, last = until_tile(seq)
                mg = conv(cv[:, :], pad[a], 0, last, *cv_free)
                mg2 = av(cv[:, :], cv[:, :], ACT.Gelu_apprx_tanh, mg)
                _, last = until_tile(seq)
                v = pad[a][:, 1:T + 1]
                m = conv(v, pad[b], 1, last, mg)
                pad_free[b] = [m]
                m = tt(dve, v, v, cv[:, :], ALU.mult, m, mg2)
                cv_free[:] = [m]
                m = split_act(H, i % 6, v, ALL, True, m, *free)
                pad_free[a] = [m]
                return m

            tmp = [cv[:, 0:512], cv[:, 512:T], pad[1][:, 0:512], pad[2][:, 0:512]]
            mA = ffn("f1", 22, lambda: gemm_seq("f1u", range(44), evac_f1, by_half(mA), 3, pre), hid1, Y, nrm, H, t["xs"],
                     lambda mx: residual(Y, nrm, XA, mx, t["xs2"], gm(5), lambda j: col("n1", j), None, tmp, pad[0][:, 0:512],
                                         key="rb"), lambda mA: heads("w_in2", (6, 7, 8), mA))
            pre = heads_out[:]
            c5.close()
        fence(False)

        pb2 = ExitStack()
        c6 = ExitStack()
        hz = sb([P, 8, T], c=pb2)
        wb = [sb([P, 2, 128], c=pb2) for _ in range(4)]
        slot = {0: 2, 1: 4, 2: 6, 3: 3, 4: 0, 5: 1, 6: 5, 7: 7}
        my = {}

        def load_branch(n_free, *after):
            for i in (0, 1, 2, 3, 6, 7)[:n_free]:
                if i in yb_m and i not in my:
                    my[i] = dma(sp, f"ybl{i}", hz[:, slot[i], :], t["yb"][i], yb_m[i], *after)

        gate_order = [(j, k) for j in range(8) for k in range(4)]
        wb_free = {}

        def wb_load(n):
            if n < 32:
                j, k = gate_order[n]
                return dma(sp, f"wb{n % 4}", wb[n % 4][:, :, :], t["w_branch"][j, k], *wb_free.get(n - 4, []))
        ld = {n: wb_load(n) for n in range(2)}

        bd = sb([P, 8, 128], c=c6)
        lbd = dma(sp, "bd", bd[:, :, :], t["bd"])
        cc = sb([P, 64], c=c6)

        def stor(n):
            return sb([P, n, T], c=c6)

        z2 = stor(0 + 4)
        m_h = {}

        def proj(idx, dsts, marks, free=(), head=0):
            at = dict(zip(idx, dsts))

            def evac_of(i):
                def evac(half, ps, m):
                    r = av(at[i][:, HALF[half]], ps[:, :], ACT.Copy, m, *free)
                    marks[i] = r
                    return r
                return evac
            yield from gemm_seq("w_in2", idx, evac_of, by_half(mA), head, pre if head else ())

        ring[0] = 2
        fill = []
        sgt = [sb([P, T], c=c6) for _ in range(2)]
        sg_free = [[], []]

        def gates_ahead():
            for n, (j, k) in enumerate(gate_order):
                b = n % 2

                def evac_of(i, b=b):
                    def evac(half, ps, m):
                        return av(sgt[b][:, HALF[half]], ps[:, :], ACT.Sigmoid, m, *sg_free[b])
                    return evac
                for r in gemm_seq("w_in2", [20 + 8 * k + j], evac_of, by_half(mA)):
                    if r is not None:
                        d = dma(sp, f"gs{b}", t["gs"][n], sgt[b][:, :], r[1])
                        sg_free[b] = [d]
                        fill.append(d)
                    yield

        for _ in proj(list(range(6, 14)), [hz[:, i, :] for i in range(8)], m_h, (), 3):
            pass

        yb_m = {}

        def hgrn():
            with ExitStack() as ch:
                bcum = sb([P, T], c=ch)
                E = sb([P, T], c=ch)
                Qp = sb([P, T], c=ch)
                Kp = sb([P, T], c=ch)
                Kt = sb([P, T], c=ch)
                kdt = sb([P, 128], c=ch)
                vr = sb([P, 8, 128], c=ch)
                st = sb([P, 128], c=ch)
                msk = sb([P, 8, 128], mybir.dt.uint8, c=ch)
                lm = dma(sp, "msk2", E[:, :], t["hmask"].rearrange("p l s -> p (l s)"))
                lm = dve.put(lambda g: g.tensor_copy(msk[:, :, :].rearrange("p l s -> p (l s)"), E[:, :]), lm)
                m = av(cc[:, 0:2], col("hlb", 0, 2), ACT.Copy, m_par)
                m = tt(dve, cc[:, 2:4], cc[:, 0:2], cc[:, 0:2], ALU.subtract, m)
                m = av(cc[:, 2:4], cc[:, 2:4], ACT.Exp, m)
                m = dve.put(lambda g: g.reciprocal(cc[:, 4:6], cc[:, 2:4]), m)
                m = tt(dve, cc[:, 2:4], cc[:, 2:4], cc[:, 4:6], ALU.mult, m)
                m = tt(dve, cc[:, 6:8], cc[:, 2:4], cc[:, 2:4], ALU.subtract, m)
                mlb = ts(dve, cc[:, 8:10], cc[:, 6:8], -1.0, 1.0, ALU.mult, ALU.add, m)
                yield
                last = []
                for tl in range(2):
                    q, f, v, g = (hz[:, 2 * e + tl, :] for e in range(4))
                    mz = [m_h[6 + 2 * e + tl] for e in range(4)]
                    m = av(f, f, ACT.Sigmoid, mz[1])
                    m = ts(dve, f, f, cc[:, 8 + tl:9 + tl], cc[:, 6 + tl:7 + tl], ALU.mult, ALU.add, m, mlb)
                    mk = ts(dve, Kt[:, :], f, -1.0, 1.0, ALU.mult, ALU.add, m, *last)
                    m = ts(dve, f, f, 2.0 ** -63, None, ALU.max, None, m)
                    m = av(f, f, ACT.Ln, m)
                    for n in range(8):
                        c = slice(n * 128, n * 128 + 128)
                        mb = dve.put(lambda g_, f=f, c=c: g_.tensor_tensor_scan(bcum[:, c], onesm[:, :], f[:, c], 0.0,
                                                                              ALU.mult, ALU.add), m, m_ones, *last)
                    yield
                    for b in range(2):
                        for n in range(4):
                            r = transpose(PSB[2 + b][:, n * 128:n * 128 + 128],
                                          v[:, (4 * b + n) * 128:(4 * b + n) * 128 + 128], mz[2], *bank(2 + b))
                        r = av(vr[:, 4 * b:4 * b + 4, :], PSB[2 + b][:, :].rearrange("p (n d) -> p n d", d=128), ACT.Copy,
                               r, *last)
                        banks[2 + b] = r
                    mv = r
                    yield
                    lv_free = list(last)
                    for L in range(8):
                        if L == 7:
                            mq, mk2 = mz[0], mk
                            qs, ks = q, Kt[:, :]
                        else:
                            w = 1 << L
                            nb = T // (2 * w)
                            b3 = bcum[:, :].rearrange("p (n w) -> p n w", w=2 * w)
                            e3 = E[:, :].rearrange("p (n w) -> p n w", w=2 * w)
                            m = tt(dve, e3, b3, b3[:, :, w - 1:w].broadcast_to([P, nb, 2 * w]), ALU.subtract, mb, *lv_free)
                            m = av(E[:, :], E[:, :], ACT.Abs, m)
                            me = av(E[:, :], E[:, :], ACT.Exp, m, scale=-1.0)
                            mq = tt(dve, Qp[:, :], q, E[:, :], ALU.mult, me, mz[0], *lv_free)
                            mk2 = tt(dve, Kp[:, :], Kt[:, :], E[:, :], ALU.mult, me, mk, *lv_free)
                            qs, ks = Qp[:, :], Kp[:, :]
                        yield
                        yield
                        for h in range(2):
                            pr = slice(64 * h, 64 * h + 64)
                            for b in range(2):
                                pb = (h * 2 + b) % 2
                                for n in range(4):
                                    cs_ = slice((4 * b + n) * 128, (4 * b + n) * 128 + 128)
                                    r = mm(PSS[:, pb, n * 128:n * 128 + 128], ks[pr, cs_], qs[pr, cs_], True, True, True,
                                           mq, mk2, *bank(4 + pb))
                                o = hs[:, h, b * 512:b * 512 + 512].rearrange("p (n s) -> p n s", s=128)
                                mkx = msk[:, L, :].unsqueeze(1).broadcast_to([P, 4, 128])
                                src = PSS[:, pb, :].rearrange("p (n s) -> p n s", s=128)
                                r2 = dve.put(lambda g_, o=o, mkx=mkx, src=src: g_.copy_predicated(o, mkx, src), r, lm, *hs_m)
                                banks[4 + pb] = r2
                            yield
                        if tl == 1:
                            load_branch(3, *last)
                        hs_m[:] = [r2]
                        lv_free = [r]
                    m_sc = r2
                    m = memset(dve, st[:, :], 0.0, *last)
                    ms = m
                    b3 = bcum[:, :].rearrange("p (n w) -> p n w", w=128)
                    e3 = E[:, :].rearrange("p (n w) -> p n w", w=128)
                    m = av(E[:, :], bcum[:, :], ACT.Exp, mb, *lv_free)
                    mq = tt(dve, Qp[:, :], q, E[:, :], ALU.mult, m, *lv_free)
                    m = tt(dve, e3, b3, b3[:, :, 127:128].broadcast_to([P, 8, 128]), ALU.subtract, mq)
                    m = av(E[:, :], E[:, :], ACT.Exp, m, scale=-1.0)
                    mk2 = tt(dve, Kp[:, :], Kt[:, :], E[:, :], ALU.mult, m)
                    m_el = av(cc[:, 16:24], b3[:, :, 127], ACT.Exp, mb, *last)
                    yield
                    for n in range(8):
                        cs_ = slice(n * 128, n * 128 + 128)
                        o = PSB[3][:, (n % 4) * 128:(n % 4) * 128 + 128]
                        for h in range(2):
                            oh = PSB[3][64 * h:64 * h + 64, (n % 4) * 128:(n % 4) * 128 + 128]
                            mm(oh, vr[:, n, 64 * h:64 * h + 64], hs[:, h, cs_], True, False, False, mv, m_sc, *bank(3))
                            ro = mm(oh, st[:, 64 * h:64 * h + 64], Qp[:, cs_], False, True, True, mq, ms)
                        if n < 7:
                            r = transpose(PSB[2][:, 0:128], Kp[:, cs_], mk2, *bank(2))
                            r = av(kdt[:, :], PSB[2][:, 0:128], ACT.Copy, r, *kd_free)
                            banks[2] = r
                            yield
                            r = mm(PSS[:, 0, 0:128], kdt[:, :], vr[:, n, :], True, True, True, r, *bank(4))
                            kd_free[:] = [r]
                            for h in range(2):
                                pr = slice(64 * h, 64 * h + 64)
                                c_ = slice(64 * h, 64 * h + 64)
                                ms = stt(st[pr, c_], st[pr, c_], cc[pr, 16 + n:17 + n], PSS[pr, 0, c_], ALU.mult, ALU.add,
                                         r, ro, m_el)
                            banks[4] = ms
                        if n % 4 == 3:
                            c = slice((n - 3) * 128, (n + 1) * 128)
                            mo = av(E[:, c], PSB[3][:, :], ACT.Copy, ro, mk2)
                            banks[3] = mo
                        yield
                    m = av(Qp[:, :], E[:, :], ACT.Square, mo, ro)
                    mg = av(g, g, ACT.Silu, mz[3])
                    for half in range(2):
                        c = slice(half * 512, half * 512 + 512)
                        r = mm(PSS[:, half, :], bd[:, 6, :], Qp[:, c], True, True, True, m, lbd, *bank(4 + half))
                        m2 = av(Kp[:, c], PSS[:, half, :], ACT.Sqrt, r, bias=col("eps"), scale=1.0 / 64)
                        banks[4 + half] = m2
                    m = dve.put(lambda g_: g_.reciprocal(Kp[:, :], Kp[:, :]), m2)
                    m = tt(dve, E[:, :], E[:, :], Kp[:, :], ALU.mult, m)
                    m = stt(hz[:, tl, :], E[:, :], col("hnorm", tl), g, ALU.mult, ALU.mult, m, mg)
                    my[4 + tl] = m
                    last = [m, m2]
                    yield

        hs = sb([P, 2, T], c=c6)
        hs_m = [memset(dve, hs[:, :, :], 0.0)]
        kd_free = []
        gm_ = {}

        def rest():
            a = z2
            for tl in range(2):
                yield from proj([tl, 2 + tl], [a[:, 0, :], a[:, 1, :]], gm_, tuple(rfree))
                x, g = a[:, 0, :], a[:, 1, :]
                xc, r_ = a[:, 2, :], a[:, 3, :]
                mx_, mg_ = gm_[tl], gm_[2 + tl]
                w = lambda j: col("lcw", 2 * j + tl)
                m = ts(dve, xc, x, w(3), col("lcb", tl), ALU.mult, ALU.add, mx_, *rfree)
                for d in (1, 2, 3):
                    m = stt(xc[:, d:T], x[:, 0:T - d], w(3 - d), xc[:, d:T], ALU.mult, ALU.add, m)
                yield
                m0 = m
                for half in range(2):
                    c = slice(half * 512, half * 512 + 512)
                    r = mm(PSC[0][:, :], bd[:, tl, :], xc[:, c], True, True, True, m0, lbd, *bank(6))
                    m = av(r_[:, c], PSC[0][:, :], ACT.Sigmoid, r, bias=col("lba", tl))
                    banks[6] = m
                    r = mm(PSC[1][:, :], bd[:, 2 + tl, :], xc[:, c], True, True, True, m0, lbd, *bank(7))
                    m = av(x[:, c], PSC[1][:, :], ACT.Sigmoid, r, m0, bias=col("lbx", tl))
                    banks[7] = m
                yield
                m1 = tt(dve, x, x, xc, ALU.mult, m)
                m2 = ts(dve, r_, r_, cc[:, 40 + tl:41 + tl], None, ALU.mult, None, m, m_sp)
                m = av(xc, r_, ACT.Tanh, m2, m1, scale=-1.0)
                ma = av(r_, r_, ACT.Exp, m)
                m3 = av(tq[:, :], r_, ACT.Square, ma, *rfree)
                m3 = stt(xc, tq[:, :], 1.0, xc, ALU.add, ALU.mult, m3, m)
                m3 = av(xc, xc, ACT.Sqrt, m3)
                m3 = tt(dve, x, x, xc, ALU.mult, m3)
                yield
                m3 = dve.put(lambda g_, x=x, r_=r_, xc=xc: g_.tensor_tensor_scan(xc, r_, x, 0.0, ALU.mult, ALU.add), m3, ma)
                mg_ = av(g, g, ACT.Gelu_apprx_tanh, mg_)
                m3 = tt(dve, g, xc, g, ALU.mult, m3, mg_)
                yb_m[tl] = dma(sp, f"yr{tl}", t["yb"][tl], g, m3)
                rfree[:] = [m3, yb_m[tl]]
                yield
            for tl in range(2):
                yield from proj([4 + tl], [a[:, 0, :]], gm_, tuple(rfree))
                x = a[:, 0, :]
                s2, s4 = a[:, 2, :], a[:, 3, :]

                def dbl(dst, src, w, pr, *after):
                    m = dve.put(lambda g_: g_.tensor_copy(dst[pr, 0:w], src[pr, 0:w]), *after)
                    return tt(dve, dst[pr, w:T], src[pr, w:T], src[pr, 0:T - w], ALU.add, *after, m)
                al = slice(0, 128)
                up_ = slice(64, 128)
                if tl == 0:
                    m = dbl(s2, x, 1, al, gm_[4 + tl], *rfree)
                    m = dbl(s4, s2, 2, up_, m)
                    m = dve.put(lambda g_: g_.tensor_copy(s4[0:64, :], s2[0:64, :]), m)
                else:
                    m = dbl(s2, x, 1, al, gm_[4 + tl], *rfree)
                    m = dbl(s4, s2, 2, al, m)
                    m = dbl(s2, s4, 4, al, m)
                    m = dbl(s4, s2, 8, up_, m)
                    m = dve.put(lambda g_: g_.tensor_copy(s4[0:64, :], s2[0:64, :]), m)
                yield
                m0 = tt(dve, s4[:, 0:16], s4[:, 0:16], prec[:, tl, 0:16], ALU.mult, m, lpr)
                m = ts(dve, s4[:, 16:T], s4[:, 16:T], prec[:, tl, 15:16], None, ALU.mult, None, m, lpr, m0)
                m = tt(dve, s4, s4, x, ALU.subtract, m)
                for half in range(2):
                    c = slice(half * 512, half * 512 + 512)
                    r = mm(PSC[half][:, :], bd[:, 4 + tl, :], s4[:, c], True, True, True, m, lbd, *bank(6 + half))
                    r = ts(dve, s2[:, c], PSC[half][:, :], col("pscale", tl), None, ALU.mult, None, r)
                    banks[6 + half] = r
                yb_m[2 + tl] = dma(sp, f"yp{tl}", t["yb"][2 + tl], s2, r)
                rfree[:] = [r, yb_m[2 + tl]]
                yield
            for tl in range(2):
                yield from proj([14 + tl, 16 + tl, 18 + tl], [a[:, e, :] for e in range(3)], gm_, tuple(rfree))
                w = lambda j: col("scw", 2 * j + tl)
                m = tt(dve, a[:, 1, :], a[:, 1, :], a[:, 2, :], ALU.mult, gm_[16 + tl], gm_[18 + tl])
                m = ts(dve, a[:, 2, :], a[:, 1, :], w(2), None, ALU.mult, None, m)
                for d in (1, 2):
                    m = stt(a[:, 2, d:T], a[:, 1, 0:T - d], w(2 - d), a[:, 2, d:T], ALU.mult, ALU.add, m)
                m = tt(dve, a[:, 0, :], a[:, 0, :], a[:, 2, :], ALU.mult, m, gm_[14 + tl])
                yb_m[6 + tl] = dma(sp, f"yc{tl}", t["yb"][6 + tl], a[:, 0, :], m)
                rfree[:] = [m, yb_m[6 + tl]]
                yield

        rfree = []
        tq = sb([P, T], c=c6)
        prec = sb([P, 2, 16], c=c6)
        lpr = dma(sp, "prec", prec[:, :, :], t["prec"])
        lam = col("lam", 0, 2)
        s_ = lambda i: cc[:, 24 + 2 * i:26 + 2 * i]
        m = ts(dve, s_(0), lam, -1.0, 0.0, ALU.mult, ALU.max, m_par)
        m2 = av(s_(1), lam, ACT.Abs, m_par)
        m2 = av(s_(1), s_(1), ACT.Exp, m2, scale=-1.0)
        m = ts(dve, s_(2), s_(1), 1.0, None, ALU.add, None, m2, m)
        m2 = av(s_(3), s_(2), ACT.Ln, m)
        m = ts(dve, s_(2), s_(2), -1.0, None, ALU.add, None, m, m2)
        m = ts(dve, s_(4), s_(2), 0.0, None, ALU.is_equal, None, m)
        m = tt(dve, s_(3), s_(3), s_(1), ALU.mult, m)
        m = tt(dve, s_(5), s_(4), s_(1), ALU.mult, m)
        m = tt(dve, s_(3), s_(3), s_(5), ALU.add, m)
        m = tt(dve, s_(2), s_(2), s_(4), ALU.add, m)
        m = dve.put(lambda g: g.reciprocal(s_(2), s_(2)), m)
        m = tt(dve, s_(3), s_(3), s_(2), ALU.mult, m)
        m = tt(dve, s_(3), s_(3), s_(0), ALU.add, m)
        m_sp = ts(dve, cc[:, 40:42], s_(3), -8.0, None, ALU.mult, None, m)

        live = [1]

        def both():
            gens = [rest(), hgrn()]
            while gens:
                for g in list(gens):
                    try:
                        next(g)
                        yield
                    except StopIteration:
                        gens.remove(g)
            live.clear()

        work, ahead = both(), gates_ahead()
        while live:
            next(work, None)
            next(work, None)
            next(ahead, None)
        load_branch(6, my[5])
        fence(False)
        c6.close()

        ring[0] = 4
        with ExitStack() as c7:
            M = sb([P, NK, T], c=c7)
            sgt = [sb([P, T], c=c7) for _ in range(3)]
            sg_free, m_m = {}, {}

            def gate(n):
                b = n % 3
                j, k = gate_order[n]
                if n < len(fill):
                    q = act if n < 2 else sp
                    m = dma(q, f"gl{b}{q is act}", sgt[b][:, :], t["gs"][n], *fill[-2:], *sg_free.get(n - 3, []))
                    return m

                def evac_of(i):
                    def evac(half, ps, m):
                        return av(sgt[b][:, HALF[half]], ps[:, :], ACT.Sigmoid, m, *sg_free.get(n - 3, []))
                    return evac
                _, e = until_tile(gemm_seq("w_in2", [20 + 8 * k + j], evac_of, by_half(mA)))
                return e

            gm2 = {0: gate(0), 1: gate(1)}
            for n, (j, k) in enumerate(gate_order):
                if n + 2 < 32:
                    gm2[n + 2] = gate(n + 2)
                if n + 2 < 32:
                    ld[n + 2] = wb_load(n + 2)
                mg, s, b = gm2[n], n % 4, n % 3
                for half in range(2):
                    c = HALF[half]
                    bk = 6 + half
                    for e in range(2):
                        r = mm(PSC[half][:, :], wb[s][:, e, :], hz[:, slot[2 * k + e], c], e == 0, e == 1, e == 1, ld[n],
                               my[2 * k + e], *bank(bk))
                    wb_free[n] = [r]
                    if k == 0:
                        r = tt(dve, M[:, j, c], sgt[b][:, c], PSC[half][:, :], ALU.mult, r, mg)
                    else:
                        r = tt(dve, sgt[b][:, c], sgt[b][:, c], PSC[half][:, :], ALU.mult, r, mg)
                    banks[bk] = r
                    if k:
                        r = tt(dve, M[:, j, c], M[:, j, c], sgt[b][:, c], ALU.add, r, m_m[(j, half)])
                    m_m[(j, half)] = r
                sg_free[n] = [r]
            done = used[state["use"] - 1]
            mA = [[split_act(A, j, M[:, j, c], c, j % 4 == 3, m_m[(j, h)], done) for j in range(8)]
                  for h, c in enumerate(HALF)]
            fence(False)
        pb2.close()
        with ExitStack() as c8:
            Y = sb([P, NK, T], c=c8)
            X = sb([P, NK, T], c=c8)
            nrm = norm_bufs(c8)
            tmp = [sb([P, 512], c=c8) for _ in range(4)]
            diag = sb([P, 512], c=c8)
            mx = [dma(act, f"xc{j}", X[:, j, :], t["xs2"][j]) for j in range(8)]
            res = residual(Y, nrm, lambda j: X[:, j, :], mx, t["xs"], lambda j: col("n2", j), lambda j: col("n3", j), None,
                           tmp, diag, key="rc")
            mA = finish(lambda half: out_proj("w_out2", Y, nrm, by_half(mA), half), res,
                        lambda mA: heads("f2u", (0, 1, 2), mA))
            pre = heads_out[:]
        fence(False)

        with ExitStack() as c9:
            Y = sb([P, NK, T], c=c9)
            H = sb([P, 2, 6, T], F32R, c=c9)
            rl = [sb([P, T], c=c9) for _ in range(3)]
            nrm = norm_bufs(c9)
            rl_free = [[], [], []]

            def evac_f2(i):
                def evac(half, ps, m):
                    return av(rl[i % 3][:, HALF[half]], ps[:, :], ACT.Relu, m, *rl_free[i % 3])
                return evac

            def hid2(i, seq, H, free):
                v = rl[i % 3][:, :]
                _, last = until_tile(seq)
                m = tt(dve, v, v, v, ALU.mult, last)
                m = split_act(H, i % 6, v, ALL, True, m, *free)
                rl_free[i % 3] = [m]
                return m

            ffn("f2", 32, lambda: gemm_seq("f2u", range(32), evac_f2, by_half(mA), 3, pre), hid2, Y, nrm, H, t["xs"],
                lambda mx: residual(Y, nrm, XA, mx, t["out"], lambda j: col("n4", j), None, None, None, rl[0][:, 0:512],
                                    final=True, key="rd"), None)
        for key, (s, total) in dma_total.items():
            sp.wait((s, total))

        assert state["use"] == len(stream)
        block = ctx.enter_context(nc.Block())

        @block.sync
        def _(eng):
            sp.emit(eng)

        @block.gpsimd
        def _(eng):
            pool.emit(eng)

        @block.scalar
        def _(eng):
            act.emit(eng)

        @block.vector
        def _(eng):
            dve.emit(eng)

        @block.tensor
        def _(eng):
            pe.emit(eng)


def _panels(w):
    k, m = w.shape
    a = w.reshape(k // 128, 128, m // 128, 128).transpose(2, 1, 0, 3)
    return np.ascontiguousarray(a).reshape(m // 128, 128, k)


def _down(w):
    out = []
    a = w.reshape(-1, 128, 8, 128)
    for c, k in ffn_chunks(a.shape[0]):
        b = a[c:c + k].transpose(2, 1, 0, 3)
        per = 8 // k
        for j in range(0, 8, per):
            out.append(b[j:j + per].transpose(1, 0, 2, 3).reshape(128, 1024))
    return np.ascontiguousarray(np.stack(out))


def _vec(v):
    return v.reshape(-1, 128).T


def _constants():
    f = np.float32
    out = {"ident": np.eye(128, dtype=f)}
    n = np.arange(1024)
    ang = (n[:, None] * n[None, :]) % 1024 * (2 * np.pi / 1024)
    c, s = np.cos(ang), -np.sin(ang)
    d = np.empty((8, 128, 1024), f)
    for tp in range(8):
        r = slice(tp * 128, tp * 128 + 128)
        d[tp, :, 0:512] = c[r, 0:512]
        d[tp, :, 512:] = s[r, 0:512]
    out["dft"] = d
    m = np.arange(64)
    a64 = (m[:, None] * m[None, :]) % 64 * (2 * np.pi / 64)
    c64 = np.zeros((128, 2, 128))
    for b in range(2):
        q = slice(64 * b, 64 * b + 64)
        c64[q, 0, q] = np.cos(a64) / 256
        c64[q, 1, q] = np.sin(a64) / 256
    out["c64"] = c64.astype(f)
    dist = np.abs(np.arange(128)[:, None] + 128 - np.arange(384)[None, :]).astype(f)
    out["dist"] = np.where(dist <= 128, -dist, f(-1e30)).astype(f)
    out["alt"] = (1 - 2 * (np.arange(128) % 2)).astype(f)[:, None]
    ex = np.zeros((128, 31), f)
    msk = np.zeros((128, 15), f)
    j = np.arange(15)
    ex[:64, 0:15] = np.maximum(j - 7, 0)
    ex[64:, 0:15] = np.maximum(7 - j, 0)
    msk[:64] = j >= 7
    msk[64:] = j <= 7
    e = np.arange(8)
    ex[:64, 15:23] = e + 1
    ex[64:, 15:23] = 8 - e
    ex[:64, 23:31] = 7 - e
    ex[64:, 23:31] = e
    out["exps"], out["mask15"] = ex, msk
    k = np.arange(128, dtype=f)
    out["kidx"] = np.tile(k, (128, 1))
    nz = np.ones((128, 128), f)
    nz[:, 0] = 0
    out["nz"] = nz
    hm = np.zeros((128, 8, 128), f)
    sidx, tidx = np.arange(128)[:, None], np.arange(128)[None, :]
    for L in range(7):
        w = 1 << L
        hm[:, L, :] = (sidx // (2 * w) == tidx // (2 * w)) & (sidx % (2 * w) < w) & (tidx % (2 * w) >= w)
    hm[:, 7, :] = sidx == tidx
    out["hmask"] = hm
    pos = np.arange(1, 1025, dtype=f)
    prec = np.empty((128, 2, 16), f)
    for i, w in enumerate((2, 4, 8, 16)):
        prec[64 * (i % 2):64 * (i % 2) + 64, i // 2, :] = 1.0 / np.minimum(pos[:16], w)
    out["prec"] = prec
    return out


def _blocks(mats, n):
    per = 128 // n
    out = np.zeros((mats.shape[0] // per, 128, 128), mats.dtype)
    for i in range(mats.shape[0]):
        r = slice((i % per) * n, (i % per) * n + n)
        out[i // per, r, r] = mats[i]
    return out


def _layout(v):
    a = dict(_constants())
    a["xT"] = np.ascontiguousarray(v["x"][0].T).reshape(8, 128, 1024)
    a["w_ada"] = np.ascontiguousarray(v["w_ada"][0].reshape(8, 128, 6, 1024).transpose(2, 0, 1, 3))
    pair = np.concatenate([np.arange(64) + 64 * h for i in range(3) for h in (i, 3 + i)])
    w_in = v["w_in"][0]
    cols = np.concatenate([np.arange(384), 640 + pair, np.arange(1024, 1280), np.arange(384, 640)])
    a["w_in"] = _panels(w_in[:, cols])
    rows = np.concatenate([np.arange(640), 640 + pair])
    a["w_out"] = _panels(v["w_out"][0][rows])
    up = v["w_up"][0].reshape(1024, 2, 22, 128).transpose(0, 2, 1, 3).reshape(1024, 5632)
    a["f1u"] = _panels(up)
    a["f1d"] = _down(v["w_down"][0])
    a["w_in2"] = _panels(v["w_in_2"][0])
    a["w_out2"] = _panels(v["w_out_2"][0])
    a["f2u"] = _panels(v["w_up_2"][0])
    a["f2d"] = _down(v["w_down_2"][0])
    wb = v["w_branch_2"][0].reshape(4, 2, 128, 8, 128)
    a["w_branch"] = np.ascontiguousarray(wb.transpose(3, 0, 2, 1, 4))
    a["w_glu"] = np.ascontiguousarray(v["w_glu"][0].reshape(3, 128, 3, 128).transpose(1, 0, 2, 3))
    a["w_fft"] = np.ascontiguousarray(_blocks(v["w_fft"][0], 64).transpose(1, 0, 2))
    one = np.ones((64, 64), np.float32)
    bd = np.concatenate([_blocks(v["lru_w_a_2"][0], 32), _blocks(v["lru_w_x_2"][0], 32), _blocks(v["pool_w_2"][0], 64),
                         _blocks(np.stack([one, one]), 64), np.zeros((1, 128, 128), np.float32)])
    a["bd"] = np.ascontiguousarray(bd.transpose(1, 0, 2))
    G, S = 24, 64
    p = np.empty((2, S, 3, G), np.float32)
    p[:, :, 0] = v["lam_re"][0].transpose(0, 2, 1)
    p[:, :, 1] = v["lam_im"][0].transpose(0, 2, 1)
    p[:, :, 2] = v["log_dt"][0][:, None, :]
    a["ssm_p"] = p.reshape(128, 3, G)
    b = np.stack([v["b_re"][0], v["b_im"][0]]).transpose(1, 3, 0, 2, 4)
    a["ssm_b"] = np.ascontiguousarray(b).reshape(128, 2, G, 16)
    c = np.stack([v["c_re"][0], v["c_im"][0]]).transpose(3, 0, 1, 2)
    a["ssm_c"] = np.ascontiguousarray(np.concatenate([c, c]))
    dI = np.zeros((16, G, 16), np.float32)
    i16 = np.arange(16)
    dI[i16, :, i16] = v["d_skip"][0].reshape(G, 16).T
    a["dI"] = dI
    par = np.empty((128, NPAR), np.float32)

    def put(name, x):
        at, n = PARAM_COLS[name]
        par[:, at:at + n] = x

    put("c", _vec(v["c"][0]))
    put("b_ada", _vec(v["b_ada"][0]))
    for n in ("g_pre_mix", "g_post_mix", "g_pre_ffn", "g_post_ffn"):
        put(n, _vec(v[n][0]))
    put("conv_w", _vec(v["conv_w"][0]))
    put("conv_b", _vec(v["conv_b"][0]))
    s = v["sink"][0]
    put("sink", np.array([s[3 * g + i] for i in range(3) for g in range(2)], np.float32)[None, :])
    put("eps", np.float32(EPS))
    for n, k in (("n1", "norm_mix_pre_2"), ("n2", "norm_mix_post_2"), ("n3", "norm_mlp_pre_2"), ("n4", "norm_mlp_post_2"),
                 ("lcw", "lru_conv_w_2"), ("lcb", "lru_conv_b_2"), ("lba", "lru_b_a_2"), ("lbx", "lru_b_x_2"),
                 ("lam", "lru_lambda_2"), ("pscale", "pool_scale_2"), ("hlb", "hgrn_lower_bound_2"), ("scw", "sconv_w_2")):
        put(n, _vec(v[k][0]))
    put("hnorm", np.concatenate([v["hgrn_norm_2"][0]] * 2)[:, None])
    a["par"] = par
    return a


SCRATCH = {
    "uscr": (3, 128, 1024), "yscr": (3, 128, 1024), "vscr": (128, 2, NG, 128), "wscr": (128, 2, NG, 128),
    "cscr": (128, 2, NG, 128), "kscr": (NG, 16, 240), "yb": (8, 128, 1024), "gs": (32, 128, 1024), "xs": (8, 128, 1024), "xs2": (8, 128, 1024),
}


def kernel(**inputs):
    import concourse.bacc as _bacc
    from concourse.bass_utils import run_bass_kernel_spmd as _run

    arrays = {k: np.ascontiguousarray(a) for k, a in _layout({k: np.asarray(a) for k, a in inputs.items()}).items()}
    nc = _bacc.Bacc("TRN2", target_bir_lowering=False, num_devices=1)
    t = {}
    for k, a in arrays.items():
        t[k] = nc.dram_tensor("in_" + k, a.shape, mybir.dt.from_np(a.dtype), kind="ExternalInput").ap()
    for k, shape in SCRATCH.items():
        t[k] = nc.dram_tensor(k, shape, F32).ap()
    t["out"] = nc.dram_tensor("out_T", (8, 128, 1024), F32, kind="ExternalOutput").ap()
    build(nc, t)
    r = _run(nc, [{"in_" + k: a for k, a in arrays.items()}], core_ids=[0])
    return np.ascontiguousarray(r.results[0]["out_T"].reshape(1024, 1024).T).reshape(1, 1024, 1024)
```
